# Optimizing a Trainium2 kernel written in Bass

```python
import math
import jax, jax.numpy as jnp
from jax import lax
import numpy as np

D_MODEL = 1024
BATCH = 1
SEQ = 1024
DEPTH = 1

D_PLE = 256
D_MIX = D_MODEL
ATTN_HEADS = 8
HEAD_DIM = 64
D_ATTN = ATTN_HEADS * HEAD_DIM
POOL_WINDOWS = (2, 4, 8, 16)
POOL_GROUPS = len(POOL_WINDOWS)
D_POOL = D_MIX - D_ATTN
POOL_CH = D_POOL // POOL_GROUPS
D_IN = 3 * D_ATTN + ATTN_HEADS + D_POOL
D_FF = int(math.ceil(8 * D_MODEL / 3 / 256) * 256)
Q_BLOCK = 128
RMS_EPS = 1e-6


def rms_norm(x, g):
    xf = x.astype(jnp.float32)
    y = xf * lax.rsqrt(jnp.mean(xf * xf, axis=-1, keepdims=True) + RMS_EPS)
    return (y * g.astype(jnp.float32)).astype(x.dtype)

def forgetting_attention(q, k, v, log_f):
    b, s, h, dh = q.shape
    scale = 1.0 / math.sqrt(dh)
    c = jnp.cumsum(log_f, axis=1).transpose(0, 2, 1)
    nb = s // Q_BLOCK
    qb = q.reshape(b, nb, Q_BLOCK, h, dh).transpose(1, 0, 2, 3, 4)
    cb = c.reshape(b, h, nb, Q_BLOCK).transpose(2, 0, 1, 3)
    starts = jnp.arange(nb, dtype=jnp.int32) * Q_BLOCK
    kpos = jnp.arange(s, dtype=jnp.int32)

    def one_block(args):
        q_i, c_i, s0 = args
        scores = jnp.einsum('bqhd,bkhd->bhqk', q_i, k).astype(jnp.float32) * scale
        scores = scores + c_i[:, :, :, None] - c[:, :, None, :]
        qpos = s0 + jnp.arange(Q_BLOCK, dtype=jnp.int32)
        causal = kpos[None, :] <= qpos[:, None]
        scores = jnp.where(causal, scores, -jnp.inf)
        probs = jax.nn.softmax(scores, axis=-1).astype(v.dtype)
        return jnp.einsum('bhqk,bkhd->bqhd', probs, v)

    out = lax.map(one_block, (qb, cb, starts))
    return out.transpose(1, 0, 2, 3, 4).reshape(b, s, h * dh)

def multiscale_pool(u, w_pool, pool_scale):
    b, s, _ = u.shape
    uf = u.astype(jnp.float32)
    cs = jnp.cumsum(uf, axis=1)
    pos = jnp.arange(s, dtype=jnp.int32)
    outs = []
    for g, w in enumerate(POOL_WINDOWS):
        lo, hi = g * POOL_CH, (g + 1) * POOL_CH
        cs_g = cs[:, :, lo:hi]
        cs_shift = jnp.pad(cs_g, ((0, 0), (w, 0), (0, 0)))[:, :s]
        count = jnp.minimum(pos + 1, w).astype(jnp.float32)[None, :, None]
        outs.append((cs_g - cs_shift) / count - uf[:, :, lo:hi])
    y = jnp.stack(outs, axis=2).astype(u.dtype)
    y = jnp.einsum('bsgc,gcd->bsgd', y, w_pool).reshape(b, s, D_POOL)
    return y * pool_scale

def first_inputs(seed: int = 0) -> dict:
    key = jax.random.key(seed)
    ks = jax.random.split(key, 24)
    f32 = jnp.float32

    def nrm(k, shape, fan_in):
        return jax.random.normal(k, shape, f32) * (fan_in ** -0.5)

    def gain(k, shape):
        return 1.0 + 0.05 * jax.random.normal(k, shape, f32)

    return {
        "x": jax.random.normal(ks[0], (BATCH, SEQ, D_MODEL), f32),
        "p": jax.random.normal(ks[1], (DEPTH, BATCH, SEQ, D_PLE), f32),
        "g_mix_pre": gain(ks[2], (DEPTH, D_MODEL)),
        "w_in": nrm(ks[3], (DEPTH, D_MODEL, D_IN), D_MODEL),
        "b_forget": jax.random.uniform(ks[4], (DEPTH, ATTN_HEADS), f32, 1.0, 4.0),
        "g_attn_grp": gain(ks[5], (DEPTH, D_ATTN)),
        "g_pool_grp": gain(ks[6], (DEPTH, D_POOL)),
        "w_pool": nrm(ks[7], (DEPTH, POOL_GROUPS, POOL_CH, POOL_CH), POOL_CH),
        "pool_scale": 1.0 + 0.1 * jax.random.normal(ks[8], (DEPTH, D_POOL), f32),
        "w_out": nrm(ks[9], (DEPTH, D_MIX, D_MODEL), D_MIX),
        "g_mix_post": gain(ks[10], (DEPTH, D_MODEL)),
        "g_ffn_pre": gain(ks[11], (DEPTH, D_MODEL)),
        "w_ffn_gate": nrm(ks[12], (DEPTH, D_MODEL, D_FF), D_MODEL),
        "w_ffn_up": nrm(ks[13], (DEPTH, D_MODEL, D_FF), D_MODEL),
        "w_ffn_down": nrm(ks[14], (DEPTH, D_FF, D_MODEL), D_FF),
        "g_ffn_post": gain(ks[15], (DEPTH, D_MODEL)),
        "w_ple_proj": nrm(ks[16], (DEPTH, D_PLE, D_MODEL), D_PLE),
        "g_ple": gain(ks[17], (DEPTH, D_MODEL)),
        "w_ple_gate": nrm(ks[18], (DEPTH, D_MODEL, D_MODEL), D_MODEL),
    }

def first_block(x, p, g_mix_pre, w_in, b_forget, g_attn_grp, g_pool_grp, w_pool, pool_scale,
              w_out, g_mix_post, g_ffn_pre, w_ffn_gate, w_ffn_up, w_ffn_down, g_ffn_post,
              w_ple_proj, g_ple, w_ple_gate):
    b, s, _ = x.shape
    h = x
    for i in range(DEPTH):
        hn = rms_norm(h, g_mix_pre[i])
        z = hn @ w_in[i]
        o = 0
        q = z[..., o:o + D_ATTN].reshape(b, s, ATTN_HEADS, HEAD_DIM); o += D_ATTN
        k = z[..., o:o + D_ATTN].reshape(b, s, ATTN_HEADS, HEAD_DIM); o += D_ATTN
        v = z[..., o:o + D_ATTN].reshape(b, s, ATTN_HEADS, HEAD_DIM); o += D_ATTN
        f_logit = z[..., o:o + ATTN_HEADS]; o += ATTN_HEADS
        u = z[..., o:o + D_POOL]
        log_f = jax.nn.log_sigmoid(f_logit.astype(jnp.float32) + b_forget[i].astype(jnp.float32))
        a = forgetting_attention(q, k, v, log_f)
        m = multiscale_pool(u, w_pool[i], pool_scale[i])
        mix = jnp.concatenate([rms_norm(a, g_attn_grp[i]), rms_norm(m, g_pool_grp[i])], axis=-1)
        h = h + rms_norm(mix @ w_out[i], g_mix_post[i])
        hn = rms_norm(h, g_ffn_pre[i])
        ff = (jax.nn.silu(hn @ w_ffn_gate[i]) * (hn @ w_ffn_up[i])) @ w_ffn_down[i]
        h = h + rms_norm(ff, g_ffn_post[i])
        e = rms_norm(p[i] @ w_ple_proj[i], g_ple[i])
        h = h + jax.nn.sigmoid(h @ w_ple_gate[i]) * e
    return h


DEPTH_2 = 2

CHUNK = 64
MEM_LEN = 256
MEM_HEADS = 4
MEM_W = MEM_HEADS * HEAD_DIM
MIX_W = D_MODEL
BR_W = MIX_W - MEM_W
A_HEADS = BR_W // HEAD_DIM
B_HEADS = BR_W // (2 * HEAD_DIM)
LORA_W = 64
LORA_A = 64
N_A = DEPTH_2 // 2
N_B = DEPTH_2 - N_A
A_SHIFT = 3 * BR_W + LORA_W + LORA_A
A_IN = A_SHIFT + BR_W + 2 * MEM_W
B_IN = 2 * BR_W + 2 * MEM_W
NORM_EPS = 1e-6
LNX_EPS = 64e-5


def rms_norm_2(x, g):
    xf = x.astype(jnp.float32)
    y = xf * lax.rsqrt(jnp.mean(xf * xf, axis=-1, keepdims=True) + NORM_EPS)
    return (y * g.astype(jnp.float32)).astype(x.dtype)

def token_shift(z):
    return jnp.pad(z, ((0, 0), (1, 0), (0, 0)))[:, :-1]

def alibi_slopes(n):
    def pow2(m):
        start = 2.0 ** (-8.0 / m)
        return [start ** (i + 1) for i in range(m)]
    if math.log2(n).is_integer():
        s = pow2(n)
    else:
        c = 2 ** int(math.floor(math.log2(n)))
        s = pow2(c) + pow2(2 * c)[0::2][: n - c]
    return jnp.asarray(np.array(s, dtype=np.float32))

def rwkv7_time_mix(z, mu, w0, w2, a0, a2, k_k, k_a, r_k, lnx_w, lnx_b):
    B, S, _ = z.shape
    z = z.astype(jnp.float32)
    z = z + (token_shift(z) - z) * mu
    r, k, v, wd, ad = jnp.split(z, [BR_W, 2 * BR_W, 3 * BR_W, 3 * BR_W + LORA_W], axis=-1)
    w = -jax.nn.softplus(-(w0 + jnp.tanh(wd) @ w2)) - 0.5
    decay = jnp.exp(-jnp.exp(w))
    a = jax.nn.sigmoid(a0 + ad @ a2)
    heads = lambda t: t.reshape(B, S, A_HEADS, HEAD_DIM)
    kk = heads(k * k_k)
    kk = kk * lax.rsqrt(jnp.maximum(jnp.sum(kk * kk, axis=-1, keepdims=True), 1e-12))
    k = k * (1.0 + (a - 1.0) * k_a)
    r, k, v, decay, a = heads(r), heads(k), heads(v), heads(decay), heads(a)

    def step(state, inp):
        r_t, w_t, k_t, v_t, kk_t, a_t = inp
        sa = jnp.einsum('bhvk,bhk->bhv', state, -kk_t)
        state = (state * w_t[:, :, None, :]
                 + sa[..., None] * (kk_t * a_t)[:, :, None, :]
                 + v_t[..., None] * k_t[:, :, None, :])
        y_t = jnp.einsum('bhvk,bhk->bhv', state, r_t)
        return state, y_t

    tm = lambda t: jnp.moveaxis(t, 1, 0)
    state0 = jnp.zeros((B, A_HEADS, HEAD_DIM, HEAD_DIM), jnp.float32)
    _, y = lax.scan(step, state0, (tm(r), tm(decay), tm(k), tm(v), tm(kk), tm(a)))
    y = jnp.moveaxis(y, 0, 1)
    mean = jnp.mean(y, axis=-1, keepdims=True)
    var = jnp.mean(jnp.square(y - mean), axis=-1, keepdims=True)
    y = ((y - mean) * lax.rsqrt(var + LNX_EPS)).reshape(B, S, BR_W) * lnx_w + lnx_b
    bonus = jnp.sum(r * k * r_k, axis=-1, keepdims=True) * v
    return y + bonus.reshape(B, S, BR_W)

def diff_attention(q, k_sh, v_sh, lq1, lk1, lq2, lk2, subln, lam_init):
    B, S, _ = q.shape
    q = q.reshape(B, S, B_HEADS, 2, HEAD_DIM) * (HEAD_DIM ** -0.5)
    k = k_sh.reshape(B, S, B_HEADS, 2, HEAD_DIM)
    v = v_sh.reshape(B, S, B_HEADS, 2 * HEAD_DIM)
    lq1f, lk1f = lq1.astype(jnp.float32), lk1.astype(jnp.float32)
    lq2f, lk2f = lq2.astype(jnp.float32), lk2.astype(jnp.float32)
    lam = jnp.exp(jnp.sum(lq1f * lk1f)) - jnp.exp(jnp.sum(lq2f * lk2f)) + lam_init
    slopes = alibi_slopes(B_HEADS)
    pos = jnp.arange(S)
    nb = S // Q_BLOCK
    qb = jnp.moveaxis(q.reshape(B, nb, Q_BLOCK, B_HEADS, 2, HEAD_DIM), 1, 0)

    def block(args):
        q_blk, i = args
        t = i * Q_BLOCK + jnp.arange(Q_BLOCK)
        s = jnp.einsum('bqhcd,bkhcd->bhcqk', q_blk, k, preferred_element_type=jnp.float32)
        dist = jnp.abs(t[:, None] - pos[None, :]).astype(jnp.float32)
        bias = -slopes[:, None, None] * dist
        allowed = (pos[None, :] // CHUNK) <= (t[:, None] // CHUNK)
        s = jnp.where(allowed, s + bias[None, :, None], -jnp.inf)
        p = jax.nn.softmax(s, axis=-1)
        attn = (p[:, :, 0] - lam * p[:, :, 1]).astype(v.dtype)
        return jnp.einsum('bhqk,bkhe->bqhe', attn, v)

    o = lax.map(block, (qb, jnp.arange(nb)))
    o = jnp.moveaxis(o, 0, 1).reshape(B, S, B_HEADS, 2 * HEAD_DIM)
    o = rms_norm_2(o, subln) * (1.0 - lam_init)
    return o.reshape(B, S, BR_W)

def memory_cross_attention(q, mem_n, w_mem_kv):
    B, S, _ = q.shape
    k, v = jnp.split(mem_n @ w_mem_kv, 2, axis=-1)
    k = k.reshape(B, -1, MEM_HEADS, HEAD_DIM)
    v = v.reshape(B, -1, MEM_HEADS, HEAD_DIM)
    q = q.reshape(B, S, MEM_HEADS, HEAD_DIM)
    s = jnp.einsum('bshd,bmhd->bhsm', q, k, preferred_element_type=jnp.float32) * (HEAD_DIM ** -0.5)
    p = jax.nn.softmax(s, axis=-1).astype(v.dtype)
    o = jnp.einsum('bhsm,bmhd->bshd', p, v)
    return o.reshape(B, S, MEM_W)

def second_inputs(seed: int = 0) -> dict:
    key = jax.random.key(seed)
    ks = jax.random.split(key, 32)
    nrm = lambda k, shape, scale: scale * jax.random.normal(k, shape, jnp.float32)
    gain = lambda k, shape: 1.0 + 0.05 * jax.random.normal(k, shape, jnp.float32)
    return {
        'x': jax.random.normal(ks[0], (BATCH, SEQ, D_MODEL), jnp.float32),
        'mem': jax.random.normal(ks[1], (BATCH, MEM_LEN, D_MODEL), jnp.float32),
        'pre_norm': gain(ks[2], (DEPTH_2, D_MODEL)),
        'post_norm': gain(ks[3], (DEPTH_2, D_MODEL)),
        'w_out': nrm(ks[4], (DEPTH_2, MIX_W, D_MODEL), MIX_W ** -0.5),
        'mem_norm': gain(ks[5], (DEPTH_2, D_MODEL)),
        'w_mem_kv': nrm(ks[6], (DEPTH_2, D_MODEL, 2 * MEM_W), D_MODEL ** -0.5),
        'a_w_in': nrm(ks[7], (N_A, D_MODEL, A_IN), D_MODEL ** -0.5),
        'a_shift_mu': jax.random.uniform(ks[8], (N_A, A_SHIFT), jnp.float32),
        'a_w0': jax.random.uniform(ks[9], (N_A, BR_W), jnp.float32, minval=-6.0, maxval=0.0),
        'a_w2': nrm(ks[10], (N_A, LORA_W, BR_W), 0.5 * LORA_W ** -0.5),
        'a_a0': nrm(ks[11], (N_A, BR_W), 0.1),
        'a_a2': nrm(ks[12], (N_A, LORA_A, BR_W), 0.5 * LORA_A ** -0.5),
        'a_k_k': 0.85 + 0.05 * jax.random.normal(ks[13], (N_A, BR_W), jnp.float32),
        'a_k_a': gain(ks[14], (N_A, BR_W)),
        'a_r_k': nrm(ks[15], (N_A, A_HEADS, HEAD_DIM), 0.1),
        'a_lnx_w': gain(ks[16], (N_A, BR_W)),
        'a_lnx_b': nrm(ks[17], (N_A, BR_W), 0.02),
        'kv_norm': gain(ks[18], (D_MODEL,)),
        'w_kv': nrm(ks[19], (D_MODEL, 2 * BR_W), D_MODEL ** -0.5),
        'b_w_in': nrm(ks[20], (N_B, D_MODEL, B_IN), D_MODEL ** -0.5),
        'b_lam_q1': nrm(ks[21], (N_B, HEAD_DIM), 0.1),
        'b_lam_k1': nrm(ks[22], (N_B, HEAD_DIM), 0.1),
        'b_lam_q2': nrm(ks[23], (N_B, HEAD_DIM), 0.1),
        'b_lam_k2': nrm(ks[24], (N_B, HEAD_DIM), 0.1),
        'b_subln': gain(ks[25], (N_B, 2 * HEAD_DIM)),
    }

def second_block(x, mem, pre_norm, post_norm, w_out, mem_norm, w_mem_kv,
              a_w_in, a_shift_mu, a_w0, a_w2, a_a0, a_a2, a_k_k, a_k_a, a_r_k, a_lnx_w, a_lnx_b,
              kv_norm, w_kv,
              b_w_in, b_lam_q1, b_lam_k1, b_lam_q2, b_lam_k2, b_subln):
    k_sh = None
    v_sh = None
    for l in range(DEPTH_2):
        h = rms_norm_2(x, pre_norm[l])
        mem_n = rms_norm_2(mem, mem_norm[l])
        if l < N_A:
            i = l
            proj = h @ a_w_in[i]
            z, gate, q_mem, g_mem = jnp.split(
                proj, [A_SHIFT, A_SHIFT + BR_W, A_SHIFT + BR_W + MEM_W], axis=-1)
            y_br = rwkv7_time_mix(z, a_shift_mu[i], a_w0[i], a_w2[i], a_a0[i], a_a2[i],
                                  a_k_k[i], a_k_a[i], a_r_k[i], a_lnx_w[i], a_lnx_b[i])
        else:
            if l == N_A:
                k_sh, v_sh = jnp.split(rms_norm_2(x, kv_norm) @ w_kv, 2, axis=-1)
            i = l - N_A
            proj = h @ b_w_in[i]
            q, gate, q_mem, g_mem = jnp.split(
                proj, [BR_W, 2 * BR_W, 2 * BR_W + MEM_W], axis=-1)
            lam_init = 0.8 - 0.6 * math.exp(-0.3 * l)
            y_br = diff_attention(q, k_sh, v_sh, b_lam_q1[i], b_lam_k1[i], b_lam_q2[i],
                                  b_lam_k2[i], b_subln[i], lam_init)
        y_mem = memory_cross_attention(q_mem, mem_n, w_mem_kv[l])
        y = jnp.concatenate([(y_br * jax.nn.silu(gate.astype(jnp.float32))).astype(x.dtype),
                             y_mem * jax.nn.silu(g_mem)], axis=-1) @ w_out[l]
        x = x + rms_norm_2(y, post_norm[l])
    return x


def setup_inputs(seed=0):
    out = dict(first_inputs(seed))
    for name, value in second_inputs(seed + 1).items():
        if name != "x":
            out[name + "_2"] = value
    return out


def reference(
    x, p, g_mix_pre, w_in, b_forget, g_attn_grp, g_pool_grp, w_pool, pool_scale, w_out,
    g_mix_post, g_ffn_pre, w_ffn_gate, w_ffn_up, w_ffn_down, g_ffn_post, w_ple_proj, g_ple,
    w_ple_gate, mem_2, pre_norm_2, post_norm_2, w_out_2, mem_norm_2, w_mem_kv_2, a_w_in_2,
    a_shift_mu_2, a_w0_2, a_w2_2, a_a0_2, a_a2_2, a_k_k_2, a_k_a_2, a_r_k_2, a_lnx_w_2,
    a_lnx_b_2, kv_norm_2, w_kv_2, b_w_in_2, b_lam_q1_2, b_lam_k1_2, b_lam_q2_2, b_lam_k2_2,
    b_subln_2,
):
    x = first_block(
        x, p, g_mix_pre, w_in, b_forget, g_attn_grp, g_pool_grp, w_pool, pool_scale, w_out,
        g_mix_post, g_ffn_pre, w_ffn_gate, w_ffn_up, w_ffn_down, g_ffn_post, w_ple_proj, g_ple,
        w_ple_gate,
    )
    return second_block(
        x, mem_2, pre_norm_2, post_norm_2, w_out_2, mem_norm_2, w_mem_kv_2, a_w_in_2,
        a_shift_mu_2, a_w0_2, a_w2_2, a_a0_2, a_a2_2, a_k_k_2, a_k_a_2, a_r_k_2, a_lnx_w_2,
        a_lnx_b_2, kv_norm_2, w_kv_2, b_w_in_2, b_lam_q1_2, b_lam_k1_2, b_lam_q2_2, b_lam_k2_2,
        b_subln_2,
    )


_drawn_inputs = setup_inputs


def setup_inputs(seed=0):
    import zlib

    import numpy as np

    out = dict(_drawn_inputs(seed))
    spreads = {}
    factors = {'mem_norm_2': 8.0,
     'a_w2_2': 8.398,
     'a_lnx_b_2': 13.529,
     'b_lam_k1_2': 4.654,
     'b_subln_2': 15.966,
     'a_a0_2': 6.11,
     'a_k_k_2': 6.032,
     'a_k_a_2': 4.831,
     'a_lnx_w_2': 4.992,
     'kv_norm_2': 3.589}
    for name, (base, spread) in spreads.items():
        noise = np.random.default_rng([zlib.crc32(name.encode()), seed]).standard_normal(out[name].shape)
        drawn = base * np.exp(spread * noise) if base else spread * noise
        out[name] = __import__('jax').numpy.asarray(drawn.astype(out[name].dtype))
    for name, factor in factors.items():
        out[name] = (out[name] * factor).astype(out[name].dtype)
    return out
```

```python
import math
from contextlib import ExitStack, contextmanager

import numpy as np
import concourse.bass as bass
import concourse.mybir as mybir

F32 = mybir.dt.float32
ALU = mybir.AluOpType
ACT = mybir.ActivationFunctionType
AX = mybir.AxisListType
ds = bass.ds

P = 128
D = 1024
S = 1024
KT = D // P
ST = S // P
HALF = 512
EPS = 1e-6
NEG = -1.0e30

HD = 64
ATT_H = 8
ATT_W = ATT_H * HD
POOL_G = 4
FF = 2816
FT = FF // P
PLE = 256
MEM = 256
MEM_W = 256
BR = 768
BT = BR // P
LORA = 64
LNX_EPS = 64e-5
CH = 64
NCH = S // CH
LAM_INIT = 0.8 - 0.6 * math.exp(-0.3)
DECAY_C = math.exp(-0.5)


class Tick:

    def __init__(self, sem, loop, base, k):
        self.sem, self.loop, self.base, self.k = sem, loop, base, k


class Chip:

    def __init__(self, nc, ctx, known):
        self.nc, self.ctx, self.known = nc, ctx, known
        self.pe, self.act, self.dve, self.pool, self.sp = nc.tensor, nc.scalar, nc.vector, nc.gpsimd, nc.sync
        self.engines = {"pe": self.pe, "act": self.act, "dve": self.dve, "pool": self.pool}
        self.names = {id(e): n for n, e in (*self.engines.items(), ("sp", self.sp))}
        self.sems, self.count, self.seen = {}, {}, {}
        self.loop, self.n_loops = None, 0
        self.fresh = {}
        self.idle = ctx.enter_context(nc.semaphore("s_idle"))
        for n, e in self.engines.items():
            self.new_sem(n, e)

    def new_sem(self, name, engine=None):
        self.sems[name] = self.ctx.enter_context(self.nc.semaphore("s_" + name))
        start = max([v for k, v in self.known.items() if k[0] == "per" and k[2] == name], default=0)
        self.count[name] = start
        if start:
            engine = engine or self.sp
            engine.sem_inc(self.sems[name], start)
            engine.wait_ge(self.sems[name], start)
        return name

    def mark(self, name, instruction, by=1, label=None):
        instruction.then_inc(self.sems[name], by)
        self.count[name] += by
        if not self.loop:
            return Tick(name, None, self.count[name], 0)
        base = self.loop["base"].get(name, 0)
        if label:
            self.known["label", self.loop["id"], label] = (name, self.count[name] - base)
        return Tick(name, self.loop, base, self.count[name] - base)

    def on_pe(self, ins, label=None):
        return self.mark("pe", ins, label=label)

    def on_act(self, ins, label=None):
        return self.mark("act", ins, label=label)

    def on_dve(self, ins, label=None):
        return self.mark("dve", ins, label=label)

    def on_pool(self, ins, label=None):
        return self.mark("pool", ins, label=label)

    def load(self, sem, out, in_, label=None):
        self.settle(self.sp)
        return self.mark(sem, self.sp.dma_start(out, in_), 16, label)

    def wait(self, engine, *ticks):
        for t in ticks:
            if t is None:
                continue
            e = self.names[id(engine)]
            if t.loop is not None and t.loop is self.loop:
                self._wait_in_loop(engine, t.sem, t.k, t.base)
                continue
            value = t.base if t.loop is None else t.base + t.loop["per"][t.sem] * (t.loop["n"] - 1) + t.k
            if self.seen.get((e, t.sem, None), 0) < value:
                self.seen[e, t.sem, None] = value
                engine.wait_ge(self.sems[t.sem], value)

    def wait_before(self, engine, *labels):
        for label in labels:
            sem, k = self.known.get(("label", self.loop["id"], label), ("pe", 0))
            per = self.known.get(("per", self.loop["id"], sem), 4096)
            self._wait_in_loop(engine, sem, k - per, self.loop["base"].get(sem, 0))

    def _wait_in_loop(self, engine, sem, k, base):
        per = self.known.get(("per", self.loop["id"], sem), 4096)
        key = (self.names[id(engine)], sem, self.loop["id"])
        if self.seen.get(key, -1 << 40) < k:
            self.seen[key] = k
            engine.wait_ge(self.sems[sem], self.loop["i"] * per + max(base + k, 0))
            self.fresh[self.names[id(engine)]] = True
            if engine is self.sp:
                self.settle(engine)

    def settle(self, engine):
        if self.loop and self.fresh.pop(self.names[id(engine)], False):
            engine.sem_inc(self.idle, 1)

    @contextmanager
    def fori(self, n):
        assert self.loop is None
        self.n_loops += 1
        base = dict(self.count)
        with self.nc.Fori(0, n) as i:
            self.loop = dict(id=self.n_loops, i=i, base=base, n=n)
            yield i
        per = {s: self.count[s] - b for s, b in base.items()}
        for s, marks in per.items():
            self.known["per", self.n_loops, s] = marks
            self.count[s] = base[s] + n * marks
        self.loop["per"] = per
        self.loop = None

    def now_in(self, name):
        base = self.loop["base"].get(name, 0)
        return Tick(name, self.loop, base, self.count[name] - base)

    def now(self, name):
        assert self.loop is None
        return Tick(name, None, self.count[name], 0)

    def join(self, *engines):
        for e in engines or self.engines.values():
            self.wait(e, *(self.now(n) for n in self.engines))


class Mem:

    def __init__(self, tile):
        self.tile = tile

    def at(self, col, *shape):
        n = math.prod(shape)
        ap = self.tile[:, col:col + n]
        if len(shape) == 1:
            return ap
        names = "abcd"[:len(shape)]
        sizes = {names[j]: shape[j] for j in range(1, len(shape))}
        return ap.rearrange(f"p ({' '.join(names)}) -> p {' '.join(names)}", **sizes)


def over_tokens(vec, n):
    return vec.unsqueeze(2).broadcast_to((P, vec.shape[1], n))


def over_pairs(mask, n=BT):
    return mask.unsqueeze(1).broadcast_to((mask.shape[0], n, mask.shape[1]))


VEC_ROWS = [
    ("g_mix_pre", 8), ("g_attn_grp", 4), ("g_pool_grp", 4), ("pool_scale", 4), ("g_mix_post", 8),
    ("g_ffn_pre", 8), ("g_ffn_post", 8), ("g_ple", 8), ("pre_norm_2", 16), ("post_norm_2", 16),
    ("mem_norm_2", 16), ("a_shift_mu_2", 19),
    ("a_w0_2", 6), ("a_a0_2", 6), ("a_k_k_2", 6), ("a_k_a_2", 6), ("a_r_k_2", 6),
    ("a_lnx_w_2", 6), ("a_lnx_b_2", 6), ("kv_norm_2", 8), ("b_subln_2", 1),
]


def build(nc, A, out, known, upto="all"):
    with ExitStack() as ctx:
        c = Chip(nc, ctx, known)
        k = Kernel(c, ctx, A, out)
        k.constants()
        k.load_x()
        if upto != "b2":
            k.block_one()
        if upto != "b1":
            k.block_two()
        k.store()


class Kernel:
    X = 0
    HN = 8192
    W = 16384
    WSLOT = FT * P // 2
    CONST = W + 4 * (FT * P // 2)
    BIG = CONST + 3328

    def __init__(self, c, ctx, A, out):
        self.c, self.A, self.out = c, A, out
        nc = c.nc
        cols = 53200
        self.sb = Mem(ctx.enter_context(nc.sbuf_tensor("sb", [P, cols], F32)))
        self.ps = ctx.enter_context(nc.psum_tensor("ps", [P, 8, HALF], F32))
        self.x = self.sb.at(self.X, KT, S)
        self.hn = self.sb.at(self.HN, KT, S)
        self.wsem = [c.new_sem(f"w{j}") for j in range(4)]
        self.wfree = [None] * 4
        self.ring = 0
        self.io = [c.new_sem("io0"), c.new_sem("io1")]
        self.misc = c.new_sem("misc")
        self.scratch_c = nc.dram_tensor("negc", [ATT_H, S], F32).ap()
        col = self.CONST
        def const(*shape):
            nonlocal col
            ap = self.sb.at(col, *shape)
            col += math.prod(shape)
            return ap
        self.ident, self.ones, self.block64 = const(P), const(P), const(P)
        self.n_vec = sum(n for _, n in VEC_ROWS)
        self.vecs = const(self.n_vec)
        self.vec, at = {}, 0
        for name, n in VEC_ROWS:
            self.vec[name] = self.vecs[:, at:at + n]
            at += n
        self.eps, self.lnx_eps, self.stat = const(1), const(1), const(64)
        self.low = const(CH)
        self.up_col = col
        self.up, self.upi, self.eye = const(CH), const(CH), const(CH)
        self.level = [const(CH) for _ in range(6)]
        self.level0t = const(CH)
        self.slopes, self.neglam = const(BT), const(1)
        self.sel = const(BT, 12)
        self.selt = const(BR)
        assert col <= self.BIG, col - self.CONST


    def constants(self):
        c, sb, A = self.c, self.sb, self.A
        I32 = mybir.dt.int32

        def step(ins):
            c.wait(c.pool, c.on_pool(ins))
        pool, dve = c.pool, c.dve
        step(pool.memset(self.ident, 0.0))
        step(pool.memset(self.ones, 1.0))
        step(pool.memset(self.block64, 0.0))
        step(pool.memset(self.eps, EPS))
        step(pool.memset(self.lnx_eps, LNX_EPS))
        rows = sb.at(self.BIG, 2, P)
        step(pool.memset(rows, 0.0))
        step(pool.memset(self.sel, 0.0))
        step(pool.memset(self.selt, 0.0))
        for j in range(BT):
            slope = 2.0 ** (-2.0 * (j + 1)) if j < 4 else 2.0 ** (-1.0 - 2.0 * (j - 4))
            step(pool.memset(self.slopes[:, j:j + 1], slope))
        t = c.now("pool")
        c.wait(pool, t)
        for h in range(2):
            o = 64 * h
            step(pool.memset(self.block64[o:o + 64, o:o + 64], 1.0 / 64))
            for p in range(BT):
                step(pool.memset(self.sel[o:o + 64, p, 2 * p + h:2 * p + h + 1], 1.0))
        step(pool.affine_select(self.ident, self.ident, [[-1, P]], ALU.not_equal, 1.0, base=0,
                                     channel_multiplier=1))
        keep = sb.at(self.BIG + 512, BR)
        step(pool.memset(keep, 1.0))
        t = c.now("pool")
        c.wait(pool, t)
        step(pool.affine_select(keep[0:12], keep[0:12], [[1, BR]], ALU.is_ge, 0.0, base=0,
                                     channel_multiplier=-64))
        c.wait(pool, c.now("pool"))
        step(pool.affine_select(self.selt[0:12], keep[0:12], [[-1, BR]], ALU.is_ge, 0.0, base=63,
                                     channel_multiplier=64))
        ri, ci, xi = (sb.at(self.BIG + 2048 + CH * j, CH).bitcast(I32) for j in range(3))
        rf, cf = (sb.at(self.BIG + 2048 + CH * (3 + j), CH) for j in range(2))
        si = [sb.at(self.BIG + 2048 + CH * (5 + j), CH).bitcast(I32) for j in range(6)]
        sf = [sb.at(self.BIG + 2048 + CH * (11 + j), CH) for j in range(6)]
        for h in range(2):
            step(pool.iota(ri[64 * h:64 * h + 64], [[0, CH]], base=0, channel_multiplier=1))
        step(pool.iota(ci, [[1, CH]], base=0, channel_multiplier=0))
        c.wait(dve, c.now("pool"))
        c.on_dve(dve.tensor_copy(rf, ri))
        c.on_dve(dve.tensor_copy(cf, ci))
        c.on_dve(dve.tensor_tensor(xi, ri, ci, ALU.bitwise_xor))
        c.wait(dve, c.now("dve"))
        c.on_dve(dve.tensor_tensor(self.low, rf, cf, ALU.is_gt))
        c.on_dve(dve.tensor_tensor(self.up, cf, rf, ALU.is_gt))
        c.on_dve(dve.tensor_tensor(self.upi, cf, rf, ALU.is_ge))
        c.on_dve(dve.tensor_tensor(self.eye, cf, rf, ALU.is_equal))
        for j in range(6):
            c.on_dve(dve.tensor_scalar(si[j], xi, j, None, ALU.logical_shift_right))
        c.wait(dve, c.now("dve"))
        for j in range(6):
            c.on_dve(dve.tensor_copy(sf[j], si[j]))
        c.wait(dve, c.now("dve"))
        for j in range(6):
            c.on_dve(dve.scalar_tensor_tensor(self.level[j], sf[j], 1.0, self.low, ALU.is_equal, ALU.mult))
        c.on_dve(dve.scalar_tensor_tensor(self.level0t, sf[0], 1.0, self.up, ALU.is_equal, ALU.mult))
        c.wait(c.sp, c.now("pool"))
        at = 0
        for name, n in VEC_ROWS:
            v = A[name]
            flat = v if len(v.shape) == 1 else v.rearrange("a b -> (a b)") if len(v.shape) == 2 else v.rearrange("a b d -> (a b d)")
            v = flat.rearrange("(r p) -> r p", p=P)
            done = 0
            while done < n:
                m = min(n - done, P - at % P)
                t = c.load(self.misc, rows[at % P:at % P + m, at // P, :], v[done:done + m, :])
                at, done = at + m, done + m
        c.wait(c.pe, t, c.now("pool"))
        c.on_pe(c.pe.transpose(self.ps[:, 0, 0:P], rows[:, 0, :], self.ident))
        c.on_pe(c.pe.transpose(self.ps[:, 0, P:2 * P], rows[:, 1, :], self.ident))
        c.wait(dve, c.now("pe"))
        c.on_dve(dve.tensor_copy(self.vecs, self.ps[:, 0, 0:self.n_vec]))
        c.join()


    def load_rows(self, src, n_rows, n_cols, dst, at):
        c, kt = self.c, n_cols // P
        stage = [self.sb.at(at + j * n_cols, n_cols) for j in range(2)]
        c.wait(c.sp, *(c.now(n) for n in c.engines))
        with c.fori(n_rows // (2 * P)) as i:
            for j in range(2):
                c.wait_before(c.sp, f"turned{j}")
                t = c.load(self.io[j], stage[j], src[ds(i * 2 * P + j * P, P), :])
                c.wait(c.pe, t)
                c.wait_before(c.pe, *(f"copied{j}{b}" for b in range((kt + 3) // 4)))
                for f in range(kt):
                    t = c.pe.transpose(self.ps[:, 2 * j + f // 4, (f % 4) * P:(f % 4 + 1) * P],
                                       stage[j][:, f * P:(f + 1) * P], self.ident)
                t = c.on_pe(t, label=f"turned{j}")
                for b in range((kt + 3) // 4):
                    n = min(4, kt - 4 * b)
                    to = dst[:, 4 * b:4 * b + n, ds(i * 2 * P + j * P, P)]
                    fr = self.ps[:, 2 * j + b, 0:n * P].rearrange("p (a b) -> p a b", a=n)
                    if b == 0:
                        c.wait(c.dve, t)
                        c.on_dve(c.dve.tensor_copy(to, fr), label=f"copied{j}0")
                    else:
                        c.wait(c.act, t)
                        c.on_act(c.act.copy(to, fr), label=f"copied{j}1")
        c.join()

    def load_x(self):
        self.load_rows(self.A["x"].rearrange("b s d -> (b s) d"), S, D, self.x, self.BIG)


    def rstd(self, tiles, n, width, eps, out, tmp):
        c = self.c
        acc = self.sb.at(tmp, n)
        sq = [self.sb.at(tmp + n * (1 + j), n) for j in range(2)]
        c.wait(c.act, *(c.now(e) for e in c.engines))
        t = c.on_act(c.act.activation(acc, tiles[0], ACT.Square))
        added = [None, None]
        for j, tile in enumerate(tiles[1:]):
            c.wait(c.act, added[j % 2])
            s = c.on_act(c.act.activation(sq[j % 2], tile, ACT.Square))
            c.wait(c.dve, t, s)
            t = added[j % 2] = c.on_dve(c.dve.tensor_tensor(acc, acc, sq[j % 2], ALU.add))
        c.wait(c.pe, t, *(c.now(e) for e in c.engines))
        for h in range(0, n, HALF):
            m = min(HALF, n - h)
            t = c.on_pe(c.pe.matmul(self.ps[:, h // HALF, 0:m], self.ones, acc[:, h:h + m], start=True, stop=True))
        c.wait(c.act, t)
        src = self.ps[:, 0:(n + HALF - 1) // HALF, :].rearrange("p a b -> p (a b)")[:, 0:n]
        c.wait(c.act, c.on_act(c.act.activation(out, src, ACT.Ln, bias=eps, scale=1.0 / width)))
        return c.on_act(c.act.activation(out, out, ACT.Exp, scale=-0.5))

    def scale_tiles(self, dst, src, gain, rstd):
        c = self.c
        c.wait(c.dve, *(c.now(e) for e in c.engines))
        for j in range(len(src)):
            c.on_dve(c.dve.scalar_tensor_tensor(dst[j], src[j], gain[:, j:j + 1], rstd, ALU.mult, ALU.mult))

    def norm_x(self, gain, tmp):
        r = self.sb.at(tmp, S)
        tiles = [self.x[:, j, :] for j in range(KT)]
        self.rstd(tiles, S, D, self.eps, r, tmp + S)
        self.scale_tiles([self.hn[:, j, :] for j in range(KT)], tiles, gain, r)
        self.c.join()

    def add_normed(self, y, gain, tmp):
        c = self.c
        r = self.sb.at(tmp, S)
        self.rstd([y[:, j, :] for j in range(KT)], S, D, self.eps, r, tmp + S)
        c.wait(c.dve, *(c.now(e) for e in c.engines))
        for j in range(KT):
            t = c.on_dve(c.dve.scalar_tensor_tensor(y[:, j, :], y[:, j, :], gain[:, j:j + 1], r, ALU.mult, ALU.mult))
            c.wait(c.pool, t)
            c.on_pool(c.pool.tensor_tensor(self.x[:, j, :], self.x[:, j, :], y[:, j, :], ALU.add))
        c.join()


    def linear(self, w, nk, column, n, x, evac, n_cols=S, width=P):
        c = self.c
        slots = (0, 1) if self.ring == 0 else (2, 3)
        banks = 0 if self.ring == 0 else 4
        self.ring ^= 1
        wt = [self.sb.at(self.W + s * self.WSLOT, nk, P) for s in slots] if nk <= 11 else \
             [self.sb.at(self.W + 2 * j * self.WSLOT, nk, P) for j in range(2)]
        halves = (n_cols + HALF - 1) // HALF
        c.wait(c.sp, *(self.wfree if nk > 11 else [self.wfree[s] for s in slots]))
        wv = [m.rearrange("(k p) n -> p k n", p=P) for m in (w if isinstance(w, list) else [w, w])]
        c.wait(c.pe, *(c.now(e) for e in c.engines))
        with c.fori(n) as i:
            for j in range(2):
                c.wait_before(c.sp, f"read{j}")
                t = c.load(self.wsem[slots[j]], wt[j][:, :, 0:width], wv[j][:, :, ds(column(i, j), width)])
                c.wait(c.pe, t)
                for h in range(halves):
                    m = min(HALF, n_cols - h * HALF)
                    bank = self.ps[0:width, banks + 2 * j + h, 0:m]
                    c.wait_before(c.pe, f"bank{j}{h}")
                    for q in range(nk):
                        t = c.pe.matmul(bank, wt[j][:, q, 0:width], x[:, q, h * HALF:h * HALF + m],
                                        start=(q == 0), stop=(q == nk - 1))
                    t = c.on_pe(t, label=f"read{j}" if h == halves - 1 else None)
                    if h == halves - 1:
                        last = t
                    free = evac(i, j, h, bank, t)
                    c.known["label", c.loop["id"], f"bank{j}{h}"] = (free.sem, free.k)
        for s in (range(4) if nk > 11 else slots):
            self.wfree[s] = last
        c.join()

    def linear_once(self, w, nk, col, width, x, evac, n_cols=S):
        c = self.c
        c.wait(c.sp, *self.wfree)
        wt = self.sb.at(self.W, nk, P)[:, :, 0:width]
        t = c.load(self.wsem[0], wt, w.rearrange("(k p) n -> p k n", p=P)[:, :, col:col + width])
        c.wait(c.pe, t, *(c.now(e) for e in c.engines))
        for h in range((n_cols + HALF - 1) // HALF):
            m = min(HALF, n_cols - h * HALF)
            bank = self.ps[0:width, h, 0:m]
            for q in range(nk):
                t = c.pe.matmul(bank, wt[:, q, :], x[:, q, h * HALF:h * HALF + m], start=(q == 0), stop=(q == nk - 1))
            t = c.on_pe(t)
            evac(h, bank, t)
        self.wfree = [t] * 4
        c.join()

    def linear_tokens(self, w, col, width, blocks, x, dst, rows=S):
        c = self.c
        wt = self.sb.at(self.W, KT, width)
        assert KT * width <= 4 * self.WSLOT
        c.wait(c.sp, *self.wfree)
        wv = w.rearrange("(k p) n -> p k n", p=P)
        c.wait(c.pe, *(c.now(e) for e in c.engines))
        with c.fori(blocks) as i:
            c.wait_before(c.sp, "read")
            t = c.load(self.wsem[0], wt, wv[:, :, ds(i * width + col, width)])
            c.wait(c.pe, t)
            for s in range(rows // P):
                bank = self.ps[:, s % 8, 0:width]
                c.wait_before(c.pe, f"bank{s}")
                for q in range(KT):
                    t = c.pe.matmul(bank, x[:, q, s * P:(s + 1) * P], wt[:, q, :], start=(q == 0), stop=(q == KT - 1))
                t = c.on_pe(t, label="read")
                to = dst[:, s, ds(i * width, width)]
                if s % 2:
                    c.wait(c.dve, t)
                    c.on_dve(c.dve.tensor_copy(to, bank), label=f"bank{s}")
                else:
                    c.wait(c.act, t)
                    c.on_act(c.act.copy(to, bank), label=f"bank{s}")
        self.wfree = [t] * 4
        c.join()

    def to(self, dst):
        c = self.c

        def evac(i, j, h, bank, t):
            m = bank.shape[1]
            d = dst(i, j)[:, h * HALF:h * HALF + m]
            if h == 0:
                c.wait(c.act, t)
                return c.on_act(c.act.copy(d, bank))
            c.wait(c.dve, t)
            return c.on_dve(c.dve.tensor_copy(d, bank))
        return evac


    def attention(self, n, q, k, v, out, at, nkeys, bias=None, per_pair=None, diff=False):
        c, ps = self.c, self.ps
        qz = self.sb.at(at, 2, S)
        sc = self.sb.at(at + 2 * S, 4, S)
        pt = self.sb.at(at + 6 * S, 2, HALF)
        on = self.sb.at(at + 7 * S, 2, P)
        st = self.stat
        c.on_dve(c.dve.memset(qz, 0.0))
        c.join()
        with c.fori(n) as i:
            if per_pair:
                per_pair(i)
            c.wait_before(c.act, "last_scores")
            for h in range(2):
                o = 64 * h
                staged = c.on_act(c.act.activation(qz[o:o + 64, h, :], q(i)[o:o + 64, :], ACT.Copy, scale=0.125))
            exped, normed, scored = {}, {}, {}
            freed = {}
            group = [0]

            def scores(u):
                iq, h = divmod(u, 2)
                nk = nkeys(iq)
                bank = ps[:, 2 * h:2 * h + 2, :].rearrange("p a b -> p (a b)")
                c.wait(c.pe, staged)
                if u < 2:
                    c.wait_before(c.pe, f"sfree{h}")
                else:
                    c.wait(c.pe, freed["s", h])
                for b in range(0, nk, HALF):
                    m = min(HALF, nk - b)
                    t = c.pe.matmul(bank[:, b:b + m], qz[:, h, iq * P:(iq + 1) * P], k(i)[:, b:b + m], start=True, stop=True)
                t = c.on_pe(t, label="last_scores")
                buf = sc[:, u % 4, 0:nk]
                s4 = st[:, 4 * (u % 16):4 * (u % 16) + 4]
                if u < 4:
                    c.wait_before(c.dve, f"buf{u}")
                    c.wait_before(c.act, f"buf{u}")
                else:
                    c.wait(c.dve, freed["buf", u % 4])
                    c.wait(c.act, freed["buf", u % 4])
                c.wait(c.dve, t)
                if bias:
                    add, ready = bias(h, iq, freed)
                    c.wait(c.dve, ready)
                    c.settle(c.dve)
                    t = c.on_dve(c.dve.tensor_tensor_reduce(buf, bank[:, 0:nk], add, 1.0, -3.0e38, ALU.add, ALU.max, s4[:, 0:1]),
                                 label=f"bias{h}{iq % 2}")
                    freed["s", h] = t
                    src = buf
                    freed["bias", h, iq] = t
                else:
                    t = c.on_dve(c.dve.tensor_reduce(s4[:, 0:1], bank[:, 0:nk], AX.X, ALU.max))
                    src = bank[:, 0:nk]
                c.wait(c.dve, t)
                t = c.on_dve(c.dve.tensor_scalar(s4[:, 1:2], s4[:, 0:1], -1.0, None, ALU.mult))
                c.wait(c.act, t)
                t = c.on_act(c.act.activation(buf, src, ACT.Exp, bias=s4[:, 1:2], accum_out=s4[:, 2:3]))
                if not bias:
                    freed["s", h] = t
                exped[u] = t
                if u >= 2 * ST - 2:
                    f = freed["s", h]
                    c.known["label", c.loop["id"], f"sfree{h}"] = (f.sem, f.k)
                c.wait(c.dve, t)
                normed[u] = c.on_dve(c.dve.reciprocal(s4[:, 3:4], s4[:, 2:3]))

            def turned(src, src_tick, nj, use):
                for g in range(0, nj, 4):
                    m = min(4, nj - g)
                    b = group[0] % 2
                    group[0] += 1
                    c.wait(c.pe, src_tick)
                    if group[0] <= 2:
                        c.wait_before(c.pe, f"ptbank{b}")
                    else:
                        c.wait(c.pe, freed["ptbank", b])
                    for j in range(m):
                        t = c.pe.transpose(ps[:, 4 + b, j * P:(j + 1) * P], src[:, (g + j) * P:(g + j + 1) * P], self.ident)
                    t = c.on_pe(t)
                    e, on_e, cp = (c.act, c.on_act, c.act.copy) if b else (c.dve, c.on_dve, c.dve.tensor_copy)
                    c.wait(e, t)
                    if group[0] <= 2:
                        c.wait_before(e, f"pt{b}")
                    else:
                        c.wait(e, freed["pt", b])
                    t = freed["ptbank", b] = on_e(cp(pt[:, b, 0:m * P], ps[:, 4 + b, 0:m * P]), label=f"ptbank{b}")
                    pending.append((b, g, m, t, use))
                    flush(keep=1)

            pending = []

            def flush(keep=0):
                while len(pending) > keep:
                    b, g, m, t, use = pending.pop(0)
                    c.wait(c.pe, t)
                    for j in range(m):
                        t = use(g + j, pt[:, b, j * P:(j + 1) * P])
                    freed["pt", b] = c.on_pe(t, label=f"pt{b}")

            def post(iq):
                nj = nkeys(iq) // P
                ob = ps[:, 6 + iq % 2, :]
                if iq < 2:
                    c.wait_before(c.pe, f"obank{iq}")
                else:
                    c.wait(c.pe, freed["obank", iq % 2])
                u0, u1 = 2 * iq, 2 * iq + 1
                s0 = st[:, 4 * (u0 % 16):4 * (u0 % 16) + 4]
                s1 = st[:, 4 * (u1 % 16):4 * (u1 % 16) + 4]
                o = on[:, iq % 2, :]
                if diff:
                    c.wait(c.dve, normed[u1])
                    t = c.on_dve(c.dve.scalar_tensor_tensor(s1[:, 0:1], s0[:, 2:3], self.neglam, s1[:, 3:4], ALU.mult, ALU.mult))
                    c.wait(c.dve, t, exped[u0], exped[u1])
                    w = nkeys(iq)
                    t = c.on_dve(c.dve.scalar_tensor_tensor(sc[:, u0 % 4, 0:w], sc[:, u1 % 4, 0:w], s1[:, 0:1],
                                                            sc[:, u0 % 4, 0:w], ALU.mult, ALU.add))
                    freed["buf", u1 % 4] = t
                    turned(sc[:, u0 % 4, :], t, nj, lambda j, tile: c.pe.matmul(
                        ob[:, 0:P], tile, v(i, j), start=(j == 0), stop=(j == nj - 1)))
                    freed["buf", u0 % 4] = c.now_in("pe")
                    if iq >= ST - 2:
                        for u in (u0, u1):
                            f = freed["buf", u % 4]
                            c.known["label", c.loop["id"], f"buf{u % 4}"] = (f.sem, f.k)
                    flush()
                    c.wait(c.dve, freed["pt", (group[0] - 1) % 2])
                    t = c.on_dve(c.dve.tensor_scalar(o, ob[:, 0:P], s0[:, 3:4], None, ALU.mult), label=f"obank{iq % 2}")
                else:
                    for h, u in ((0, u0), (1, u1)):
                        def use(j, tile, h=h):
                            return c.pe.matmul(ob[:, 64 * h:64 * h + 64], tile, v(i, j)[:, 64 * h:64 * h + 64],
                                               start=(j == 0), stop=(j == nj - 1))
                        turned(sc[:, u % 4, :], exped[u], nj, use)
                        freed["buf", u % 4] = c.now_in("pe")
                        if iq >= ST - 2:
                            f = freed["buf", u % 4]
                            c.known["label", c.loop["id"], f"buf{u % 4}"] = (f.sem, f.k)
                    flush()
                    c.wait(c.dve, freed["pt", (group[0] - 1) % 2], normed[u0], normed[u1])
                    for h, s in ((0, s0), (1, s1)):
                        t = c.on_dve(c.dve.tensor_scalar(o[:, 64 * h:64 * h + 64], ob[:, 64 * h:64 * h + 64], s[:, 3:4],
                                                         None, ALU.mult), label=f"obank{iq % 2}")
                freed["obank", iq % 2] = t
                c.wait(c.pe, t)
                t = c.on_pe(c.pe.transpose(ob[:, P:2 * P], o, self.ident))
                c.wait(c.act, t)
                c.settle(c.act)
                t = c.on_act(c.act.copy(out(i, iq), ob[:, P:2 * P]), label=f"obank{iq % 2}")
                freed["obank", iq % 2] = t

            scores(0)
            scores(1)
            for iq in range(ST):
                if iq + 1 < ST:
                    scores(2 * iq + 2)
                    scores(2 * iq + 3)
                post(iq)
        c.join()


    def block_one(self):
        self.mixer()
        self.feed_forward()
        self.embedding_gate()

    def mixer(self):
        c, sb, A, ps = self.c, self.sb, self.A, self.ps
        B = self.BIG
        w_in = A["w_in"].rearrange("l a b -> (l a) b")
        q, k = sb.at(B, 4, S), sb.at(B + 4096, 4, S)
        v = sb.at(B + 8192, ST, ATT_W)
        at = B + 12288
        LEAD = 16
        u = sb.at(at, POOL_G, LEAD + S)
        self.norm_x(self.vec["g_mix_pre"], B + 16384)

        def qk(i, j):
            return sb.at(B, KT, S)[:, ds(2 * i + j, 1), :].rearrange("p a b -> p (a b)")
        self.linear(w_in, KT, lambda i, j: (2 * i + j) * P, 4, self.hn, self.to(qk))
        c.on_pool(c.pool.memset(u[:, :, 0:LEAD], 0.0))
        u0 = 3 * ATT_W + ATT_H
        self.linear(w_in, KT, lambda i, j: (2 * i + j) * P + u0, 2, self.hn,
                    self.to(lambda i, j: u[:, ds(2 * i + j, 1), LEAD:].rearrange("p a b -> p (a b)")))
        self.linear_tokens(w_in, 2 * ATT_W, ATT_W, 1, self.hn, v)

        fz, fa, fone = sb.at(at + 4160, S), sb.at(at + 5184, S), sb.at(at + 6208, S)
        bf = self.stat[0:ATT_H, 0:1]
        c.wait(c.sp, *(c.now(e) for e in c.engines))
        tb = c.load(self.misc, bf, A["b_forget"].rearrange("l h -> (l h)").rearrange("(h o) -> h o", o=1))
        c.wait(c.dve, tb)

        def forget(h, bank, t):
            c.wait(c.dve, t)
            return c.on_dve(c.dve.tensor_scalar(fz[0:ATT_H, h * HALF:(h + 1) * HALF], bank, bf, None, ALU.add))
        self.linear_once(w_in, KT, 3 * ATT_W, ATT_H, self.hn, forget)
        z, a, one = fz[0:ATT_H], fa[0:ATT_H], fone[0:ATT_H]
        c.on_dve(c.dve.memset(one, 1.0))
        c.wait(c.act, c.on_act(c.act.activation(a, z, ACT.Abs)))
        c.wait(c.act, c.on_act(c.act.activation(a, a, ACT.Exp, scale=-1.0)))
        t = c.on_act(c.act.activation(a, a, ACT.Ln, bias=self.ones[0:ATT_H, 0:1]))
        c.wait(c.dve, t)
        t = c.on_dve(c.dve.scalar_tensor_tensor(a, z, 0.0, a, ALU.min, ALU.subtract))
        c.wait(c.dve, t)
        t = c.on_dve(c.dve.tensor_tensor_scan(z, one, a, 0.0, ALU.mult, ALU.subtract))
        c.wait(c.sp, t)
        c.load(self.misc, self.scratch_c, z)

        mix = self.hn
        s1, s2, inv = sb.at(at + 7232, LEAD + S), sb.at(at + 8272, LEAD + S), sb.at(at + 9312, S)
        pw = sb.at(self.W, POOL_G, P)
        c.wait(c.sp, *self.wfree)
        tw = c.load(self.wsem[0], pw, A["w_pool"].rearrange("l g a b -> (l g a) b").rearrange("(g a) b -> a g b", a=P))
        c.join()
        free = None
        for g in range(POOL_G):
            win = 2 << g
            src = u[:, g, :]
            c.wait(c.pool, *(c.now(e) for e in ("dve", "pe")))
            c.wait(c.pool, c.on_pool(c.pool.iota(inv, [[1, S]], base=1, channel_multiplier=0,
                                                 allow_small_or_imprecise_dtypes=True)))
            t = c.on_pool(c.pool.tensor_scalar(inv, inv, float(win), None, ALU.min))
            c.wait(c.dve, t)
            c.on_dve(c.dve.reciprocal(inv, inv))
            cur, bufs, step = src, [s1, s2], 1
            while step < win:
                nxt = bufs[0]
                bufs.reverse()
                c.on_dve(c.dve.memset(nxt[:, 0:LEAD], 0.0))
                t = c.on_dve(c.dve.tensor_tensor(nxt[:, LEAD:], cur[:, LEAD:], cur[:, LEAD - step:LEAD + S - step], ALU.add))
                c.wait(c.dve, t)
                cur, step = nxt, step * 2
            t = c.on_dve(c.dve.tensor_tensor(cur[:, LEAD:], cur[:, LEAD:], inv, ALU.mult))
            c.wait(c.dve, t)
            t = c.on_dve(c.dve.tensor_tensor(cur[:, LEAD:], cur[:, LEAD:], src[:, LEAD:], ALU.subtract))
            c.wait(c.pe, t, tw, free)
            for h in range(2):
                t = c.on_pe(c.pe.matmul(ps[:, h, :], pw[:, g, :], cur[:, LEAD + h * HALF:LEAD + (h + 1) * HALF], start=True, stop=True))
            c.wait(c.act, t)
            free = c.on_act(c.act.activation(mix[:, 4 + g, :], ps[:, 0:2, :].rearrange("p a b -> p (a b)"), ACT.Copy,
                                             scale=self.vec["pool_scale"][:, g:g + 1]))
        c.join()
        self.wfree = [c.now("pe")] * 4

        cb, bb = sb.at(at + 7424 + 0, 2, S), sb.at(at + 7424 + 2 * S, 4, S)

        masked = c.pool.to_reg(NEG)

        def rows_of_pair(i):
            c.wait_before(c.sp, "biased")
            self.tc = c.load(self.misc, cb, self.scratch_c[ds(2 * i, 2), :].partition_broadcast(P))

        def bias(h, iq, freed):
            buf = bb[:, 2 * h + iq % 2, 0:(iq + 1) * P]
            c.wait(c.pool, self.tc)
            if iq < 2:
                c.wait_before(c.pool, f"bias{h}{iq}")
            else:
                c.wait(c.pool, freed["bias", h, iq - 2])
            c.settle(c.pool)
            t = c.on_pool(c.pool.affine_select(buf, cb[:, h, 0:(iq + 1) * P], [[-1, (iq + 1) * P]], ALU.is_ge, masked,
                                               base=iq * P, channel_multiplier=1), label="biased")
            return buf, t
        c.wait(c.sp, *(c.now(e) for e in ("pe", "act", "dve", "pool", "misc")))
        self.attention(
            4, lambda i: q[:, ds(i, 1), :].rearrange("p a b -> p (a b)"),
            lambda i: k[:, ds(i, 1), :].rearrange("p a b -> p (a b)"),
            lambda i, j: v[:, j, ds(i * P, P)],
            lambda i, iq: mix[:, ds(i, 1), iq * P:(iq + 1) * P].rearrange("p a b -> p (a b)"),
            at, lambda iq: (iq + 1) * P, bias=bias, per_pair=rows_of_pair)

        for t0, gain in ((0, "g_attn_grp"), (4, "g_pool_grp")):
            tiles = [mix[:, t0 + j, :] for j in range(4)]
            r = sb.at(B, S)
            self.rstd(tiles, S, ATT_W, self.eps, r, B + S)
            self.scale_tiles(tiles, tiles, self.vec[gain], r)
        c.join()
        y = sb.at(B + 4096, KT, S)
        self.linear(A["w_out"].rearrange("l a b -> (l a) b"), KT, lambda i, j: (2 * i + j) * P, 4, mix,
                    self.to(lambda i, j: y[:, ds(2 * i + j, 1), :].rearrange("p a b -> p (a b)")))
        self.add_normed(y, self.vec["g_mix_post"], B)

    def feed_forward(self):
        c, sb, A = self.c, self.sb, self.A
        B = self.BIG
        g = sb.at(B, FT, S)
        self.norm_x(self.vec["g_ffn_pre"], B)
        w = [A[n].rearrange("l a b -> (l a) b") for n in ("w_ffn_gate", "w_ffn_up")]

        def evac(i, j, h, bank, t):
            d = g[:, ds(i, 1), h * HALF:(h + 1) * HALF].rearrange("p a b -> p (a b)")
            if j == 0:
                c.wait(c.act, t)
                self.silu[h] = c.on_act(c.act.activation(d, bank, ACT.Silu))
                return self.silu[h]
            c.wait(c.dve, t, self.silu[h])
            return c.on_dve(c.dve.tensor_tensor(d, d, bank, ALU.mult))
        self.silu = {}
        self.linear(w, KT, lambda i, j: i * P, FT, self.hn, evac)
        self.linear(A["w_ffn_down"].rearrange("l a b -> (l a) b"), FT, lambda i, j: (2 * i + j) * P, 4, g,
                    self.to(lambda i, j: self.hn[:, ds(2 * i + j, 1), :].rearrange("p a b -> p (a b)")))
        self.add_normed(self.hn, self.vec["g_ffn_post"], B)

    def embedding_gate(self):
        c, sb, A = self.c, self.sb, self.A
        B = self.BIG
        pT = sb.at(B, PLE // P, S)
        self.load_rows(A["p"].rearrange("l b s d -> (l b s) d"), S, PLE, pT, B + 2 * S)
        e = self.hn
        self.linear(A["w_ple_proj"].rearrange("l a b -> (l a) b"), PLE // P, lambda i, j: (2 * i + j) * P, 4, pT,
                    self.to(lambda i, j: e[:, ds(2 * i + j, 1), :].rearrange("p a b -> p (a b)")))
        r = sb.at(B, S)
        tiles = [e[:, j, :] for j in range(KT)]
        self.rstd(tiles, S, D, self.eps, r, B + S)
        self.scale_tiles(tiles, tiles, self.vec["g_ple"], r)
        c.join()
        s = sb.at(B, 4, HALF)
        y = sb.at(B + 4096, KT, S)

        def gate(i, j, h, bank, t):
            b = s[:, 2 * j + h, :]
            c.wait(c.act, t)
            c.wait_before(c.act, f"gated{j}{h}")
            t = free = c.on_act(c.act.activation(b, bank, ACT.Sigmoid))
            c.wait(c.dve, t)
            part = slice(h * HALF, (h + 1) * HALF)
            c.on_dve(c.dve.tensor_tensor(y[:, ds(2 * i + j, 1), part].rearrange("p a b -> p (a b)"), b,
                                         e[:, ds(2 * i + j, 1), part].rearrange("p a b -> p (a b)"), ALU.mult),
                     label=f"gated{j}{h}")
            return free
        self.linear(A["w_ple_gate"].rearrange("l a b -> (l a) b"), KT, lambda i, j: (2 * i + j) * P, 4, self.x, gate)
        for j in range(KT):
            c.on_dve(c.dve.tensor_tensor(self.x[:, j, :], self.x[:, j, :], y[:, j, :], ALU.add))
        c.join()

    def store(self):
        c, ps = self.c, self.ps
        o = self.out.rearrange("b s d -> (b s) d")
        st = self.sb.at(self.BIG, 2, KT, P)
        row = self.sb.at(self.BIG + 2 * D, 2, D)
        with c.fori(ST // 2) as i:
            for j in range(2):
                c.wait_before(c.pool, f"turned{j}")
                t = c.on_pool(c.pool.tensor_copy(st[:, j], self.x[:, :, ds(i * 2 * P + j * P, P)]))
                c.wait(c.pe, t)
                c.wait_before(c.pe, f"a{j}", f"b{j}")
                for f in range(KT):
                    t = c.pe.transpose(ps[:, 2 * j + f // 4, (f % 4) * P:(f % 4 + 1) * P], st[:, j, f, :], self.ident)
                t = c.on_pe(t, label=f"turned{j}")
                c.wait(c.act, t)
                c.wait(c.dve, t)
                c.wait_before(c.act, f"stored{j}")
                c.wait_before(c.dve, f"stored{j}")
                ta = c.on_act(c.act.copy(row[:, j, 0:HALF], ps[:, 2 * j, :]), label=f"a{j}")
                tb = c.on_dve(c.dve.tensor_copy(row[:, j, HALF:D], ps[:, 2 * j + 1, :]), label=f"b{j}")
                c.wait(c.sp, ta, tb)
                c.load(self.io[j], o[ds(i * 2 * P + j * P, P), :], row[:, j, :], label=f"stored{j}")
        c.wait(c.sp, c.now("io0"), c.now("io1"))


    def block_two(self):
        self.memory()
        self.layer_a()
        self.layer_b()

    def memory(self):
        c, sb = self.c, self.sb
        B = self.BIG
        self.mhat = sb.at(B + 25600, KT, MEM)
        self.load_rows(self.A["mem_2"].rearrange("b m d -> (b m) d"), MEM, D, self.mhat, B)
        r = sb.at(B, MEM)
        tiles = [self.mhat[:, j, :] for j in range(KT)]
        c.wait(c.dve, self.rstd(tiles, MEM, D, self.eps, r, B + MEM))
        for t in tiles:
            c.on_dve(c.dve.tensor_tensor(t, t, r, ALU.mult))
        c.join()

    def do(self, engine, deps, make):
        c = self.c
        c.wait(engine, *deps)
        return c.mark(c.names[id(engine)], make())

    def layer_a(self):
        c, sb, A, ps = self.c, self.sb, self.A, self.ps
        B = self.BIG
        w_in = A["a_w_in_2"].rearrange("l a b -> (l a) b")
        mix = sb.at(B, KT, S)
        rkv = sb.at(B, 3 * BT, S)
        lora = sb.at(B + 18432, S)
        rs12 = sb.at(B + 19456, S)
        w2, a2 = sb.at(B + 20480, BR), sb.at(B + 20480 + BR, BR)
        zt = [sb.at(B + 22016 + j * (S + 1), S + 1) for j in range(2)]
        dz = sb.at(B + 22016 + 2 * (S + 1), S)
        reset = sb.at(B + 22016, BT, CH)
        mu = self.vec["a_shift_mu_2"]
        self.norm_x(self.vec["pre_norm_2"][:, 0:KT], B)
        for j in range(2):
            c.on_dve(c.dve.memset(zt[j][:, 0:1], 0.0))
        c.on_dve(c.dve.memset(w2, 0.0))
        c.on_dve(c.dve.memset(a2, 0.0))
        c.wait(c.sp, c.now("dve"))
        tl = c.load(self.misc, w2[0:LORA, :], A["a_w2_2"].rearrange("l a b -> (l a) b"))
        tl = c.load(self.misc, a2[LORA:P, :], A["a_a2_2"].rearrange("l a b -> (l a) b"))
        c.join()

        def shifted(dst, j, col):
            t = self.do(c.dve, [self.copied[0], self.copied[1]],
                        lambda: c.dve.tensor_tensor(dz, zt[j][:, 0:S], zt[j][:, 1:S + 1], ALU.subtract))
            c.wait(c.dve, t)
            return c.dve.scalar_tensor_tensor(dst, dz, mu[:, col], zt[j][:, 1:S + 1], ALU.mult, ALU.add)

        self.copied = {}

        def evac(i, j, h, bank, t):
            e, on_e, cp = ((c.act, c.on_act, c.act.copy), (c.dve, c.on_dve, c.dve.tensor_copy))[h]
            c.wait(e, t)
            c.wait_before(e, f"shifted{j}")
            free = self.copied[h] = on_e(cp(zt[j][:, 1 + h * HALF:1 + (h + 1) * HALF], bank))
            if h == 1:
                if j == 1:
                    c.wait(c.dve, self.shift_done)
                else:
                    c.wait_before(c.dve, "shifted1")
                ins = shifted(rkv[:, ds(2 * i + j, 1), :].rearrange("p a b -> p (a b)"), j, ds(2 * i + j, 1))
                self.shift_done = c.on_dve(ins, label=f"shifted{j}")
            return free
        self.linear(w_in, KT, lambda i, j: (2 * i + j) * P, 9, self.hn, evac)

        def evac_lora(h, bank, t):
            self.copied[h] = self.do(c.act, [t], lambda: c.act.copy(zt[0][:, 1 + h * HALF:1 + (h + 1) * HALF], bank))
            if h == 1:
                t = c.on_dve(shifted(lora, 0, slice(18, 19)))
                self.do(c.act, [t], lambda: c.act.activation(lora[0:LORA, :], lora[0:LORA, :], ACT.Tanh))
        self.linear_once(w_in, KT, 3 * BR, P, self.hn, evac_lora)

        sq = [zt[0][:, 0:S], zt[1][:, 0:S]]
        read = [None, None]
        for p in range(BT):
            c.wait(c.act, read[p % 2])
            t = c.on_act(c.act.activation(sq[p % 2], rkv[:, BT + p, :], ACT.Square, scale=self.vec["a_k_k_2"][:, p:p + 1]))
            c.wait(c.pe, t)
            for h in range(2):
                t = c.pe.matmul(ps[0:12, h, :], self.sel[:, p, :], sq[p % 2][:, h * HALF:(h + 1) * HALF],
                                start=(p == 0), stop=(p == BT - 1))
            read[p % 2] = c.on_pe(t)
        n2 = rs12[0:12, :]
        t = self.do(c.dve, [read[1]], lambda: c.dve.tensor_scalar(
            n2, ps[0:12, 0:2, :].rearrange("p a b -> p (a b)"), 1e-12, None, ALU.max))
        t = self.do(c.act, [t], lambda: c.act.activation(n2, n2, ACT.Ln))
        self.do(c.act, [t], lambda: c.act.activation(n2, n2, ACT.Exp, scale=-0.5))
        c.join()
        c.on_dve(c.dve.memset(reset, 1.0))
        c.wait(c.dve, c.now("dve"))
        c.on_dve(c.dve.memset(reset[:, :, 0:1], 0.0))
        c.wait(c.dve, tl)
        c.join()
        self.rwkv(rkv, lora, rs12, w2, a2, reset)
        self.rwkv_norm(mix, rkv)

        self.norm_x(self.vec["pre_norm_2"][:, 0:KT], B + 12288)
        gate0 = 3 * BR + 2 * LORA
        self.finish_layer(0, w_in, gate0, gate0 + BR, mix, sb.at(B + 8192, 4, S), B + 12288)

    def rwkv(self, rkv, lora, rs12, w2, a2, reset):
        c, sb, ps = self.c, self.sb, self.ps
        pe, act, dve, pool, do = c.pe, c.act, c.dve, c.pool, self.do
        at = [self.HN]

        def buf(*shape):
            shape = shape or (BT, CH)
            n = math.prod(shape)
            if at[0] < self.W <= at[0] + n - 1:
                pass
            ap = sb.at(at[0], *shape)
            at[0] += n
            return ap
        tw, ta, ld, run, pinv = buf(), buf(), buf(), buf(), buf()
        pc = buf(BT, CH + 1)
        kk, kp, u1, nb, bbar, kbar, rk, vc = (buf() for _ in range(8))
        ar, lr, ak = buf(BT, 2, CH), buf(BT, 2 * CH), buf(BT, 2 * CH)
        x_, xt, w_ = buf(), buf(), buf()
        vt, kt, bt = buf(), buf(), buf()
        rhs, g, st = buf(), buf(), buf()
        assert at[0] <= self.CONST, at[0] - self.CONST
        V = self.vec
        w0, a0, k_k, k_a, r_k = (over_tokens(V[n], CH) for n in ("a_w0_2", "a_a0_2", "a_k_k_2", "a_k_a_2", "a_r_k_2"))
        mask2 = sb.at(self.up_col, 2 * CH)

        def bank(b, n=BT, w=CH):
            return ps[:, b, 0:n * w].rearrange("p (a b) -> p a b", a=n)

        def heads(out, pairs):
            c.settle(pe)
            for p in range(BT):
                for n, (lhsT, rhs_) in enumerate(pairs):
                    for h in range(2):
                        o = slice(64 * h, 64 * h + 64)
                        t = pe.matmul(out(p)[o], lhsT(p)[o], rhs_(p)[o], start=(n == 0), stop=(n == len(pairs) - 1),
                                      skip_group_check=True)
            return c.on_pe(t)

        def of(a):
            return lambda p: a[:, p, :]

        c.on_dve(dve.memset(pc, 1.0))
        c.on_dve(dve.memset(st, 0.0))
        c.join()
        with c.fori(NCH) as i:
            tok = ds(i * CH, CH)
            rC, kC, vC = (rkv[:, n * BT:(n + 1) * BT, tok] for n in range(3))
            for e in (pe, act, dve, pool):
                c.wait_before(e, "end_pe", "end_act", "end_dve", "end_pool")
            for p in range(BT):
                pe.matmul(bank(0)[:, p, :], w2[:, p * P:(p + 1) * P], lora[:, tok], start=True, stop=True)
            t_w = c.on_pe(pe.matmul(bank(1)[:, 0, :], a2[:, 0:P], lora[:, tok], start=True, stop=True))
            for p in range(1, BT):
                t = pe.matmul(bank(1)[:, p, :], a2[:, p * P:(p + 1) * P], lora[:, tok], start=True, stop=True)
            t_a = c.on_pe(t)
            for p in range(BT):
                t = pe.matmul(bank(2)[:, p, :], self.selt[0:12, p * P:(p + 1) * P], rs12[0:12, tok], start=True, stop=True)
            t_n = c.on_pe(t)
            t = do(dve, [t_w], lambda: dve.tensor_tensor(tw, bank(0), w0, ALU.add))
            t_tw = do(act, [t], lambda: act.activation(tw, tw, ACT.Tanh, scale=0.5))
            t = do(dve, [t_a], lambda: dve.tensor_tensor(ta, bank(1), a0, ALU.add))
            t_ta = do(act, [t], lambda: act.activation(ta, ta, ACT.Tanh, scale=0.5))
            t_vc = do(pool, [], lambda: pool.tensor_copy(vc, vC))
            t = do(dve, [t_tw], lambda: dve.tensor_scalar(ld, tw, -0.5 * DECAY_C, -0.5 * DECAY_C, ALU.mult, ALU.add))
            flat = lambda a: a.rearrange("p a b -> p (a b)")
            t_run = do(dve, [t], lambda: dve.tensor_tensor_scan(flat(run), flat(reset), flat(ld), 0.0, ALU.mult, ALU.add))
            t_pc = do(act, [t_run], lambda: act.activation(pc[:, :, 1:CH + 1], run, ACT.Exp))
            t_pi = do(act, [], lambda: act.activation(pinv, run, ACT.Exp, scale=-1.0))
            t = do(dve, [t_n], lambda: dve.tensor_tensor(kk, kC, k_k, ALU.mult))
            t_kk = do(dve, [t], lambda: dve.tensor_tensor(kk, kk, bank(2), ALU.mult))
            t_ra = do(dve, [t_ta], lambda: dve.tensor_scalar(ta, ta, 0.5, 0.5, ALU.mult, ALU.add))
            t = do(dve, [t_ra], lambda: dve.scalar_tensor_tensor(u1, ta, -1.0, k_a, ALU.add, ALU.mult))
            t_kp = do(dve, [t], lambda: dve.scalar_tensor_tensor(kp, u1, 1.0, kC, ALU.add, ALU.mult))
            t = do(pool, [t_kp], lambda: pool.tensor_tensor(rk, rC, kp, ALU.mult))
            t_rk = do(pool, [t], lambda: pool.tensor_tensor(rk, rk, r_k, ALU.mult))
            t_nb = do(dve, [t_kk], lambda: dve.scalar_tensor_tensor(nb, kk, -1.0, ta, ALU.mult, ALU.mult))
            do(dve, [t_pc], lambda: dve.tensor_tensor(ar[:, :, 0, :], kk, pc[:, :, 0:CH], ALU.mult))
            t_ar = do(dve, [], lambda: dve.tensor_tensor(ar[:, :, 1, :], rC, pc[:, :, 1:CH + 1], ALU.mult))
            t_b = do(dve, [t_pi, t_nb], lambda: dve.tensor_tensor(bbar, nb, pinv, ALU.mult))
            t_k = do(pool, [t_pi], lambda: pool.tensor_tensor(kbar, kp, pinv, ALU.mult))
            c.wait(pe, t_ar, t_b)
            arf = ar.rearrange("p a b c -> p a (b c)")
            three = lambda b: (lambda p: bank(b + p // 3, 3, 2 * CH)[:, p % 3, :])
            t_lr = heads(three(0), [(of(bbar), of(arf))])
            c.wait(pe, t_kk)
            c.wait(pe, t_k)
            t_ak = heads(three(2), [(of(kbar), of(arf))])
            t_x = heads(of(bank(4)), [(lambda p: ar[:, p, 0, :], of(bbar))])
            c.wait(pe, t_vc)
            t_vt = heads(of(bank(5)), [(of(vc), lambda p: self.eye)])
            t_kt = heads(of(bank(6)), [(of(kbar), lambda p: self.eye)])
            t_bt = heads(of(bank(7)), [(of(bbar), lambda p: self.eye)])
            m3 = over_pairs(mask2, 3)
            do(dve, [t_lr], lambda: dve.tensor_tensor(lr[:, 0:3, :], bank(0, 3, 2 * CH), m3, ALU.mult))
            t_lrs = do(dve, [], lambda: dve.tensor_tensor(lr[:, 3:6, :], bank(1, 3, 2 * CH), m3, ALU.mult))
            t = do(dve, [t_x], lambda: dve.tensor_tensor(x_, bank(4), over_pairs(self.level[0]), ALU.mult))
            t_xs = do(dve, [t], lambda: dve.tensor_tensor(x_, x_, over_pairs(self.eye), ALU.add))
            t = do(pool, [t_lrs], lambda: pool.tensor_tensor(xt, lr[:, :, 0:CH], over_pairs(self.level0t), ALU.mult))
            t_xts = do(pool, [t], lambda: pool.tensor_tensor(xt, xt, over_pairs(self.eye), ALU.add))
            do(dve, [t_ak], lambda: dve.tensor_tensor(ak[:, 0:3, :], bank(2, 3, 2 * CH), m3, ALU.mult))
            t_aks = do(dve, [], lambda: dve.tensor_tensor(ak[:, 3:6, :], bank(3, 3, 2 * CH), m3, ALU.mult))
            t_vts = do(act, [t_vt], lambda: act.copy(vt, bank(5)))
            do(act, [t_kt], lambda: act.copy(kt, bank(6)))
            t_kbs = do(act, [t_bt], lambda: act.copy(bt, bank(7)))
            c.wait(pe, t_rk, t_kbs)
            t = c.on_pe(pe.matmul(bank(7), self.block64, flat(rk), start=True, stop=True))
            t_bonus = do(dve, [t, t_vc], lambda: dve.scalar_tensor_tensor(vC, bank(7), 64.0, vc, ALU.mult, ALU.mult))
            for lev in range(1, 6):
                c.wait(pe, t_lrs, t_xs, t_xts)
                t = heads(of(bank(0)), [(lambda p: lr[:, p, 0:CH], of(x_))])
                t_ws = do(dve, [t], lambda: dve.tensor_tensor(w_, bank(0), over_pairs(self.level[lev]), ALU.mult))
                c.wait(pe, t_ws)
                t2 = heads(of(bank(5)), [(of(w_), of(xt))])
                if lev < 5:
                    t1 = heads(of(bank(4)), [(of(xt), of(w_))])
                    t_xs = do(dve, [t1], lambda: dve.tensor_tensor(x_, x_, bank(4), ALU.add))
                t_xts = do(dve, [t2, t1], lambda: dve.tensor_tensor(xt, xt, bank(5), ALU.add))
            c.wait(pe, t_aks, t_vts, t_kbs)
            t = heads(of(bank(1)), [(lambda p: ar[:, p, 0, :], of(st)), (lambda p: ak[:, p, 0:CH], of(vt))])
            t = do(act, [t], lambda: act.copy(rhs, bank(1)))
            c.wait(pe, t, t_xts)
            t = heads(of(bank(2)), [(of(xt), of(rhs))])
            t = do(act, [t], lambda: act.copy(g, bank(2)))
            c.wait(pe, t)
            t_s = heads(of(bank(4)), [(of(kt), of(vt)), (of(bt), of(g))])
            t_y = heads(of(bank(3)), [(of(st), lambda p: ar[:, p, 1, :]), (of(vt), lambda p: ak[:, p, CH:2 * CH]),
                                      (of(g), lambda p: lr[:, p, CH:2 * CH])])
            c.known["label", c.loop["id"], "end_pe"] = (t_y.sem, t_y.k)
            c.wait(act, t_y, t_ar, t_rk)
            c.settle(act)
            t = c.on_act(act.copy(rC, bank(3)))
            c.known["label", c.loop["id"], "end_act"] = (t.sem, t.k)
            t = do(dve, [t_s, t_y], lambda: dve.tensor_tensor(st, st, bank(4), ALU.add))
            t = do(dve, [t], lambda: dve.tensor_tensor(st, st, pc[:, :, CH:CH + 1].broadcast_to((P, BT, CH)), ALU.mult))
            c.known["label", c.loop["id"], "end_dve"] = (t.sem, t.k)
            t = c.now_in("pool")
            c.known["label", c.loop["id"], "end_pool"] = (t.sem, t.k)
        c.join()

    def rwkv_norm(self, y, rkv):
        c, sb, ps, do = self.c, self.sb, self.ps, self.do
        yc, sq, rs = (sb.at(self.HN + j * S, S) for j in range(3))
        both = ps[:, 0:2, :].rearrange("p a b -> p (a b)")
        var = ps[:, 2:4, :].rearrange("p a b -> p (a b)")
        one = lambda a, i: a[:, ds(i, 1), :].rearrange("p a b -> p (a b)")
        with c.fori(BT) as i:
            for e in (c.pe, c.act, c.dve):
                c.wait_before(e, "end")
            for h in range(2):
                t = c.pe.matmul(ps[:, h, :], self.block64, one(y, i)[:, h * HALF:(h + 1) * HALF], start=True, stop=True)
            t = c.on_pe(t)
            t = do(c.dve, [t], lambda: c.dve.tensor_tensor(yc, one(y, i), both, ALU.subtract))
            t = do(c.act, [t], lambda: c.act.activation(sq, yc, ACT.Square))
            c.wait(c.pe, t)
            for h in range(2):
                t = c.pe.matmul(ps[:, 2 + h, :], self.block64, sq[:, h * HALF:(h + 1) * HALF], start=True, stop=True)
            t = c.on_pe(t)
            t = do(c.act, [t], lambda: c.act.activation(rs, var, ACT.Ln, bias=self.lnx_eps))
            t = do(c.act, [t], lambda: c.act.activation(rs, rs, ACT.Exp, scale=-0.5))
            w = self.vec["a_lnx_w_2"][:, ds(i, 1)]
            b = self.vec["a_lnx_b_2"][:, ds(i, 1)]
            t = do(c.dve, [t], lambda: c.dve.scalar_tensor_tensor(yc, yc, w, rs, ALU.mult, ALU.mult))
            c.wait(c.dve, t)
            c.on_dve(c.dve.scalar_tensor_tensor(one(y, i), yc, b, rkv[:, ds(i + 2 * BT, 1), :].rearrange("p a b -> p (a b)"),
                                                ALU.add, ALU.add), label="end")
        c.join()

    def finish_layer(self, l, w_in, gate_col, mem_col, mix, qg, tmp):
        c, sb, A, do = self.c, self.sb, self.A, self.do
        s = sb.at(tmp, 4, HALF)

        def silu_into(i, j, h, bank, t):
            b = s[:, 2 * j + h, :]
            c.wait(c.act, t)
            c.wait_before(c.act, f"gated{j}{h}")
            free = c.on_act(c.act.activation(b, bank, ACT.Silu))
            c.wait(c.dve, free)
            d = mix[:, ds(2 * i + j, 1), h * HALF:(h + 1) * HALF].rearrange("p a b -> p (a b)")
            c.on_dve(c.dve.tensor_tensor(d, d, b, ALU.mult), label=f"gated{j}{h}")
            return free
        self.linear(w_in, KT, lambda i, j: (2 * i + j) * P + gate_col, 3, self.hn, silu_into)
        self.linear(w_in, KT, lambda i, j: (2 * i + j) * P + mem_col, 1, self.hn,
                    self.to(lambda i, j: qg[:, j, :]))
        self.linear(w_in, KT, lambda i, j: (2 * i + j) * P + mem_col + MEM_W, 1, self.hn,
                    lambda i, j, h, bank, t: do(c.act, [t], lambda: c.act.activation(
                        qg[:, 2 + j, h * HALF:(h + 1) * HALF], bank, ACT.Silu)))
        mn = sb.at(tmp, KT, MEM)
        km, vm = sb.at(tmp + 2048, 2, MEM), sb.at(tmp + 2560, 2, MEM_W)
        for j in range(KT):
            c.on_dve(c.dve.tensor_scalar(mn[:, j, :], self.mhat[:, j, :],
                                         self.vec["mem_norm_2"][:, l * KT + j:l * KT + j + 1], None, ALU.mult))
        c.join()
        w_kv = A["w_mem_kv_2"][l]
        self.linear(w_kv, KT, lambda i, j: (2 * i + j) * P, 1, mn, self.to(lambda i, j: km[:, j, :]), n_cols=MEM)
        self.linear_tokens(w_kv, MEM_W, MEM_W, 1, mn, vm, rows=MEM)
        one = lambda a, i: a[:, ds(i, 1), :].rearrange("p a b -> p (a b)")
        self.attention(2, lambda i: one(qg, i), lambda i: one(km, i), lambda i, j: vm[:, j, ds(i * P, P)],
                       lambda i, iq: mix[:, ds(i + 6, 1), iq * P:(iq + 1) * P].rearrange("p a b -> p (a b)"),
                       self.HN, lambda iq: MEM)
        for j in range(2):
            c.on_dve(c.dve.tensor_tensor(mix[:, 6 + j, :], mix[:, 6 + j, :], qg[:, 2 + j, :], ALU.mult))
        c.join()
        self.linear(A["w_out_2"][l], KT, lambda i, j: (2 * i + j) * P, 4, mix,
                    self.to(lambda i, j: self.hn[:, ds(2 * i + j, 1), :].rearrange("p a b -> p (a b)")))
        self.add_normed(self.hn, self.vec["post_norm_2"][:, l * KT:(l + 1) * KT], tmp)

    def layer_b(self):
        c, sb, A, ps, do = self.c, self.sb, self.A, self.ps, self.do
        B = self.BIG
        w_in = A["b_w_in_2"].rearrange("l a b -> (l a) b")
        mix = sb.at(B, KT, S)
        k = sb.at(B + 8192, BT, S)
        v = sb.at(B + 14336, ST, BR)
        dist, strip = sb.at(B + 20480, S), sb.at(B + 21504, S)
        one = lambda a, i: a[:, ds(i, 1), :].rearrange("p a b -> p (a b)")
        self.norm_x(self.vec["pre_norm_2"][:, KT:2 * KT], B + 8192)
        self.linear(w_in, KT, lambda i, j: (2 * i + j) * P, 3, self.hn, self.to(lambda i, j: one(mix, 2 * i + j)))
        self.norm_x(self.vec["kv_norm_2"], B + 8192)
        self.linear(A["w_kv_2"], KT, lambda i, j: (2 * i + j) * P, 3, self.hn, self.to(lambda i, j: one(k, 2 * i + j)))
        self.linear_tokens(A["w_kv_2"], BR, BR // 2, 2, self.hn, v)

        lam = [sb.at(B + 22528 + 64 * j, HD) for j in range(4)]
        e = [sb.at(B + 22528 + 256 + j, 1) for j in range(3)]
        for a, n in zip(lam, ("q1", "k1", "q2", "k2")):
            t = c.load(self.misc, a, A[f"b_lam_{n}_2"].rearrange("l a -> (l a)").partition_broadcast(P))
        for j in range(2):
            t2 = do(c.dve, [t], lambda: c.dve.tensor_tensor(lam[2 * j], lam[2 * j], lam[2 * j + 1], ALU.mult))
            t2 = do(c.dve, [t2], lambda: c.dve.tensor_reduce(e[j], lam[2 * j], AX.X, ALU.add))
            t2 = do(c.act, [t2], lambda: c.act.activation(e[j], e[j], ACT.Exp))
        t = do(c.dve, [t2], lambda: c.dve.tensor_tensor(e[2], e[1], e[0], ALU.subtract))
        do(c.dve, [t], lambda: c.dve.tensor_scalar(self.neglam, e[2], -LAM_INIT, None, ALU.add))
        t = do(c.pool, [c.now("dve")], lambda: c.pool.iota(dist, [[-1, S]], base=S - P, channel_multiplier=1,
                                                          allow_small_or_imprecise_dtypes=True))
        t = do(c.act, [t], lambda: c.act.activation(dist, dist, ACT.Abs))
        t = do(c.dve, [t], lambda: c.dve.tensor_scalar(dist, dist, -1.0, None, ALU.mult))
        do(c.dve, [t], lambda: c.dve.memset(dist[0:64, S - 64:S], NEG * 100))
        c.join()

        def strip_of(i):
            c.wait_before(c.dve, "bias10", "bias11")
            self.t_strip = c.on_dve(c.dve.tensor_scalar(strip, dist, self.slopes[:, ds(i, 1)], None, ALU.mult))

        self.attention(BT, lambda i: one(mix, i), lambda i: one(k, i), lambda i, j: v[:, j, ds(i * P, P)],
                       lambda i, iq: mix[:, ds(i, 1), iq * P:(iq + 1) * P].rearrange("p a b -> p (a b)"),
                       self.HN, lambda iq: (iq + 1) * P,
                       bias=lambda h, iq, freed: (strip[:, S - (iq + 1) * P:S], self.t_strip),
                       per_pair=strip_of, diff=True)

        sub = e[0]
        c.on_dve(c.dve.tensor_scalar(sub, self.vec["b_subln_2"], 1.0 - LAM_INIT, None, ALU.mult))
        sq, rs = sb.at(self.HN, S), sb.at(self.HN + S, S)
        both = ps[:, 0:2, :].rearrange("p a b -> p (a b)")
        c.join()
        with c.fori(BT) as i:
            for eng in (c.pe, c.act, c.dve):
                c.wait_before(eng, "end")
            t = do(c.act, [], lambda: c.act.activation(sq, one(mix, i), ACT.Square))
            c.wait(c.pe, t)
            for h in range(2):
                t = c.pe.matmul(ps[:, h, :], self.ones, sq[:, h * HALF:(h + 1) * HALF], start=True, stop=True)
            t = c.on_pe(t)
            t = do(c.act, [t], lambda: c.act.activation(rs, both, ACT.Ln, bias=self.eps, scale=1.0 / P))
            t = do(c.act, [t], lambda: c.act.activation(rs, rs, ACT.Exp, scale=-0.5))
            c.wait(c.dve, t)
            c.on_dve(c.dve.scalar_tensor_tensor(one(mix, i), one(mix, i), sub, rs, ALU.mult, ALU.mult), label="end")
        c.join()
        self.norm_x(self.vec["pre_norm_2"][:, KT:2 * KT], B + 14336)
        self.finish_layer(1, w_in, BR, 2 * BR, mix, sb.at(B + 8192, 4, S), B + 14336)


_INS = [
    "x", "p", "g_mix_pre", "w_in", "b_forget", "g_attn_grp", "g_pool_grp", "w_pool", "pool_scale", "w_out",
    "g_mix_post", "g_ffn_pre", "w_ffn_gate", "w_ffn_up", "w_ffn_down", "g_ffn_post", "w_ple_proj", "g_ple",
    "w_ple_gate", "mem_2", "pre_norm_2", "post_norm_2", "w_out_2", "mem_norm_2", "w_mem_kv_2", "a_w_in_2",
    "a_shift_mu_2", "a_w0_2", "a_w2_2", "a_a0_2", "a_a2_2", "a_k_k_2", "a_k_a_2", "a_r_k_2", "a_lnx_w_2",
    "a_lnx_b_2", "kv_norm_2", "w_kv_2", "b_w_in_2", "b_lam_q1_2", "b_lam_k1_2", "b_lam_q2_2", "b_lam_k2_2",
    "b_subln_2",
]


def kernel(**inputs):
    import numpy as _np
    import concourse.bacc as _bacc
    from concourse import mybir as _mybir
    from concourse.bass_utils import run_bass_kernel_spmd as _run

    arrays = {f"in_{n}": _np.ascontiguousarray(inputs[n]) for n in _INS}
    known = {}
    for _ in range(2):
        nc = _bacc.Bacc("TRN2", target_bir_lowering=False, num_devices=1)
        A = {n: nc.dram_tensor(f"in_{n}", arrays[f"in_{n}"].shape, _mybir.dt.float32, kind="ExternalInput").ap()
             for n in _INS}
        out = nc.dram_tensor("out", (1, S, D), _mybir.dt.float32, kind="ExternalOutput").ap()
        build(nc, A, out, known)
    r = _run(nc, [arrays], core_ids=[0])
    return r.results[0]["out"]
```

```python
import math
from contextlib import ExitStack, contextmanager

import numpy as np
import concourse.bass as bass
import concourse.mybir as mybir

F32 = mybir.dt.float32
F32R = mybir.dt.float32r
ALU = mybir.AluOpType
ACT = mybir.ActivationFunctionType
AX = mybir.AxisListType
ds = bass.ds

P = 128
D = 1024
S = 1024
KT = D // P
ST = S // P
HALF = 512
EPS = 1e-6
NEG = -1.0e30

HD = 64
ATT_H = 8
ATT_W = ATT_H * HD
POOL_G = 4
FF = 2816
FT = FF // P
PLE = 256
MEM = 256
MEM_W = 256
BR = 768
BT = BR // P
LORA = 64
LNX_EPS = 64e-5
CH = 64
NCH = S // CH
LAM_INIT = 0.8 - 0.6 * math.exp(-0.3)
DECAY_C = math.exp(-0.5)


class Tick:

    def __init__(self, sem, loop, base, k):
        self.sem, self.loop, self.base, self.k = sem, loop, base, k


class Chip:

    def __init__(self, nc, ctx, known):
        self.nc, self.ctx, self.known = nc, ctx, known
        self.pe, self.act, self.dve, self.pool, self.sp = nc.tensor, nc.scalar, nc.vector, nc.gpsimd, nc.sync
        self.engines = {"pe": self.pe, "act": self.act, "dve": self.dve, "pool": self.pool}
        self.names = {id(e): n for n, e in (*self.engines.items(), ("sp", self.sp))}
        self.sems, self.count, self.seen = {}, {}, {}
        self.loop, self.n_loops = None, 0
        self.events = {}
        self.fresh = {}
        self.idle = ctx.enter_context(nc.semaphore("s_idle"))
        for n, e in self.engines.items():
            self.new_sem(n, e)

    def new_sem(self, name, engine=None):
        self.sems[name] = self.ctx.enter_context(self.nc.semaphore("s_" + name))
        start = max([v for k, v in self.known.items() if k[0] == "per" and k[2] == name], default=0)
        self.count[name] = start
        if start:
            engine = engine or self.sp
            engine.sem_inc(self.sems[name], start)
            engine.wait_ge(self.sems[name], start)
        return name

    def mark(self, name, instruction, by=1, label=None):
        instruction.then_inc(self.sems[name], by)
        self.count[name] += by
        if not self.loop:
            return Tick(name, None, self.count[name], 0)
        base = self.loop["base"].get(name, 0)
        if label:
            self.known["label", self.loop["id"], label] = (name, self.count[name] - base)
        return Tick(name, self.loop, base, self.count[name] - base)

    def on_pe(self, ins, label=None):
        return self.mark("pe", ins, label=label)

    def on_act(self, ins, label=None):
        return self.mark("act", ins, label=label)

    def on_dve(self, ins, label=None):
        return self.mark("dve", ins, label=label)

    def on_pool(self, ins, label=None):
        return self.mark("pool", ins, label=label)

    def load(self, sem, out, in_, label=None):
        self.settle(self.sp)
        return self.mark(sem, self.sp.dma_start(out, in_), 16, label)

    def wait(self, engine, *ticks):
        for t in ticks:
            if t is None:
                continue
            e = self.names[id(engine)]
            if t.loop is not None and t.loop is self.loop:
                self._wait_in_loop(engine, t.sem, t.k, t.base)
                continue
            value = t.base if t.loop is None else t.base + t.loop["per"][t.sem] * (t.loop["n"] - 1) + t.k
            if self.seen.get((e, t.sem, None), 0) < value:
                self.seen[e, t.sem, None] = value
                engine.wait_ge(self.sems[t.sem], value)

    def wait_before(self, engine, *labels):
        for label in labels:
            sem, k = self.known.get(("label", self.loop["id"], label), ("pe", 0))
            per = self.known.get(("per", self.loop["id"], sem), 4096)
            self._wait_in_loop(engine, sem, k - per, self.loop["base"].get(sem, 0))

    def _wait_in_loop(self, engine, sem, k, base):
        per = self.known.get(("per", self.loop["id"], sem), 4096)
        key = (self.names[id(engine)], sem, self.loop["id"])
        if self.seen.get(key, -1 << 40) < k:
            self.seen[key] = k
            engine.wait_ge(self.sems[sem], self.loop["i"] * per + max(base + k, 0))
            self.fresh[self.names[id(engine)]] = True
            if engine is self.sp:
                self.settle(engine)

    def settle(self, engine):
        if self.loop and self.fresh.pop(self.names[id(engine)], False):
            engine.sem_inc(self.idle, 1)

    @contextmanager
    def fori(self, n):
        assert self.loop is None
        self.n_loops += 1
        base = dict(self.count)
        with self.nc.Fori(0, n) as i:
            self.loop = dict(id=self.n_loops, i=i, base=base, n=n)
            yield i
        per = {s: self.count[s] - b for s, b in base.items()}
        for s, marks in per.items():
            self.known["per", self.n_loops, s] = marks
            self.count[s] = base[s] + n * marks
        self.loop["per"] = per
        for name, ticks in self.events.items():
            if any(t.loop is self.loop for t in ticks):
                self.known["event", self.n_loops, name] = [(t.sem, t.k) for t in ticks if t.loop is self.loop]
        self.loop = None

    def post(self, name, *ticks):
        self.events[name] = ticks

    def need(self, engine, *names):
        for name in names:
            ticks = self.events.get(name, ())
            self.wait(engine, *ticks)
            if self.loop and not any(t.loop is self.loop for t in ticks):
                for sem, k in self.known.get(("event", self.loop["id"], name), ()):
                    per = self.known.get(("per", self.loop["id"], sem), 4096)
                    self._wait_in_loop(engine, sem, k - per, self.loop["base"].get(sem, 0))

    def now_in(self, name):
        base = self.loop["base"].get(name, 0)
        return Tick(name, self.loop, base, self.count[name] - base)

    def now(self, name):
        assert self.loop is None
        return Tick(name, None, self.count[name], 0)

    def join(self, *engines):
        for e in engines or self.engines.values():
            self.wait(e, *(self.now(n) for n in self.engines))


class Rounded:

    def __init__(self, nc, base):
        self.nc, self.base, self.pieces = nc, base, {}

    def at(self, col, *shape):
        n = math.prod(shape)
        if (col, n) not in self.pieces:
            self.pieces[col, n] = self.nc.alloc_sbuf_tensor_at(f"r{col}_{n}", [P, n], F32R, offset=self.base + 4 * col)
        ap = self.pieces[col, n][:, :]
        return ap if len(shape) == 1 else ap.rearrange("p (a b) -> p a b", a=shape[0])


class Mem:

    def __init__(self, tile):
        self.tile = tile

    def at(self, col, *shape):
        n = math.prod(shape)
        ap = self.tile[:, col:col + n]
        if len(shape) == 1:
            return ap
        names = "abcd"[:len(shape)]
        sizes = {names[j]: shape[j] for j in range(1, len(shape))}
        return ap.rearrange(f"p ({' '.join(names)}) -> p {' '.join(names)}", **sizes)


def over_tokens(vec, n):
    return vec.unsqueeze(2).broadcast_to((P, vec.shape[1], n))


def over_pairs(mask, n=BT):
    return mask.unsqueeze(1).broadcast_to((mask.shape[0], n, mask.shape[1]))


VEC_ROWS = [
    ("g_mix_pre", 8), ("g_attn_grp", 4), ("g_pool_grp", 4), ("pool_scale", 4), ("g_mix_post", 8),
    ("g_ffn_pre", 8), ("g_ffn_post", 8), ("g_ple", 8), ("pre_norm_2", 16), ("post_norm_2", 16),
    ("mem_norm_2", 16), ("a_shift_mu_2", 19),
    ("a_w0_2", 6), ("a_a0_2", 6), ("a_k_k_2", 6), ("a_k_a_2", 6), ("a_r_k_2", 6),
    ("a_lnx_w_2", 6), ("a_lnx_b_2", 6), ("kv_norm_2", 8), ("b_subln_2", 1),
]


def build(nc, A, out, known, upto="all"):
    with ExitStack() as ctx:
        c = Chip(nc, ctx, known)
        k = Kernel(c, ctx, A, out)
        k.constants()
        k.load_x()
        if upto != "b2":
            k.block_one()
        if upto != "b1":
            k.block_two()
        k.store()


class Kernel:
    X = 0
    HN = 8192
    W = 16384
    WSLOT = FT * P // 2
    CONST = W + 4 * (FT * P // 2)
    BIG = CONST + 3328

    def __init__(self, c, ctx, A, out):
        self.c, self.A, self.out = c, A, out
        nc = c.nc
        cols = 53200
        base = (nc.sbuf_base + 63) // 64 * 64
        self.sb = Mem(nc.alloc_sbuf_tensor_at("sb", [P, cols], F32, offset=base))
        self.sr = Rounded(nc, base)
        self.ps = ctx.enter_context(nc.psum_tensor("ps", [P, 8, HALF], F32))
        self.x = self.sb.at(self.X, KT, S)
        self.hn = self.sb.at(self.HN, KT, S)
        self.wsem = [c.new_sem(f"w{j}") for j in range(4)]
        self.io = [c.new_sem("io0"), c.new_sem("io1")]
        self.misc, self.xio = c.new_sem("misc"), c.new_sem("xio")
        self.scratch_c = nc.dram_tensor("negc", [ATT_H, S], F32).ap()
        self.scratch_x = nc.dram_tensor("xs", [P, KT, S], F32).ap()
        self.x_kept = self.x_back = None
        col = self.CONST
        def const(*shape):
            nonlocal col
            ap = self.sb.at(col, *shape)
            col += math.prod(shape)
            return ap
        self.ident, self.ones, self.block64 = const(P), const(P), const(P)
        self.n_vec = sum(n for _, n in VEC_ROWS)
        self.vecs = const(self.n_vec)
        self.vec, at = {}, 0
        for name, n in VEC_ROWS:
            self.vec[name] = self.vecs[:, at:at + n]
            at += n
        self.eps, self.lnx_eps, self.stat = const(1), const(1), const(64)
        self.low = const(CH)
        self.up_col = col
        self.up, self.upi, self.eye = const(CH), const(CH), const(CH)
        self.level = [const(CH) for _ in range(6)]
        self.level0t = const(CH)
        self.slopes, self.neglam = const(BT), const(1)
        self.sel = const(BT, 12)
        self.selt = const(BR)
        assert col <= self.BIG, col - self.CONST


    def constants(self):
        c, sb, A = self.c, self.sb, self.A
        I32 = mybir.dt.int32

        def step(ins):
            c.wait(c.pool, c.on_pool(ins))
        pool, dve = c.pool, c.dve
        step(pool.memset(self.ident, 0.0))
        step(pool.memset(self.ones, 1.0))
        step(pool.memset(self.block64, 0.0))
        step(pool.memset(self.eps, EPS))
        step(pool.memset(self.lnx_eps, LNX_EPS))
        rows = sb.at(self.BIG, 2, P)
        step(pool.memset(rows, 0.0))
        step(pool.memset(self.sel, 0.0))
        step(pool.memset(self.selt, 0.0))
        for j in range(BT):
            slope = 2.0 ** (-2.0 * (j + 1)) if j < 4 else 2.0 ** (-1.0 - 2.0 * (j - 4))
            step(pool.memset(self.slopes[:, j:j + 1], slope))
        t = c.now("pool")
        c.wait(pool, t)
        for h in range(2):
            o = 64 * h
            step(pool.memset(self.block64[o:o + 64, o:o + 64], 1.0 / 64))
            for p in range(BT):
                step(pool.memset(self.sel[o:o + 64, p, 2 * p + h:2 * p + h + 1], 1.0))
        step(pool.affine_select(self.ident, self.ident, [[-1, P]], ALU.not_equal, 1.0, base=0,
                                     channel_multiplier=1))
        keep = sb.at(self.BIG + 512, BR)
        step(pool.memset(keep, 1.0))
        t = c.now("pool")
        c.wait(pool, t)
        step(pool.affine_select(keep[0:12], keep[0:12], [[1, BR]], ALU.is_ge, 0.0, base=0,
                                     channel_multiplier=-64))
        c.wait(pool, c.now("pool"))
        step(pool.affine_select(self.selt[0:12], keep[0:12], [[-1, BR]], ALU.is_ge, 0.0, base=63,
                                     channel_multiplier=64))
        ri, ci, xi = (sb.at(self.BIG + 2048 + CH * j, CH).bitcast(I32) for j in range(3))
        rf, cf = (sb.at(self.BIG + 2048 + CH * (3 + j), CH) for j in range(2))
        si = [sb.at(self.BIG + 2048 + CH * (5 + j), CH).bitcast(I32) for j in range(6)]
        sf = [sb.at(self.BIG + 2048 + CH * (11 + j), CH) for j in range(6)]
        for h in range(2):
            step(pool.iota(ri[64 * h:64 * h + 64], [[0, CH]], base=0, channel_multiplier=1))
        step(pool.iota(ci, [[1, CH]], base=0, channel_multiplier=0))
        c.wait(dve, c.now("pool"))
        c.on_dve(dve.tensor_copy(rf, ri))
        c.on_dve(dve.tensor_copy(cf, ci))
        c.on_dve(dve.tensor_tensor(xi, ri, ci, ALU.bitwise_xor))
        c.wait(dve, c.now("dve"))
        c.on_dve(dve.tensor_tensor(self.low, rf, cf, ALU.is_gt))
        c.on_dve(dve.tensor_tensor(self.up, cf, rf, ALU.is_gt))
        c.on_dve(dve.tensor_tensor(self.upi, cf, rf, ALU.is_ge))
        c.on_dve(dve.tensor_tensor(self.eye, cf, rf, ALU.is_equal))
        for j in range(6):
            c.on_dve(dve.tensor_scalar(si[j], xi, j, None, ALU.logical_shift_right))
        c.wait(dve, c.now("dve"))
        for j in range(6):
            c.on_dve(dve.tensor_copy(sf[j], si[j]))
        c.wait(dve, c.now("dve"))
        for j in range(6):
            c.on_dve(dve.scalar_tensor_tensor(self.level[j], sf[j], 1.0, self.low, ALU.is_equal, ALU.mult))
        c.on_dve(dve.scalar_tensor_tensor(self.level0t, sf[0], 1.0, self.up, ALU.is_equal, ALU.mult))
        c.wait(c.sp, c.now("pool"))
        at = 0
        for name, n in VEC_ROWS:
            v = A[name]
            flat = v if len(v.shape) == 1 else v.rearrange("a b -> (a b)") if len(v.shape) == 2 else v.rearrange("a b d -> (a b d)")
            v = flat.rearrange("(r p) -> r p", p=P)
            done = 0
            while done < n:
                m = min(n - done, P - at % P)
                t = c.load(self.misc, rows[at % P:at % P + m, at // P, :], v[done:done + m, :])
                at, done = at + m, done + m
        c.wait(c.pe, t, c.now("pool"))
        c.on_pe(c.pe.transpose(self.ps[:, 0, 0:P], rows[:, 0, :], self.ident))
        c.on_pe(c.pe.transpose(self.ps[:, 0, P:2 * P], rows[:, 1, :], self.ident))
        c.wait(dve, c.now("pe"))
        c.on_dve(dve.tensor_copy(self.vecs, self.ps[:, 0, 0:self.n_vec]))
        c.join()


    def load_rows(self, src, n_rows, n_cols, dst, at):
        c, kt = self.c, n_cols // P
        stage = [self.sb.at(at + j * n_cols, n_cols) for j in range(2)]
        c.wait(c.sp, *(c.now(n) for n in c.engines))
        with c.fori(n_rows // (2 * P)) as i:
            for j in range(2):
                c.wait_before(c.sp, f"turned{j}")
                t = c.load(self.io[j], stage[j], src[ds(i * 2 * P + j * P, P), :])
                c.wait(c.pe, t)
                c.wait_before(c.pe, *(f"copied{j}{b}" for b in range((kt + 3) // 4)))
                for f in range(kt):
                    t = c.pe.transpose(self.ps[:, 2 * j + f // 4, (f % 4) * P:(f % 4 + 1) * P],
                                       stage[j][:, f * P:(f + 1) * P], self.ident)
                t = c.on_pe(t, label=f"turned{j}")
                for b in range((kt + 3) // 4):
                    n = min(4, kt - 4 * b)
                    to = dst[:, 4 * b:4 * b + n, ds(i * 2 * P + j * P, P)]
                    fr = self.ps[:, 2 * j + b, 0:n * P].rearrange("p (a b) -> p a b", a=n)
                    if b == 0:
                        c.wait(c.dve, t)
                        c.on_dve(c.dve.tensor_copy(to, fr), label=f"copied{j}0")
                    else:
                        c.wait(c.act, t)
                        c.on_act(c.act.copy(to, fr), label=f"copied{j}1")
        c.join()

    def load_x(self):
        self.load_rows(self.A["x"].rearrange("b s d -> (b s) d"), S, D, self.x, self.BIG)


    def rstd(self, tiles, n, width, eps, out, tmp):
        c = self.c
        acc = self.sb.at(tmp, n)
        sq = [self.sb.at(tmp + n * (1 + j), n) for j in range(2)]
        c.wait(c.act, *(c.now(e) for e in c.engines))
        t = c.on_act(c.act.activation(acc, tiles[0], ACT.Square))
        added = [None, None]
        for j, tile in enumerate(tiles[1:]):
            c.wait(c.act, added[j % 2])
            s = c.on_act(c.act.activation(sq[j % 2], tile, ACT.Square))
            c.wait(c.dve, t, s)
            t = added[j % 2] = c.on_dve(c.dve.tensor_tensor(acc, acc, sq[j % 2], ALU.add))
        c.wait(c.pe, t, *(c.now(e) for e in c.engines))
        for h in range(0, n, HALF):
            m = min(HALF, n - h)
            t = c.on_pe(c.pe.matmul(self.ps[:, h // HALF, 0:m], self.ones, acc[:, h:h + m], start=True, stop=True))
        c.wait(c.act, t)
        src = self.ps[:, 0:(n + HALF - 1) // HALF, :].rearrange("p a b -> p (a b)")[:, 0:n]
        c.wait(c.act, c.on_act(c.act.activation(out, src, ACT.Ln, bias=eps, scale=1.0 / width)))
        return c.on_act(c.act.activation(out, out, ACT.Exp, scale=-0.5))

    def scale_tiles(self, dst, src, gain, rstd):
        c = self.c
        c.wait(c.dve, *(c.now(e) for e in c.engines))
        for j in range(len(src)):
            c.on_dve(c.dve.scalar_tensor_tensor(dst[j], src[j], gain[:, j:j + 1], rstd, ALU.mult, ALU.mult))

    def norm_x(self, gain, hi, tmp):
        c = self.c
        c.wait(c.act, self.x_back)
        c.wait(c.dve, self.x_back)
        r = self.sb.at(tmp, S)
        tiles = [self.x[:, j, :] for j in range(KT)]
        t = self.rstd(tiles, S, D, self.eps, r, tmp + S)
        c.wait(c.dve, *(c.now(e) for e in c.engines))
        c.wait(c.act, self.x_kept)
        scaled = [c.on_dve(c.dve.scalar_tensor_tensor(self.hn[:, j, :], tiles[j], gain[:, j:j + 1], r, ALU.mult, ALU.mult))
                  for j in range(KT)]
        return self.split(self.HN, hi, self.HN, KT, S, scaled)

    def split(self, src, hi, lo, nk, n, ticks=None):
        c = self.c
        xs = self.sb.at(src, nk, n)
        rh, rl = ([self.sr.at(at + j * n, n) for j in range(nk)] for at in (hi, lo))
        if not ticks:
            c.join()
        for j in range(nk):
            if ticks:
                c.wait(c.act, ticks[j])
            t = c.on_act(c.act.copy(rh[j], xs[:, j, :]))
            e, on_e = (c.pool, c.on_pool) if j % 4 == 1 else (c.dve, c.on_dve)
            c.wait(e, t)
            on_e(e.tensor_tensor(rl[j], xs[:, j, :], rh[j].bitcast(F32), ALU.subtract))
        c.join()
        return rh, rl

    def keep_x(self):
        c = self.c
        c.wait(c.sp, *(c.now(e) for e in c.engines))
        self.x_kept = c.load(self.xio, self.scratch_x, self.x)

    def fetch_x(self):
        c = self.c
        c.wait(c.sp, self.x_kept, *(c.now(e) for e in c.engines))
        self.x_back = c.load(self.xio, self.x, self.scratch_x)

    def add_normed(self, y, gain, tmp):
        c = self.c
        r = self.sb.at(tmp, S)
        self.rstd([y[:, j, :] for j in range(KT)], S, D, self.eps, r, tmp + S)
        c.wait(c.dve, *(c.now(e) for e in c.engines))
        for j in range(KT):
            t = c.on_dve(c.dve.scalar_tensor_tensor(y[:, j, :], y[:, j, :], gain[:, j:j + 1], r, ALU.mult, ALU.mult))
            c.wait(c.pool, t)
            c.on_pool(c.pool.tensor_tensor(self.x[:, j, :], self.x[:, j, :], y[:, j, :], ALU.add))
        c.join()


    HI = FT * P // 2

    def fetch(self, w, nk, column, j, width=P):
        c = self.c
        at = self.W + 2 * j * self.HI
        raw, hi = self.sb.at(at, nk, P), self.sr.at(at + self.HI, nk, P).bitcast(F32)
        c.need(c.sp, f"wread{j}")
        if width < P:
            c.need(c.dve, f"wread{j}")
            c.wait(c.sp, c.on_dve(c.dve.memset(raw, 0.0)))
        t = c.load(self.wsem[j], raw[:, :, 0:width], w.rearrange("(k p) n -> p k n", p=P)[:, :, ds(column, width)])
        c.wait(c.act, t)
        th = c.on_act(c.act.copy(self.sr.at(at + self.HI, nk, P), raw))
        c.wait(c.dve, t, th)
        tl = c.on_dve(c.dve.tensor_tensor(self.sr.at(at, nk, P), raw, hi, ALU.subtract))
        c.post(f"wready{j}", th, tl)

    def product(self, bank, w, x, nk):
        for q in range(nk):
            (wh, wl), (xh, xl) = w(q), x(q)
            for n, (a, b) in enumerate(((wh, xh), (wh, xl), (wl, xh))):
                t = self.c.pe.matmul(bank, a, b, start=(q == 0 and n == 0), stop=(q == nk - 1 and n == 2))
        return t

    def weight_tile(self, nk, i, j, x, evac, n_cols=S, width=P, banks=0):
        c = self.c
        at = self.W + 2 * j * self.HI
        lo, hi = self.sr.at(at, nk, P), self.sr.at(at + self.HI, nk, P)
        halves = (n_cols + HALF - 1) // HALF
        c.need(c.pe, f"wready{j}")
        for h in range(halves):
            m = min(HALF, n_cols - h * HALF)
            part = slice(h * HALF, h * HALF + m)
            bank = self.ps[:, banks + 2 * j + h, 0:m]
            c.need(c.pe, f"lbank{j}{h}")
            t = self.product(bank, lambda q: (hi[:, q, :], lo[:, q, :]), lambda q: (x[0][q][:, part], x[1][q][:, part]), nk)
            t = c.on_pe(t)
            if h == halves - 1:
                c.post(f"wread{j}", t)
            c.post(f"lbank{j}{h}", evac(i, j, h, bank[0:width], t))

    def linear(self, w, nk, column, n, x, evac, n_cols=S):
        c = self.c
        c.wait(c.pe, *(c.now(e) for e in c.engines))
        self.fetch(w, nk, column(0, 0), 0)

        def pair(i, last):
            self.fetch(w, nk, column(i, 1), 1)
            self.weight_tile(nk, i, 0, x, evac, n_cols)
            if not last:
                self.fetch(w, nk, column(i + 1, 0), 0)
            self.weight_tile(nk, i, 1, x, evac, n_cols)
        if n > 1:
            with c.fori(n - 1) as i:
                pair(i, False)
        pair(n - 1, True)
        c.join()

    def linear_once(self, w, nk, col, width, x, evac, n_cols=S):
        self.c.wait(self.c.pe, *(self.c.now(e) for e in self.c.engines))
        self.fetch(w, nk, col, 0, width)
        self.weight_tile(nk, 0, 0, x, lambda i, j, h, bank, t: evac(h, bank, t), n_cols, width)
        self.c.join()

    def linear_tokens(self, w, col, blocks, x, dst, rows=S):
        c = self.c
        width = 2 * P
        raw = self.sb.at(self.W, KT, width)
        rl, rh = ([self.sr.at(at + j * 2 * width, 2, width) for j in range(KT // 2)] for at in (self.W, self.W + KT * width))
        wv = w.rearrange("(k p) n -> p k n", p=P)
        c.wait(c.pe, *(c.now(e) for e in c.engines))
        c.need(c.sp, "wread0", "wread1")
        with c.fori(blocks) as i:
            c.need(c.sp, "vread")
            t = c.load(self.wsem[0], raw, wv[:, :, ds(i * width + col, width)])
            c.wait(c.act, t)
            c.wait(c.dve, t)
            parts = []
            for q in range(KT // 2):
                two = raw[:, 2 * q:2 * q + 2, :]
                t = c.on_act(c.act.copy(rh[q], two))
                c.wait(c.dve, t)
                parts.append(c.on_dve(c.dve.tensor_tensor(rl[q], two, rh[q].bitcast(F32), ALU.subtract)))
            for s in range(rows // P):
                bank = self.ps[:, s % 8, 0:width]
                c.need(c.pe, f"vbank{s}")
                for q in range(KT):
                    c.wait(c.pe, parts[q // 2])
                    for n, (a, b) in enumerate(((0, rh), (0, rl), (1, rh))):
                        t = c.pe.matmul(bank, x[a][q][:, s * P:(s + 1) * P], b[q // 2][:, q % 2, :],
                                        start=(q == 0 and n == 0), stop=(q == KT - 1 and n == 2))
                t = c.on_pe(t)
                c.post("vread", t)
                to = dst[:, s, ds(i * width, width)]
                e, on_e, cp = (c.dve, c.on_dve, c.dve.tensor_copy) if s % 2 else (c.act, c.on_act, c.act.copy)
                c.wait(e, t)
                c.settle(e)
                c.post(f"vbank{s}", on_e(cp(to, bank)))
        c.post("wread0", t)
        c.join()

    def to(self, dst):
        c = self.c

        def evac(i, j, h, bank, t):
            m = bank.shape[1]
            d = dst(i, j)[:, h * HALF:h * HALF + m]
            e, on_e, cp = (c.dve, c.on_dve, c.dve.tensor_copy) if h else (c.act, c.on_act, c.act.copy)
            c.wait(e, t)
            c.settle(e)
            return on_e(cp(d, bank))
        return evac


    def attention(self, n, q, k, v, out, at, nkeys, bias=None, per_pair=None, diff=False):
        c, ps = self.c, self.ps
        qz = self.sb.at(at, 2, S)
        sc = self.sb.at(at + 2 * S, 4, S)
        pt = self.sb.at(at + 6 * S, 2, HALF)
        on = self.sb.at(at + 7 * S, 2, P)
        c.on_dve(c.dve.memset(qz, 0.0))
        c.join()
        stat = lambda iq, h: self.stat[:, 4 * ((2 * iq + h) % 16):4 * ((2 * iq + h) % 16) + 4]
        with c.fori(n) as i:
            if per_pair:
                per_pair(i)
            c.need(c.act, "scored")
            for h in range(2):
                o = slice(64 * h, 64 * h + 64)
                staged = c.on_act(c.act.activation(qz[o, h, :], q(i)[o, :], ACT.Copy, scale=0.125))
            src, maxed, exped, normed, group = {}, {}, {}, {}, [0]

            def scores(iq):
                nk = nkeys(iq)
                for h in range(2):
                    bank = ps[:, 2 * h:2 * h + 2, :].rearrange("p a b -> p (a b)")
                    c.wait(c.pe, staged)
                    c.need(c.pe, f"sbank{h}")
                    for b in range(0, nk, HALF):
                        m = min(HALF, nk - b)
                        t = c.pe.matmul(bank[:, b:b + m], qz[:, h, iq * P:(iq + 1) * P], k(i)[:, b:b + m], start=True, stop=True)
                    t = c.on_pe(t)
                    c.post("scored", t)
                    buf, s4 = sc[:, (2 * iq + h) % 4, 0:nk], stat(iq, h)
                    c.wait(c.dve, t)
                    if bias:
                        add, ready = bias(h, iq)
                        c.wait(c.dve, ready)
                        c.need(c.dve, f"turned{(2 * iq + h) % 4}")
                        c.settle(c.dve)
                        t = c.on_dve(c.dve.tensor_tensor_reduce(buf, bank[:, 0:nk], add, 1.0, -3.0e38, ALU.add, ALU.max, s4[:, 0:1]))
                        c.post(f"sbank{h}", t)
                        c.post(f"bias{h}{iq % 2}", t)
                        src[iq, h] = buf
                    else:
                        t = c.on_dve(c.dve.tensor_reduce(s4[:, 0:1], bank[:, 0:nk], AX.X, ALU.max))
                        src[iq, h] = bank[:, 0:nk]
                    c.wait(c.dve, t)
                    maxed[iq, h] = c.on_dve(c.dve.tensor_scalar(s4[:, 1:2], s4[:, 0:1], -1.0, None, ALU.mult))

            def exponentials(iq):
                for h in range(2):
                    s4, b = stat(iq, h), (2 * iq + h) % 4
                    c.wait(c.act, maxed[iq, h])
                    c.need(c.act, f"turned{b}")
                    exped[iq, h] = c.on_act(c.act.activation(sc[:, b, 0:nkeys(iq)], src[iq, h], ACT.Exp, bias=s4[:, 1:2],
                                                             accum_out=s4[:, 2:3]))
                    if not bias:
                        c.post(f"sbank{h}", exped[iq, h])

            def normalise(iq):
                s0, s1 = stat(iq, 0), stat(iq, 1)
                for h, s in ((0, s0), (1, s1)):
                    c.wait(c.dve, exped[iq, h])
                    t = normed[iq] = c.on_dve(c.dve.reciprocal(s[:, 3:4], s[:, 2:3]))
                if diff:
                    a, b = (2 * iq) % 4, (2 * iq + 1) % 4
                    c.wait(c.dve, t)
                    t = c.on_dve(c.dve.scalar_tensor_tensor(s1[:, 0:1], s0[:, 2:3], self.neglam, s1[:, 3:4], ALU.mult, ALU.mult))
                    c.wait(c.dve, t)
                    w = nkeys(iq)
                    t = exped[iq, 0] = c.on_dve(c.dve.scalar_tensor_tensor(sc[:, a, 0:w], sc[:, b, 0:w], s1[:, 0:1],
                                                                           sc[:, a, 0:w], ALU.mult, ALU.add))
                    c.post(f"turned{b}", t)

            def values(iq):
                nj = nkeys(iq) // P
                ob = ps[:, 6 + iq % 2, :]
                c.need(c.pe, f"obank{iq % 2}")
                pending = []

                def flush(keep):
                    t = None
                    while len(pending) > keep:
                        b, h, g, m, t = pending.pop(0)
                        c.wait(c.pe, t)
                        o = slice(0, P) if diff else slice(64 * h, 64 * h + 64)
                        for j in range(m):
                            t = c.pe.matmul(ob[:, o], pt[:, b, j * P:(j + 1) * P], v(i, g + j)[:, o],
                                            start=(g + j == 0), stop=(g + j == nj - 1))
                        t = c.on_pe(t)
                        c.post(f"pt{b}", t)
                    return t
                for h in range(1 if diff else 2):
                    buf = (2 * iq + h) % 4
                    c.wait(c.pe, exped[iq, h])
                    for g in range(0, nj, 4):
                        m, b = min(4, nj - g), group[0] % 2
                        group[0] += 1
                        c.need(c.pe, f"ptbank{b}")
                        for j in range(m):
                            t = c.pe.transpose(ps[:, 4 + b, j * P:(j + 1) * P], sc[:, buf, (g + j) * P:(g + j + 1) * P], self.ident)
                        t = c.on_pe(t)
                        c.post(f"turned{buf}", t)
                        c.wait(c.act, t)
                        c.need(c.act, f"pt{b}")
                        t = c.on_act(c.act.copy(pt[:, b, 0:m * P], ps[:, 4 + b, 0:m * P]))
                        c.post(f"ptbank{b}", t)
                        pending.append((b, h, g, m, t))
                        flush(1)
                return flush(0)

            def scale(iq, multiplied):
                ob, o = ps[:, 6 + iq % 2, :], on[:, iq % 2, :]
                c.wait(c.dve, multiplied, normed[iq])
                c.need(c.dve, f"out{iq % 2}")
                for h in range(1 if diff else 2):
                    w = slice(0, P) if diff else slice(64 * h, 64 * h + 64)
                    t = c.on_dve(c.dve.tensor_scalar(o[:, w], ob[:, w], stat(iq, h)[:, 3:4], None, ALU.mult))
                return t

            def turn_out(iq, scaled):
                ob = ps[:, 6 + iq % 2, :]
                c.wait(c.pe, scaled)
                t = c.on_pe(c.pe.transpose(ob[:, P:2 * P], on[:, iq % 2, :], self.ident))
                c.post(f"out{iq % 2}", t)
                c.wait(c.act, t)
                c.settle(c.act)
                c.post(f"obank{iq % 2}", c.on_act(c.act.copy(out(i, iq), ob[:, P:2 * P])))

            scores(0)
            exponentials(0)
            multiplied = None
            for iq in range(ST):
                normalise(iq)
                if iq:
                    scaled = scale(iq - 1, multiplied)
                if iq + 1 < ST:
                    scores(iq + 1)
                if iq:
                    turn_out(iq - 1, scaled)
                multiplied = values(iq)
                if iq + 1 < ST:
                    exponentials(iq + 1)
            turn_out(ST - 1, scale(ST - 1, multiplied))
        c.join()


    def block_one(self):
        self.mixer()
        self.feed_forward()
        self.embedding_gate()

    def mixer(self):
        c, sb, A, ps = self.c, self.sb, self.A, self.ps
        B = self.BIG
        w_in = A["w_in"].rearrange("l a b -> (l a) b")
        q, k = sb.at(B, 4, S), sb.at(B + 4096, 4, S)
        v = sb.at(B + 8192, ST, ATT_W)
        at = B + 12288
        LEAD = 16
        u = sb.at(at, POOL_G, LEAD + S)
        xs = self.norm_x(self.vec["g_mix_pre"], B + 17472, B)

        def qk(i, j):
            return sb.at(B, KT, S)[:, ds(2 * i + j, 1), :].rearrange("p a b -> p (a b)")
        self.linear(w_in, KT, lambda i, j: (2 * i + j) * P, 4, xs, self.to(qk))
        c.on_pool(c.pool.memset(u[:, :, 0:LEAD], 0.0))
        u0 = 3 * ATT_W + ATT_H
        self.linear(w_in, KT, lambda i, j: (2 * i + j) * P + u0, 2, xs,
                    self.to(lambda i, j: u[:, ds(2 * i + j, 1), LEAD:].rearrange("p a b -> p (a b)")))
        self.linear_tokens(w_in, 2 * ATT_W, 2, xs, v)

        fz, fa, fone = sb.at(at + 4160, S), sb.at(at + 5184, S), sb.at(at + 6208, S)
        bf = self.stat[0:ATT_H, 0:1]
        c.wait(c.sp, *(c.now(e) for e in c.engines))
        tb = c.load(self.misc, bf, A["b_forget"].rearrange("l h -> (l h)").rearrange("(h o) -> h o", o=1))
        c.wait(c.dve, tb)

        def forget(h, bank, t):
            c.wait(c.dve, t)
            return c.on_dve(c.dve.tensor_scalar(fz[0:ATT_H, h * HALF:(h + 1) * HALF], bank, bf, None, ALU.add))
        self.linear_once(w_in, KT, 3 * ATT_W, ATT_H, xs, forget)
        z, a, one = fz[0:ATT_H], fa[0:ATT_H], fone[0:ATT_H]
        c.on_dve(c.dve.memset(one, 1.0))
        c.wait(c.act, c.on_act(c.act.activation(a, z, ACT.Abs)))
        c.wait(c.act, c.on_act(c.act.activation(a, a, ACT.Exp, scale=-1.0)))
        t = c.on_act(c.act.activation(a, a, ACT.Ln, bias=self.ones[0:ATT_H, 0:1]))
        c.wait(c.dve, t)
        t = c.on_dve(c.dve.scalar_tensor_tensor(a, z, 0.0, a, ALU.min, ALU.subtract))
        c.wait(c.dve, t)
        t = c.on_dve(c.dve.tensor_tensor_scan(z, one, a, 0.0, ALU.mult, ALU.subtract))
        c.wait(c.sp, t)
        c.load(self.misc, self.scratch_c, z)

        mix = self.hn
        s1, s2, inv = sb.at(at + 7232, LEAD + S), sb.at(at + 8272, LEAD + S), sb.at(at + 9312, S)
        pw = sb.at(self.W, POOL_G, P)
        c.need(c.sp, "wread0", "wread1")
        tw = c.load(self.wsem[0], pw, A["w_pool"].rearrange("l g a b -> (l g a) b").rearrange("(g a) b -> a g b", a=P))
        c.join()
        free = None
        for g in range(POOL_G):
            win = 2 << g
            src = u[:, g, :]
            c.wait(c.pool, *(c.now(e) for e in ("dve", "pe")))
            c.wait(c.pool, c.on_pool(c.pool.iota(inv, [[1, S]], base=1, channel_multiplier=0,
                                                 allow_small_or_imprecise_dtypes=True)))
            t = c.on_pool(c.pool.tensor_scalar(inv, inv, float(win), None, ALU.min))
            c.wait(c.dve, t)
            c.on_dve(c.dve.reciprocal(inv, inv))
            cur, bufs, step = src, [s1, s2], 1
            while step < win:
                nxt = bufs[0]
                bufs.reverse()
                c.on_dve(c.dve.memset(nxt[:, 0:LEAD], 0.0))
                t = c.on_dve(c.dve.tensor_tensor(nxt[:, LEAD:], cur[:, LEAD:], cur[:, LEAD - step:LEAD + S - step], ALU.add))
                c.wait(c.dve, t)
                cur, step = nxt, step * 2
            t = c.on_dve(c.dve.tensor_tensor(cur[:, LEAD:], cur[:, LEAD:], inv, ALU.mult))
            c.wait(c.dve, t)
            t = c.on_dve(c.dve.tensor_tensor(cur[:, LEAD:], cur[:, LEAD:], src[:, LEAD:], ALU.subtract))
            c.wait(c.pe, t, tw, free)
            for h in range(2):
                t = c.on_pe(c.pe.matmul(ps[:, h, :], pw[:, g, :], cur[:, LEAD + h * HALF:LEAD + (h + 1) * HALF], start=True, stop=True))
            c.wait(c.act, t)
            free = c.on_act(c.act.activation(mix[:, 4 + g, :], ps[:, 0:2, :].rearrange("p a b -> p (a b)"), ACT.Copy,
                                             scale=self.vec["pool_scale"][:, g:g + 1]))
        c.join()
        c.post("wread0", c.now("pe"))

        cb, bb = sb.at(at + 7424 + 0, 2, S), sb.at(at + 7424 + 2 * S, 4, S)

        masked = c.pool.to_reg(NEG)

        def rows_of_pair(i):
            c.need(c.sp, "biased")
            self.tc = c.load(self.misc, cb, self.scratch_c[ds(2 * i, 2), :].partition_broadcast(P))

        def bias(h, iq):
            buf = bb[:, 2 * h + iq % 2, 0:(iq + 1) * P]
            c.wait(c.pool, self.tc)
            c.need(c.pool, f"bias{h}{iq % 2}")
            c.settle(c.pool)
            t = c.on_pool(c.pool.affine_select(buf, cb[:, h, 0:(iq + 1) * P], [[-1, (iq + 1) * P]], ALU.is_ge, masked,
                                               base=iq * P, channel_multiplier=1))
            c.post("biased", t)
            return buf, t
        c.wait(c.sp, *(c.now(e) for e in ("pe", "act", "dve", "pool", "misc")))
        self.attention(
            4, lambda i: q[:, ds(i, 1), :].rearrange("p a b -> p (a b)"),
            lambda i: k[:, ds(i, 1), :].rearrange("p a b -> p (a b)"),
            lambda i, j: v[:, j, ds(i * P, P)],
            lambda i, iq: mix[:, ds(i, 1), iq * P:(iq + 1) * P].rearrange("p a b -> p (a b)"),
            at, lambda iq: (iq + 1) * P, bias=bias, per_pair=rows_of_pair)

        for t0, gain in ((0, "g_attn_grp"), (4, "g_pool_grp")):
            tiles = [mix[:, t0 + j, :] for j in range(4)]
            r = sb.at(B, S)
            self.rstd(tiles, S, ATT_W, self.eps, r, B + S)
            self.scale_tiles(tiles, tiles, self.vec[gain], r)
        c.join()
        y = sb.at(B + 4096, KT, S)
        mix = self.split(self.HN, B + 12288, self.HN, KT, S)
        self.linear(A["w_out"].rearrange("l a b -> (l a) b"), KT, lambda i, j: (2 * i + j) * P, 4, mix,
                    self.to(lambda i, j: y[:, ds(2 * i + j, 1), :].rearrange("p a b -> p (a b)")))
        self.add_normed(y, self.vec["g_mix_post"], B)

    def feed_forward(self):
        c, sb, sr, A = self.c, self.sb, self.sr, self.A
        B = self.BIG
        y = sb.at(B + 8192, KT, S)
        down, down_hi = B + 16384, B + 18432
        g_hi, g_lo, g = B + 20480, B + 22528, sb.at(B + 24576, 2, S)
        xs = self.norm_x(self.vec["g_ffn_pre"], B, B + 8192)
        w = [A[n].rearrange("l a b -> (l a) b") for n in ("w_ffn_gate", "w_ffn_up")]
        w_down = A["w_ffn_down"].rearrange("l a b -> (l a) b").rearrange("(k p) n -> p k n", p=P)
        c.wait(c.dve, c.on_pool(c.pool.memset(y, 0.0)))
        c.wait(c.pe, *(c.now(e) for e in c.engines))
        self.fetch(w[0], KT, 0, 0)

        def fetch_down(i):
            raw = sb.at(down, 2, D)
            c.need(c.sp, "down_read")
            t = c.load(self.wsem[2], raw, w_down[:, ds(2 * i, 2), :])
            c.wait(c.act, t)
            for q in range(2):
                hi = sr.at(down_hi + q * D, D)
                th = c.on_act(c.act.copy(hi, raw[:, q, :]))
                c.wait(c.dve, t, th)
                tl = c.on_dve(c.dve.tensor_tensor(sr.at(down + q * D, D), raw[:, q, :], hi.bitcast(F32), ALU.subtract))
            c.post("down_ready", th, tl)

        def down_part():
            wh, wl, gh, gl = ([sr.at(col + q * S, S) for q in range(2)] for col in (down_hi, down, g_hi, g_lo))
            c.need(c.pe, "down_ready", "g0", "g1")
            for o in range(KT):
                for h in range(2):
                    b = 4 + (2 * o + h) % 4
                    out, tok = slice(o * P, (o + 1) * P), slice(h * HALF, (h + 1) * HALF)
                    c.need(c.pe, f"dbank{b}")
                    t = c.on_pe(self.product(self.ps[:, b, :], lambda q: (wh[q][:, out], wl[q][:, out]),
                                             lambda q: (gh[q][:, tok], gl[q][:, tok]), 2))
                    c.wait(c.dve, t)
                    c.post(f"dbank{b}", c.on_dve(c.dve.tensor_tensor(y[:, o, tok], y[:, o, tok], self.ps[:, b, :], ALU.add)))
            c.post("down_read", t)

        def evac(n):
            gn = g[:, n, :]

            def of(i, j, h, bank, t):
                part = gn[:, h * HALF:(h + 1) * HALF]
                if j == 0:
                    c.need(c.act, f"g{n}")
                    c.wait(c.act, t)
                    self.silu[h] = c.on_act(c.act.activation(part, bank, ACT.Silu))
                    return self.silu[h]
                c.wait(c.dve, t, self.silu[h])
                free = t = c.on_dve(c.dve.tensor_tensor(part, part, bank, ALU.mult))
                if h == 1:
                    c.need(c.act, "down_read")
                    c.need(c.dve, "down_read")
                    c.wait(c.act, t)
                    hi = sr.at(g_hi + n * S, S)
                    th = c.on_act(c.act.copy(hi, gn))
                    c.wait(c.dve, th)
                    tl = c.on_dve(c.dve.tensor_tensor(sr.at(g_lo + n * S, S), gn, hi.bitcast(F32), ALU.subtract))
                    c.post(f"g{n}", th, tl)
                return free
            return of
        self.silu = {}

        def pair(i, first=False, last=False):
            for n in range(2):
                self.fetch(w[1], KT, (2 * i + n) * P, 1)
                self.weight_tile(KT, i, 0, xs, evac(n))
                if n == 0:
                    if not first:
                        down_part()
                    fetch_down(i)
                if not (n and last):
                    self.fetch(w[0], KT, (2 * i + n + 1) * P, 0)
                self.weight_tile(KT, i, 1, xs, evac(n))
        pair(0, first=True)
        with c.fori(FT // 2 - 2) as i:
            pair(i + 1)
        pair(FT // 2 - 1, last=True)
        down_part()
        c.join()
        self.add_normed(y, self.vec["g_ffn_post"], B)

    def embedding_gate(self):
        c, sb, A = self.c, self.sb, self.A
        B = self.BIG
        pT = sb.at(B, PLE // P, S)
        self.load_rows(A["p"].rearrange("l b s d -> (l b s) d"), S, PLE, pT, B + 2 * S)
        e = self.hn
        pT = self.split(B, B + 2 * S, B, PLE // P, S)
        self.linear(A["w_ple_proj"].rearrange("l a b -> (l a) b"), PLE // P, lambda i, j: (2 * i + j) * P, 4, pT,
                    self.to(lambda i, j: e[:, ds(2 * i + j, 1), :].rearrange("p a b -> p (a b)")))
        r = sb.at(B, S)
        tiles = [e[:, j, :] for j in range(KT)]
        self.rstd(tiles, S, D, self.eps, r, B + S)
        self.scale_tiles(tiles, tiles, self.vec["g_ple"], r)
        c.join()
        s = sb.at(B, 4, HALF)
        y = sb.at(B + 2048, KT, S)
        xs = self.split(self.X, B + 10240, B + 18432, KT, S)

        def gate(i, j, h, bank, t):
            b = s[:, 2 * j + h, :]
            c.wait(c.act, t)
            c.need(c.act, f"gated{j}{h}")
            t = free = c.on_act(c.act.activation(b, bank, ACT.Sigmoid))
            c.wait(c.dve, t)
            part = slice(h * HALF, (h + 1) * HALF)
            c.post(f"gated{j}{h}", c.on_dve(c.dve.tensor_tensor(
                y[:, ds(2 * i + j, 1), part].rearrange("p a b -> p (a b)"), b,
                e[:, ds(2 * i + j, 1), part].rearrange("p a b -> p (a b)"), ALU.mult)))
            return free
        self.linear(A["w_ple_gate"].rearrange("l a b -> (l a) b"), KT, lambda i, j: (2 * i + j) * P, 4, xs, gate)
        for j in range(KT):
            c.on_dve(c.dve.tensor_tensor(self.x[:, j, :], self.x[:, j, :], y[:, j, :], ALU.add))
        c.join()

    def store(self):
        c, ps = self.c, self.ps
        o = self.out.rearrange("b s d -> (b s) d")
        st = self.sb.at(self.BIG, 2, KT, P)
        row = self.sb.at(self.BIG + 2 * D, 2, D)
        with c.fori(ST // 2) as i:
            for j in range(2):
                c.wait_before(c.pool, f"turned{j}")
                t = c.on_pool(c.pool.tensor_copy(st[:, j], self.x[:, :, ds(i * 2 * P + j * P, P)]))
                c.wait(c.pe, t)
                c.wait_before(c.pe, f"a{j}", f"b{j}")
                for f in range(KT):
                    t = c.pe.transpose(ps[:, 2 * j + f // 4, (f % 4) * P:(f % 4 + 1) * P], st[:, j, f, :], self.ident)
                t = c.on_pe(t, label=f"turned{j}")
                c.wait(c.act, t)
                c.wait(c.dve, t)
                c.wait_before(c.act, f"stored{j}")
                c.wait_before(c.dve, f"stored{j}")
                ta = c.on_act(c.act.copy(row[:, j, 0:HALF], ps[:, 2 * j, :]), label=f"a{j}")
                tb = c.on_dve(c.dve.tensor_copy(row[:, j, HALF:D], ps[:, 2 * j + 1, :]), label=f"b{j}")
                c.wait(c.sp, ta, tb)
                c.load(self.io[j], o[ds(i * 2 * P + j * P, P), :], row[:, j, :], label=f"stored{j}")
        c.wait(c.sp, c.now("io0"), c.now("io1"))


    def block_two(self):
        self.memory()
        self.layer_a()
        self.layer_b()

    def memory(self):
        c, sb = self.c, self.sb
        B = self.BIG
        self.mhat = sb.at(B + 25600, KT, MEM)
        self.load_rows(self.A["mem_2"].rearrange("b m d -> (b m) d"), MEM, D, self.mhat, B)
        r = sb.at(B, MEM)
        tiles = [self.mhat[:, j, :] for j in range(KT)]
        c.wait(c.dve, self.rstd(tiles, MEM, D, self.eps, r, B + MEM))
        for t in tiles:
            c.on_dve(c.dve.tensor_tensor(t, t, r, ALU.mult))
        c.join()

    def do(self, engine, deps, make):
        c = self.c
        c.wait(engine, *deps)
        return c.mark(c.names[id(engine)], make())

    def layer_a(self):
        c, sb, A, ps = self.c, self.sb, self.A, self.ps
        B = self.BIG
        w_in = A["a_w_in_2"].rearrange("l a b -> (l a) b")
        mix = sb.at(B, KT, S)
        rkv = sb.at(B, 3 * BT, S)
        lora = sb.at(B + 18432, S)
        rs12 = sb.at(B + 19456, S)
        w2, a2 = sb.at(B + 20480, BR), sb.at(B + 20480 + BR, BR)
        zt = [sb.at(B + 22016 + j * (S + 1), S + 1) for j in range(2)]
        dz = sb.at(B + 22016 + 2 * (S + 1), S)
        reset = sb.at(B + 22016, BT, CH)
        mu = self.vec["a_shift_mu_2"]
        self.keep_x()
        xs = self.norm_x(self.vec["pre_norm_2"][:, 0:KT], self.X, B)
        for j in range(2):
            c.on_dve(c.dve.memset(zt[j][:, 0:1], 0.0))
        c.on_dve(c.dve.memset(w2, 0.0))
        c.on_dve(c.dve.memset(a2, 0.0))
        c.wait(c.sp, c.now("dve"))
        tl = c.load(self.misc, w2[0:LORA, :], A["a_w2_2"].rearrange("l a b -> (l a) b"))
        tl = c.load(self.misc, a2[LORA:P, :], A["a_a2_2"].rearrange("l a b -> (l a) b"))
        c.join()

        def shifted(dst, j, col):
            t = self.do(c.dve, [self.copied[0], self.copied[1]],
                        lambda: c.dve.tensor_tensor(dz, zt[j][:, 0:S], zt[j][:, 1:S + 1], ALU.subtract))
            c.wait(c.dve, t)
            return c.dve.scalar_tensor_tensor(dst, dz, mu[:, col], zt[j][:, 1:S + 1], ALU.mult, ALU.add)

        self.copied = {}

        def evac(i, j, h, bank, t):
            e, on_e, cp = ((c.act, c.on_act, c.act.copy), (c.dve, c.on_dve, c.dve.tensor_copy))[h]
            c.wait(e, t)
            c.need(e, f"shifted{j}")
            free = self.copied[h] = on_e(cp(zt[j][:, 1 + h * HALF:1 + (h + 1) * HALF], bank))
            if h == 1:
                c.need(c.dve, f"shifted{1 - j}")
                ins = shifted(rkv[:, ds(2 * i + j, 1), :].rearrange("p a b -> p (a b)"), j, ds(2 * i + j, 1))
                c.post(f"shifted{j}", c.on_dve(ins))
            return free
        self.linear(w_in, KT, lambda i, j: (2 * i + j) * P, 9, xs, evac)

        def evac_lora(h, bank, t):
            self.copied[h] = self.do(c.act, [t], lambda: c.act.copy(zt[0][:, 1 + h * HALF:1 + (h + 1) * HALF], bank))
            if h == 1:
                t = c.on_dve(shifted(lora, 0, slice(18, 19)))
                self.do(c.act, [t], lambda: c.act.activation(lora[0:LORA, :], lora[0:LORA, :], ACT.Tanh))
            return self.copied[h]
        self.linear_once(w_in, KT, 3 * BR, P, xs, evac_lora)
        self.fetch_x()

        sq = [zt[0][:, 0:S], zt[1][:, 0:S]]
        read = [None, None]
        for p in range(BT):
            c.wait(c.act, read[p % 2])
            t = c.on_act(c.act.activation(sq[p % 2], rkv[:, BT + p, :], ACT.Square, scale=self.vec["a_k_k_2"][:, p:p + 1]))
            c.wait(c.pe, t)
            for h in range(2):
                t = c.pe.matmul(ps[0:12, h, :], self.sel[:, p, :], sq[p % 2][:, h * HALF:(h + 1) * HALF],
                                start=(p == 0), stop=(p == BT - 1))
            read[p % 2] = c.on_pe(t)
        n2 = rs12[0:12, :]
        t = self.do(c.dve, [read[1]], lambda: c.dve.tensor_scalar(
            n2, ps[0:12, 0:2, :].rearrange("p a b -> p (a b)"), 1e-12, None, ALU.max))
        t = self.do(c.act, [t], lambda: c.act.activation(n2, n2, ACT.Ln))
        self.do(c.act, [t], lambda: c.act.activation(n2, n2, ACT.Exp, scale=-0.5))
        c.join()
        c.on_dve(c.dve.memset(reset, 1.0))
        c.wait(c.dve, c.now("dve"))
        c.on_dve(c.dve.memset(reset[:, :, 0:1], 0.0))
        c.wait(c.dve, tl)
        c.join()
        self.rwkv(rkv, lora, rs12, w2, a2, reset, (B + 22016 + BR // 2, B + 25600))
        self.rwkv_norm(mix, rkv)

        xs = self.norm_x(self.vec["pre_norm_2"][:, 0:KT], B + 12288, B + 20480)
        gate0 = 3 * BR + 2 * LORA
        self.finish_layer(0, w_in, gate0, gate0 + BR, xs, B, sb.at(B + 8192, 4, S), B + 12288, B + 20480)

    def rwkv(self, rkv, lora, rs12, w2, a2, reset, spare):
        c, sb, ps = self.c, self.sb, self.ps
        pe, act, dve, pool, do = c.pe, c.act, c.dve, c.pool, self.do
        F16 = mybir.dt.float16
        rooms = [[self.HN, self.CONST], list(spare)]

        def buf(*shape, dtype=F32):
            shape = shape or (BT, CH)
            n = math.prod(shape)
            cols = n if dtype == F32 else n // 2
            room = next(r for r in rooms if r[0] + cols <= r[1])
            flat_ = sb.at(room[0], cols)
            room[0] += cols
            flat_ = flat_ if dtype == F32 else flat_.bitcast(dtype)
            return flat_.rearrange("p (a b) -> p a b", a=shape[0]) if len(shape) == 2 else \
                flat_.rearrange("p (a b c) -> p a b c", a=shape[0], b=shape[1])
        tw, ta, ld, run, pinv = buf(), buf(), buf(), buf(), buf()
        pc = buf(BT, CH + 1)
        kk, kp, nb, rk = (buf() for _ in range(4))
        ar_e, bb, kb, vc = buf(BT, 2, CH), buf(), buf(), buf()
        ar, lr, ak = ([buf(*sh) for _ in range(2)] for sh in ((BT, 2, CH), (BT, 2 * CH), (BT, 2 * CH)))
        vt, kt, bt, xt = ([buf() for _ in range(2)] for _ in range(4))
        pt = [buf(BT, 1) for _ in range(2)]
        low, z, zi = buf(), buf(), buf()
        x16, xt16, w16, l16 = (buf(BT, CH, dtype=F16) for _ in range(4))
        r16 = w16
        rhs, g, st = buf(), buf(), buf()
        V = self.vec
        w0, a0, k_k, k_a, r_k = (over_tokens(V[n], CH) for n in ("a_w0_2", "a_a0_2", "a_k_k_2", "a_k_a_2", "a_r_k_2"))
        m3 = over_pairs(sb.at(self.up_col, 2 * CH), 3)
        flat = lambda a: a.rearrange("p a b -> p (a b)")
        of = lambda a: (lambda p: a[:, p, :])

        def bank(b, n=BT, w=CH):
            return ps[:, b, 0:n * w].rearrange("p (a b) -> p a b", a=n)

        def free(b, *ticks):
            c.post(f"bank{b}", *ticks)

        def heads(out, pairs):
            c.settle(pe)
            for p in range(BT):
                for n, (lhsT, rhs_) in enumerate(pairs):
                    for h in range(2):
                        o = slice(64 * h, 64 * h + 64)
                        t = pe.matmul(out(p)[o], lhsT(p)[o], rhs_(p)[o], start=(n == 0), stop=(n == len(pairs) - 1),
                                      skip_group_check=True)
            return c.on_pe(t)

        def elementwise(m):
            tok = ds(m * CH, CH)
            rC, kC, vC = (rkv[:, n * BT:(n + 1) * BT, tok] for n in range(3))
            c.need(pe, "bank7")
            for p in range(BT):
                t = pe.matmul(bank(7)[:, p, :], w2[:, p * P:(p + 1) * P], lora[:, tok], start=True, stop=True)
            t_w = c.on_pe(t)
            t = do(dve, [t_w], lambda: dve.tensor_tensor(tw, bank(7), w0, ALU.add))
            free(7, t)
            t_tw = do(act, [t], lambda: act.activation(tw, tw, ACT.Tanh, scale=0.5))
            yield
            c.need(pe, "bank0")
            for p in range(BT):
                t = pe.matmul(bank(0)[:, p, :], a2[:, p * P:(p + 1) * P], lora[:, tok], start=True, stop=True)
            t_a = c.on_pe(t)
            t = do(dve, [t_a], lambda: dve.tensor_tensor(ta, bank(0), a0, ALU.add))
            free(0, t)
            t_ta = do(act, [t], lambda: act.activation(ta, ta, ACT.Tanh, scale=0.5))
            yield
            c.need(pe, "bank1")
            for p in range(BT):
                t = pe.matmul(bank(1)[:, p, :], self.selt[0:12, p * P:(p + 1) * P], rs12[0:12, tok], start=True, stop=True)
            t_n = c.on_pe(t)
            c.need(pool, "e_read", "e_bonus")
            c.settle(pool)
            t_vc = do(pool, [], lambda: pool.tensor_copy(vc, vC))
            c.need(dve, "e_read", "e_bonus", "e_pool")
            t = do(dve, [t_n], lambda: dve.tensor_tensor(kk, kC, k_k, ALU.mult))
            t_kk = do(dve, [t], lambda: dve.tensor_tensor(kk, kk, bank(1), ALU.mult))
            free(1, t_kk)
            yield
            t = do(dve, [t_tw], lambda: dve.tensor_scalar(ld, tw, -0.5 * DECAY_C, -0.5 * DECAY_C, ALU.mult, ALU.add))
            t_run = do(dve, [t], lambda: dve.tensor_tensor_scan(flat(run), flat(reset), flat(ld), 0.0, ALU.mult, ALU.add))
            t_pc = do(act, [t_run], lambda: act.activation(pc[:, :, 1:CH + 1], run, ACT.Exp))
            t_pi = do(act, [], lambda: act.activation(pinv, run, ACT.Exp, scale=-1.0))
            t_ra = do(dve, [t_ta], lambda: dve.tensor_scalar(ta, ta, 0.5, 0.5, ALU.mult, ALU.add))
            t = do(dve, [t_ra], lambda: dve.scalar_tensor_tensor(kp, ta, -1.0, k_a, ALU.add, ALU.mult))
            t_kp = do(dve, [t], lambda: dve.scalar_tensor_tensor(kp, kp, 1.0, kC, ALU.add, ALU.mult))
            t = do(pool, [t_kp], lambda: pool.tensor_tensor(rk, rC, kp, ALU.mult))
            t_rk = do(pool, [t], lambda: pool.tensor_tensor(rk, rk, r_k, ALU.mult))
            t_nb = do(dve, [t_kk], lambda: dve.scalar_tensor_tensor(nb, kk, -1.0, ta, ALU.mult, ALU.mult))
            yield
            do(dve, [t_pc], lambda: dve.tensor_tensor(ar_e[:, :, 0, :], kk, pc[:, :, 0:CH], ALU.mult))
            t_ar = do(dve, [], lambda: dve.tensor_tensor(ar_e[:, :, 1, :], rC, pc[:, :, 1:CH + 1], ALU.mult))
            t_b = do(dve, [t_pi, t_nb], lambda: dve.tensor_tensor(bb, nb, pinv, ALU.mult))
            t_k = do(pool, [t_pi], lambda: pool.tensor_tensor(kb, kp, pinv, ALU.mult))
            c.post("e_out", t_ar, t_b, t_k, t_vc, t_pc)
            c.post("e_pool", t_k)
            c.need(pe, "bank7")
            c.wait(pe, t_rk)
            c.settle(pe)
            t = c.on_pe(pe.matmul(bank(7), self.block64, flat(rk), start=True, stop=True))
            t = do(dve, [t, t_vc], lambda: dve.scalar_tensor_tensor(vC, bank(7), 64.0, vc, ALU.mult, ALU.mult))
            free(7, t)
            c.post("e_bonus", t)
            yield

        def products(s):
            c.need(pe, "e_out", "bank0", "bank1")
            arf = ar_e.rearrange("p a b c -> p a (b c)")
            three = lambda b: (lambda p: bank(b + p // 3, 3, 2 * CH)[:, p % 3, :])
            t_lr = heads(three(0), [(of(bb), of(arf))])
            c.need(dve, f"state{s}", "inv")
            do(dve, [t_lr], lambda: dve.tensor_tensor(lr[s][:, 0:3, :], bank(0, 3, 2 * CH), m3, ALU.mult))
            t_lrs = do(dve, [], lambda: dve.tensor_tensor(lr[s][:, 3:6, :], bank(1, 3, 2 * CH), m3, ALU.mult))
            free(0, t_lrs)
            free(1, t_lrs)
            c.need(pool, "e_out", f"state{s}")
            c.settle(pool)
            t1 = do(pool, [], lambda: pool.tensor_copy(ar[s], ar_e))
            t2 = do(pool, [], lambda: pool.tensor_copy(pt[s], pc[:, :, CH:CH + 1]))
            c.post(f"ar{s}", t1, t2)
            c.need(pe, "bank4")
            t_x = heads(of(bank(4)), [(lambda p: ar_e[:, p, 0, :], of(bb))])
            c.need(act, "inv", f"state{s}")
            t_l16 = do(act, [t_lrs], lambda: act.copy(l16, lr[s][:, :, 0:CH]))
            t_low = do(dve, [t_x], lambda: dve.tensor_tensor(low, bank(4), over_pairs(self.low), ALU.mult))
            free(4, t_low)
            c.need(pool, "inv")
            t = do(pool, [t_lrs], lambda: pool.tensor_tensor(zi, lr[s][:, :, 0:CH], over_pairs(self.level0t), ALU.mult))
            t_xt = do(pool, [t], lambda: pool.tensor_tensor(xt16, zi, over_pairs(self.eye), ALU.add))
            t = do(dve, [t_low], lambda: dve.tensor_tensor(z, low, over_pairs(self.level[0]), ALU.mult))
            t_x = do(dve, [t], lambda: dve.tensor_tensor(x16, z, over_pairs(self.eye), ALU.add))
            c.post("inv_in", t_l16, t_x)
            c.post("inv_xt", t_xt)
            c.need(pe, "bank2", "bank3")
            t_ak = heads(three(2), [(of(kb), of(arf))])
            do(dve, [t_ak], lambda: dve.tensor_tensor(ak[s][:, 0:3, :], bank(2, 3, 2 * CH), m3, ALU.mult))
            t_aks = do(dve, [], lambda: dve.tensor_tensor(ak[s][:, 3:6, :], bank(3, 3, 2 * CH), m3, ALU.mult))
            free(2, t_aks)
            free(3, t_aks)
            yield
            for n, (dst, src) in enumerate(((vt[s], vc), (kt[s], kb), (bt[s], bb))):
                c.need(pe, "bank7")
                t_pe = heads(of(bank(7)), [(of(src), lambda p: self.eye)])
                t = do(act, [t_pe], lambda: act.copy(dst, bank(7)))
                free(7, t)
                if n == 2:
                    c.post("e_read", t_pe, t1, t2)
                    c.post(f"tri{s}", t_aks, t_lrs, t)
                yield

        def inverse(s):
            c.need(pe, "inv_in")
            t_x = t_xt = None
            for lev in range(1, 6):
                c.need(pe, "bank4")
                c.wait(pe, t_x)
                t = heads(of(bank(4)), [(of(l16), of(x16))])
                t_w = do(dve, [t], lambda: dve.tensor_tensor(w16, bank(4), over_pairs(self.level[lev]), ALU.mult))
                free(4, t_w)
                yield
                c.need(pe, "bank5", "bank6")
                c.wait(pe, t_w, t_xt)
                c.need(pe, "inv_xt")
                t1 = heads(of(bank(5)), [(of(xt16), of(w16))])
                t2 = heads(of(bank(6)), [(of(w16), of(xt16))])
                t_x = do(dve, [t1], lambda: dve.tensor_tensor(x16, x16, bank(5), ALU.add))
                free(5, t_x)
                t_xt = do(dve, [t2], lambda: dve.tensor_tensor(xt16, xt16, bank(6), ALU.add))
                free(6, t_xt)
                yield
            t_z = do(act, [t_xt], lambda: act.copy(z, xt16))
            t_zi = do(pool, [t_xt], lambda: pool.tensor_tensor(zi, xt16, over_pairs(self.eye), ALU.subtract))
            c.need(pe, "bank4")
            c.wait(pe, t_z)
            t = heads(of(bank(4)), [(of(low), of(z))])
            t = do(dve, [t, t_zi], lambda: dve.tensor_tensor(r16, bank(4), zi, ALU.subtract))
            free(4, t)
            yield
            c.need(pe, "bank5")
            c.wait(pe, t)
            t = heads(of(bank(5)), [(of(x16), of(r16))])
            c.need(dve, f"state{s}")
            t = do(dve, [t], lambda: dve.tensor_tensor(xt[s], z, bank(5), ALU.add))
            free(5, t)
            c.post(f"xt{s}", t)
            c.post("inv", t)
            yield

        def state_step(m, s):
            c.need(pe, f"tri{s}", f"ar{s}", "st", "bank0")
            t = heads(of(bank(0)), [(lambda p: ar[s][:, p, 0, :], of(st)), (lambda p: ak[s][:, p, 0:CH], of(vt[s]))])
            t = do(act, [t], lambda: act.copy(rhs, bank(0)))
            free(0, t)
            yield
            c.need(pe, f"xt{s}", "bank1")
            c.wait(pe, t)
            t = heads(of(bank(1)), [(of(xt[s]), of(rhs))])
            t = do(act, [t], lambda: act.copy(g, bank(1)))
            free(1, t)
            yield
            c.need(pe, "bank2", "bank3")
            c.wait(pe, t)
            t_s = heads(of(bank(2)), [(of(kt[s]), of(vt[s])), (of(bt[s]), of(g))])
            yield
            t_y = heads(of(bank(3)), [(of(st), lambda p: ar[s][:, p, 1, :]), (of(vt[s]), lambda p: ak[s][:, p, CH:2 * CH]),
                                      (of(g), lambda p: lr[s][:, p, CH:2 * CH])])
            c.wait(act, t_y)
            c.settle(act)
            t = c.on_act(act.copy(rkv[:, 0:BT, ds(m * CH, CH)], bank(3)))
            free(3, t)
            t = do(dve, [t_s, t_y], lambda: dve.tensor_tensor(st, st, bank(2), ALU.add))
            free(2, t)
            t = do(dve, [t], lambda: dve.tensor_tensor(st, st, pt[s].broadcast_to((P, BT, CH)), ALU.mult))
            c.post("st", t)
            c.post(f"state{s}", t_y, t)
            yield

        def emit(order, **parts):
            for letter in order.replace(" ", ""):
                next(parts[letter], None)

        c.on_dve(dve.memset(pc, 1.0))
        c.on_dve(dve.memset(st, 0.0))
        c.join()
        emit("E" * 7, E=elementwise(0))
        emit("P" * 5, P=products(0))
        emit("I" * 13, I=inverse(0))
        emit("E" * 7, E=elementwise(1))

        def step(m, j, last=False):
            emit("P E IP IP IP E I E I E I S I E I S I E I S I S I I",
                P=products((j + 1) % 2), I=inverse((j + 1) % 2), S=state_step(m, j % 2),
                E=iter(()) if last else elementwise(m + 2))
        with c.fori(NCH // 2 - 1) as i:
            for j in range(2):
                step(i * 2 + j, j)
        step(NCH - 2, 0, last=True)
        emit("S" * 5, S=state_step(NCH - 1, 1))
        c.join()
        for j in range(2):
            c.post(f"wread{j}", *(c.now(e) for e in c.engines))

    def rwkv_norm(self, y, rkv):
        c, sb, ps, do = self.c, self.sb, self.ps, self.do
        yc, sq, rs = (sb.at(self.HN + j * S, S) for j in range(3))
        both = ps[:, 0:2, :].rearrange("p a b -> p (a b)")
        var = ps[:, 2:4, :].rearrange("p a b -> p (a b)")
        one = lambda a, i: a[:, ds(i, 1), :].rearrange("p a b -> p (a b)")
        with c.fori(BT) as i:
            for e in (c.pe, c.act, c.dve):
                c.wait_before(e, "end")
            for h in range(2):
                t = c.pe.matmul(ps[:, h, :], self.block64, one(y, i)[:, h * HALF:(h + 1) * HALF], start=True, stop=True)
            t = c.on_pe(t)
            t = do(c.dve, [t], lambda: c.dve.tensor_tensor(yc, one(y, i), both, ALU.subtract))
            t = do(c.act, [t], lambda: c.act.activation(sq, yc, ACT.Square))
            c.wait(c.pe, t)
            for h in range(2):
                t = c.pe.matmul(ps[:, 2 + h, :], self.block64, sq[:, h * HALF:(h + 1) * HALF], start=True, stop=True)
            t = c.on_pe(t)
            t = do(c.act, [t], lambda: c.act.activation(rs, var, ACT.Ln, bias=self.lnx_eps))
            t = do(c.act, [t], lambda: c.act.activation(rs, rs, ACT.Exp, scale=-0.5))
            w = self.vec["a_lnx_w_2"][:, ds(i, 1)]
            b = self.vec["a_lnx_b_2"][:, ds(i, 1)]
            t = do(c.dve, [t], lambda: c.dve.scalar_tensor_tensor(yc, yc, w, rs, ALU.mult, ALU.mult))
            c.wait(c.dve, t)
            c.on_dve(c.dve.scalar_tensor_tensor(one(y, i), yc, b, rkv[:, ds(i + 2 * BT, 1), :].rearrange("p a b -> p (a b)"),
                                                ALU.add, ALU.add), label="end")
        c.join()

    def finish_layer(self, l, w_in, gate_col, mem_col, xs, mix_at, qg, tmp, tmp2):
        c, sb, A, do = self.c, self.sb, self.A, self.do
        s = sb.at(tmp2, 4, HALF)
        mix = sb.at(mix_at, KT, S)

        def silu_into(i, j, h, bank, t):
            b = s[:, 2 * j + h, :]
            c.wait(c.act, t)
            c.need(c.act, f"gated{j}{h}")
            free = c.on_act(c.act.activation(b, bank, ACT.Silu))
            c.wait(c.dve, free)
            d = mix[:, ds(2 * i + j, 1), h * HALF:(h + 1) * HALF].rearrange("p a b -> p (a b)")
            c.post(f"gated{j}{h}", c.on_dve(c.dve.tensor_tensor(d, d, b, ALU.mult)))
            return free
        self.linear(w_in, KT, lambda i, j: (2 * i + j) * P + gate_col, 3, xs, silu_into)
        self.linear(w_in, KT, lambda i, j: (2 * i + j) * P + mem_col, 1, xs,
                    self.to(lambda i, j: qg[:, j, :]))
        self.linear(w_in, KT, lambda i, j: (2 * i + j) * P + mem_col + MEM_W, 1, xs,
                    lambda i, j, h, bank, t: do(c.act, [t], lambda: c.act.activation(
                        qg[:, 2 + j, h * HALF:(h + 1) * HALF], bank, ACT.Silu)))
        mn = sb.at(tmp, KT, MEM)
        km, vm = sb.at(tmp + 4096, 2, MEM), sb.at(tmp + 4608, 2, MEM_W)
        for j in range(KT):
            c.on_dve(c.dve.tensor_scalar(mn[:, j, :], self.mhat[:, j, :],
                                         self.vec["mem_norm_2"][:, l * KT + j:l * KT + j + 1], None, ALU.mult))
        c.join()
        mn = self.split(tmp, tmp + 2048, tmp, KT, MEM)
        w_kv = A["w_mem_kv_2"][l]
        self.linear(w_kv, KT, lambda i, j: (2 * i + j) * P, 1, mn, self.to(lambda i, j: km[:, j, :]), n_cols=MEM)
        self.linear_tokens(w_kv, MEM_W, 1, mn, vm, rows=MEM)
        one = lambda a, i: a[:, ds(i, 1), :].rearrange("p a b -> p (a b)")
        self.attention(2, lambda i: one(qg, i), lambda i: one(km, i), lambda i, j: vm[:, j, ds(i * P, P)],
                       lambda i, iq: mix[:, ds(i + 6, 1), iq * P:(iq + 1) * P].rearrange("p a b -> p (a b)"),
                       self.HN, lambda iq: MEM)
        for j in range(2):
            c.on_dve(c.dve.tensor_tensor(mix[:, 6 + j, :], mix[:, 6 + j, :], qg[:, 2 + j, :], ALU.mult))
        c.join()
        mix = self.split(mix_at, tmp, mix_at, KT, S)
        self.linear(A["w_out_2"][l], KT, lambda i, j: (2 * i + j) * P, 4, mix,
                    self.to(lambda i, j: self.hn[:, ds(2 * i + j, 1), :].rearrange("p a b -> p (a b)")))
        self.add_normed(self.hn, self.vec["post_norm_2"][:, l * KT:(l + 1) * KT], tmp)

    def layer_b(self):
        c, sb, A, ps, do = self.c, self.sb, self.A, self.ps, self.do
        B = self.BIG
        w_in = A["b_w_in_2"].rearrange("l a b -> (l a) b")
        mix = sb.at(B, KT, S)
        k = sb.at(B + 8192, BT, S)
        v = sb.at(B + 14336, ST, BR)
        dist, strip = sb.at(B + 20480, S), sb.at(B + 21504, S)
        one = lambda a, i: a[:, ds(i, 1), :].rearrange("p a b -> p (a b)")
        self.keep_x()
        xs = self.norm_x(self.vec["pre_norm_2"][:, KT:2 * KT], B + 8192, B + 16384)
        self.linear(w_in, KT, lambda i, j: (2 * i + j) * P, 3, xs, self.to(lambda i, j: one(mix, 2 * i + j)))
        xs = self.norm_x(self.vec["kv_norm_2"], self.X, B + 8192)
        self.linear(A["w_kv_2"], KT, lambda i, j: (2 * i + j) * P, 3, xs, self.to(lambda i, j: one(k, 2 * i + j)))
        self.linear_tokens(A["w_kv_2"], BR, 3, xs, v)
        self.fetch_x()

        lam = [sb.at(B + 22528 + 64 * j, HD) for j in range(4)]
        e = [sb.at(B + 22528 + 256 + j, 1) for j in range(3)]
        for a, n in zip(lam, ("q1", "k1", "q2", "k2")):
            t = c.load(self.misc, a, A[f"b_lam_{n}_2"].rearrange("l a -> (l a)").partition_broadcast(P))
        for j in range(2):
            t2 = do(c.dve, [t], lambda: c.dve.tensor_tensor(lam[2 * j], lam[2 * j], lam[2 * j + 1], ALU.mult))
            t2 = do(c.dve, [t2], lambda: c.dve.tensor_reduce(e[j], lam[2 * j], AX.X, ALU.add))
            t2 = do(c.act, [t2], lambda: c.act.activation(e[j], e[j], ACT.Exp))
        t = do(c.dve, [t2], lambda: c.dve.tensor_tensor(e[2], e[1], e[0], ALU.subtract))
        do(c.dve, [t], lambda: c.dve.tensor_scalar(self.neglam, e[2], -LAM_INIT, None, ALU.add))
        t = do(c.pool, [c.now("dve")], lambda: c.pool.iota(dist, [[-1, S]], base=S - P, channel_multiplier=1,
                                                          allow_small_or_imprecise_dtypes=True))
        t = do(c.act, [t], lambda: c.act.activation(dist, dist, ACT.Abs))
        t = do(c.dve, [t], lambda: c.dve.tensor_scalar(dist, dist, -1.0, None, ALU.mult))
        do(c.dve, [t], lambda: c.dve.memset(dist[0:64, S - 64:S], NEG * 100))
        c.join()

        def strip_of(i):
            c.need(c.dve, "bias10", "bias11")
            self.t_strip = c.on_dve(c.dve.tensor_scalar(strip, dist, self.slopes[:, ds(i, 1)], None, ALU.mult))

        self.attention(BT, lambda i: one(mix, i), lambda i: one(k, i), lambda i, j: v[:, j, ds(i * P, P)],
                       lambda i, iq: mix[:, ds(i, 1), iq * P:(iq + 1) * P].rearrange("p a b -> p (a b)"),
                       self.HN, lambda iq: (iq + 1) * P,
                       bias=lambda h, iq: (strip[:, S - (iq + 1) * P:S], self.t_strip),
                       per_pair=strip_of, diff=True)

        sub = e[0]
        c.on_dve(c.dve.tensor_scalar(sub, self.vec["b_subln_2"], 1.0 - LAM_INIT, None, ALU.mult))
        sq, rs = sb.at(self.HN, S), sb.at(self.HN + S, S)
        both = ps[:, 0:2, :].rearrange("p a b -> p (a b)")
        c.join()
        with c.fori(BT) as i:
            for eng in (c.pe, c.act, c.dve):
                c.wait_before(eng, "end")
            t = do(c.act, [], lambda: c.act.activation(sq, one(mix, i), ACT.Square))
            c.wait(c.pe, t)
            for h in range(2):
                t = c.pe.matmul(ps[:, h, :], self.ones, sq[:, h * HALF:(h + 1) * HALF], start=True, stop=True)
            t = c.on_pe(t)
            t = do(c.act, [t], lambda: c.act.activation(rs, both, ACT.Ln, bias=self.eps, scale=1.0 / P))
            t = do(c.act, [t], lambda: c.act.activation(rs, rs, ACT.Exp, scale=-0.5))
            c.wait(c.dve, t)
            c.on_dve(c.dve.scalar_tensor_tensor(one(mix, i), one(mix, i), sub, rs, ALU.mult, ALU.mult), label="end")
        c.join()
        xs = self.norm_x(self.vec["pre_norm_2"][:, KT:2 * KT], B + 12288, B + 20480)
        self.finish_layer(1, w_in, BR, 2 * BR, xs, B, sb.at(B + 8192, 4, S), B + 12288, B + 20480)


_INS = [
    "x", "p", "g_mix_pre", "w_in", "b_forget", "g_attn_grp", "g_pool_grp", "w_pool", "pool_scale", "w_out",
    "g_mix_post", "g_ffn_pre", "w_ffn_gate", "w_ffn_up", "w_ffn_down", "g_ffn_post", "w_ple_proj", "g_ple",
    "w_ple_gate", "mem_2", "pre_norm_2", "post_norm_2", "w_out_2", "mem_norm_2", "w_mem_kv_2", "a_w_in_2",
    "a_shift_mu_2", "a_w0_2", "a_w2_2", "a_a0_2", "a_a2_2", "a_k_k_2", "a_k_a_2", "a_r_k_2", "a_lnx_w_2",
    "a_lnx_b_2", "kv_norm_2", "w_kv_2", "b_w_in_2", "b_lam_q1_2", "b_lam_k1_2", "b_lam_q2_2", "b_lam_k2_2",
    "b_subln_2",
]


def kernel(**inputs):
    import numpy as _np
    import concourse.bacc as _bacc
    from concourse import mybir as _mybir
    from concourse.bass_utils import run_bass_kernel_spmd as _run

    arrays = {f"in_{n}": _np.ascontiguousarray(inputs[n]) for n in _INS}
    known = {}
    for _ in range(2):
        nc = _bacc.Bacc("TRN2", target_bir_lowering=False, num_devices=1)
        A = {n: nc.dram_tensor(f"in_{n}", arrays[f"in_{n}"].shape, _mybir.dt.float32, kind="ExternalInput").ap()
             for n in _INS}
        out = nc.dram_tensor("out", (1, S, D), _mybir.dt.float32, kind="ExternalOutput").ap()
        build(nc, A, out, known)
    r = _run(nc, [arrays], core_ids=[0])
    return r.results[0]["out"]
```

```python
import math
from contextlib import ExitStack, contextmanager

import numpy as np
import concourse.bass as bass
import concourse.mybir as mybir

F32 = mybir.dt.float32
F32R = mybir.dt.float32r
ALU = mybir.AluOpType
ACT = mybir.ActivationFunctionType
AX = mybir.AxisListType
ds = bass.ds

P = 128
D = 1024
S = 1024
KT = D // P
ST = S // P
HALF = 512
EPS = 1e-6
NEG = -1.0e30

HD = 64
ATT_H = 8
ATT_W = ATT_H * HD
POOL_G = 4
FF = 2816
FT = FF // P
PLE = 256
MEM = 256
MEM_W = 256
BR = 768
BT = BR // P
LORA = 64
LNX_EPS = 64e-5
CH = 64
NCH = S // CH
LAM_INIT = 0.8 - 0.6 * math.exp(-0.3)
DECAY_C = math.exp(-0.5)


class Tick:

    def __init__(self, sem, loop, base, k):
        self.sem, self.loop, self.base, self.k = sem, loop, base, k


class Chip:

    def __init__(self, nc, ctx, known):
        self.nc, self.ctx, self.known = nc, ctx, known
        self.pe, self.act, self.dve, self.pool, self.sp = nc.tensor, nc.scalar, nc.vector, nc.gpsimd, nc.sync
        self.engines = {"pe": self.pe, "act": self.act, "dve": self.dve, "pool": self.pool}
        self.names = {id(e): n for n, e in (*self.engines.items(), ("sp", self.sp))}
        self.sems, self.count, self.seen = {}, {}, {}
        self.loop, self.n_loops = None, 0
        self.events = {}
        self.fresh = {}
        self.idle = ctx.enter_context(nc.semaphore("s_idle"))
        for n, e in self.engines.items():
            self.new_sem(n, e)

    def new_sem(self, name, engine=None):
        self.sems[name] = self.ctx.enter_context(self.nc.semaphore("s_" + name))
        start = max([v for k, v in self.known.items() if k[0] == "per" and k[2] == name], default=0)
        self.count[name] = start
        if start:
            engine = engine or self.sp
            engine.sem_inc(self.sems[name], start)
            engine.wait_ge(self.sems[name], start)
        return name

    def mark(self, name, instruction, by=1, label=None):
        instruction.then_inc(self.sems[name], by)
        self.count[name] += by
        if not self.loop:
            return Tick(name, None, self.count[name], 0)
        base = self.loop["base"].get(name, 0)
        if label:
            self.known["label", self.loop["id"], label] = (name, self.count[name] - base)
        return Tick(name, self.loop, base, self.count[name] - base)

    def on_pe(self, ins, label=None):
        return self.mark("pe", ins, label=label)

    def on_act(self, ins, label=None):
        return self.mark("act", ins, label=label)

    def on_dve(self, ins, label=None):
        return self.mark("dve", ins, label=label)

    def on_pool(self, ins, label=None):
        return self.mark("pool", ins, label=label)

    def load(self, sem, out, in_, label=None):
        self.settle(self.sp)
        return self.mark(sem, self.sp.dma_start(out, in_), 16, label)

    def wait(self, engine, *ticks):
        for t in ticks:
            if t is None:
                continue
            e = self.names[id(engine)]
            if t.loop is not None and t.loop is self.loop:
                self._wait_in_loop(engine, t.sem, t.k, t.base)
                continue
            value = t.base if t.loop is None else t.base + t.loop["per"][t.sem] * (t.loop["n"] - 1) + t.k
            if self.seen.get((e, t.sem, None), 0) < value:
                self.seen[e, t.sem, None] = value
                engine.wait_ge(self.sems[t.sem], value)

    def wait_before(self, engine, *labels):
        for label in labels:
            sem, k = self.known.get(("label", self.loop["id"], label), ("pe", 0))
            per = self.known.get(("per", self.loop["id"], sem), 4096)
            self._wait_in_loop(engine, sem, k - per, self.loop["base"].get(sem, 0))

    def _wait_in_loop(self, engine, sem, k, base):
        per = self.known.get(("per", self.loop["id"], sem), 4096)
        key = (self.names[id(engine)], sem, self.loop["id"])
        if self.seen.get(key, -1 << 40) < k:
            self.seen[key] = k
            engine.wait_ge(self.sems[sem], self.loop["i"] * per + max(base + k, 0))
            self.fresh[self.names[id(engine)]] = True
            if engine is self.sp:
                self.settle(engine)

    def settle(self, engine):
        if self.loop and self.fresh.pop(self.names[id(engine)], False):
            engine.sem_inc(self.idle, 1)

    @contextmanager
    def fori(self, n):
        assert self.loop is None
        self.n_loops += 1
        base = dict(self.count)
        with self.nc.Fori(0, n) as i:
            self.loop = dict(id=self.n_loops, i=i, base=base, n=n)
            yield i
        per = {s: self.count[s] - b for s, b in base.items()}
        for s, marks in per.items():
            self.known["per", self.n_loops, s] = marks
            self.count[s] = base[s] + n * marks
        self.loop["per"] = per
        for name, ticks in self.events.items():
            if any(t.loop is self.loop for t in ticks):
                self.known["event", self.n_loops, name] = [(t.sem, t.k) for t in ticks if t.loop is self.loop]
        self.loop = None

    def post(self, name, *ticks):
        self.events[name] = ticks

    def need(self, engine, *names):
        for name in names:
            ticks = self.events.get(name, ())
            self.wait(engine, *ticks)
            if self.loop and not any(t.loop is self.loop for t in ticks):
                for sem, k in self.known.get(("event", self.loop["id"], name), ()):
                    per = self.known.get(("per", self.loop["id"], sem), 4096)
                    self._wait_in_loop(engine, sem, k - per, self.loop["base"].get(sem, 0))

    def now_in(self, name):
        base = self.loop["base"].get(name, 0)
        return Tick(name, self.loop, base, self.count[name] - base)

    def now(self, name):
        assert self.loop is None
        return Tick(name, None, self.count[name], 0)

    def join(self, *engines):
        for e in engines or self.engines.values():
            self.wait(e, *(self.now(n) for n in self.engines))


class Rounded:

    def __init__(self, nc, base):
        self.nc, self.base, self.pieces = nc, base, {}

    def at(self, col, *shape):
        n = math.prod(shape)
        if (col, n) not in self.pieces:
            self.pieces[col, n] = self.nc.alloc_sbuf_tensor_at(f"r{col}_{n}", [P, n], F32R, offset=self.base + 4 * col)
        ap = self.pieces[col, n][:, :]
        return ap if len(shape) == 1 else ap.rearrange("p (a b) -> p a b", a=shape[0])


class Mem:

    def __init__(self, tile):
        self.tile = tile

    def at(self, col, *shape):
        n = math.prod(shape)
        ap = self.tile[:, col:col + n]
        if len(shape) == 1:
            return ap
        names = "abcd"[:len(shape)]
        sizes = {names[j]: shape[j] for j in range(1, len(shape))}
        return ap.rearrange(f"p ({' '.join(names)}) -> p {' '.join(names)}", **sizes)


def over_tokens(vec, n):
    return vec.unsqueeze(2).broadcast_to((P, vec.shape[1], n))


def over_pairs(mask, n=BT):
    return mask.unsqueeze(1).broadcast_to((mask.shape[0], n, mask.shape[1]))


VEC_ROWS = [
    ("g_mix_pre", 8), ("g_attn_grp", 4), ("g_pool_grp", 4), ("pool_scale", 4), ("g_mix_post", 8),
    ("g_ffn_pre", 8), ("g_ffn_post", 8), ("g_ple", 8), ("pre_norm_2", 16), ("post_norm_2", 16),
    ("mem_norm_2", 16), ("a_shift_mu_2", 19),
    ("a_w0_2", 6), ("a_a0_2", 6), ("a_k_k_2", 6), ("a_k_a_2", 6), ("a_r_k_2", 6),
    ("a_lnx_w_2", 6), ("a_lnx_b_2", 6), ("kv_norm_2", 8), ("b_subln_2", 1),
]


def build(nc, A, out, known, upto="all"):
    with ExitStack() as ctx:
        c = Chip(nc, ctx, known)
        k = Kernel(c, ctx, A, out)
        k.load_x()
        k.constants()
        k.turn_x()
        if upto != "b2":
            k.block_one()
        if upto != "b1":
            k.block_two()
        k.store()


class Kernel:
    X = 0
    HN = 8192
    W = 16384
    WSLOT = FT * P // 2
    CONST = W + 4 * (FT * P // 2)
    BIG = CONST + 3328

    def __init__(self, c, ctx, A, out):
        self.c, self.A, self.out = c, A, out
        nc = c.nc
        cols = 53200
        base = (nc.sbuf_base + 63) // 64 * 64
        self.sb = Mem(nc.alloc_sbuf_tensor_at("sb", [P, cols], F32, offset=base))
        self.sr = Rounded(nc, base)
        self.ps = ctx.enter_context(nc.psum_tensor("ps", [P, 8, HALF], F32))
        self.x = self.sb.at(self.X, KT, S)
        self.hn = self.sb.at(self.HN, KT, S)
        self.wsem = [c.new_sem(f"w{j}") for j in range(4)]
        self.io = [c.new_sem("io0"), c.new_sem("io1")]
        self.outsem = [c.new_sem(f"out{j}") for j in range(4)]
        self.misc, self.xio = c.new_sem("misc"), c.new_sem("xio")
        self.scratch_c = nc.dram_tensor("negc", [ATT_H, S], F32).ap()
        self.scratch_r = nc.dram_tensor("rs", [P, S], F32).ap()
        self.scratch_x = nc.dram_tensor("xs", [P, KT, S], F32).ap()
        self.x_kept = self.x_back = None
        col = self.CONST
        def const(*shape):
            nonlocal col
            ap = self.sb.at(col, *shape)
            col += math.prod(shape)
            return ap
        self.ident, self.ones, self.block64 = const(P), const(P), const(P)
        self.n_vec = sum(n for _, n in VEC_ROWS)
        self.vecs = const(self.n_vec)
        self.vec, at = {}, 0
        for name, n in VEC_ROWS:
            self.vec[name] = self.vecs[:, at:at + n]
            at += n
        self.eps, self.lnx_eps, self.stat = const(1), const(1), const(64)
        self.low = const(CH)
        self.up_col = col
        self.up, self.upi, self.eye = const(CH), const(CH), const(CH)
        self.level = [const(CH) for _ in range(6)]
        self.level0t = const(CH)
        self.slopes, self.neglam = const(BT), const(1)
        self.sel = const(BT, 12)
        self.selt = const(BR)
        assert col <= self.BIG, col - self.CONST


    def constants(self):
        c, sb, A = self.c, self.sb, self.A
        I32 = mybir.dt.int32

        def step(ins):
            c.wait(c.pool, c.on_pool(ins))
        pool, dve = c.pool, c.dve
        step(pool.memset(self.ident, 0.0))
        step(pool.memset(self.ones, 1.0))
        step(pool.memset(self.block64, 0.0))
        step(pool.memset(self.eps, EPS))
        step(pool.memset(self.lnx_eps, LNX_EPS))
        rows = sb.at(self.BIG, 2, P)
        step(pool.memset(rows, 0.0))
        step(pool.memset(self.sel, 0.0))
        step(pool.memset(self.selt, 0.0))
        for j in range(BT):
            slope = 2.0 ** (-2.0 * (j + 1)) if j < 4 else 2.0 ** (-1.0 - 2.0 * (j - 4))
            step(pool.memset(self.slopes[:, j:j + 1], slope))
        t = c.now("pool")
        c.wait(pool, t)
        for h in range(2):
            o = 64 * h
            step(pool.memset(self.block64[o:o + 64, o:o + 64], 1.0 / 64))
            for p in range(BT):
                step(pool.memset(self.sel[o:o + 64, p, 2 * p + h:2 * p + h + 1], 1.0))
        step(pool.affine_select(self.ident, self.ident, [[-1, P]], ALU.not_equal, 1.0, base=0,
                                     channel_multiplier=1))
        keep = sb.at(self.BIG + 512, BR)
        step(pool.memset(keep, 1.0))
        t = c.now("pool")
        c.wait(pool, t)
        step(pool.affine_select(keep[0:12], keep[0:12], [[1, BR]], ALU.is_ge, 0.0, base=0,
                                     channel_multiplier=-64))
        c.wait(pool, c.now("pool"))
        step(pool.affine_select(self.selt[0:12], keep[0:12], [[-1, BR]], ALU.is_ge, 0.0, base=63,
                                     channel_multiplier=64))
        ri, ci, xi = (sb.at(self.BIG + 2048 + CH * j, CH).bitcast(I32) for j in range(3))
        rf, cf = (sb.at(self.BIG + 2048 + CH * (3 + j), CH) for j in range(2))
        si = [sb.at(self.BIG + 2048 + CH * (5 + j), CH).bitcast(I32) for j in range(6)]
        sf = [sb.at(self.BIG + 2048 + CH * (11 + j), CH) for j in range(6)]
        for h in range(2):
            step(pool.iota(ri[64 * h:64 * h + 64], [[0, CH]], base=0, channel_multiplier=1))
        step(pool.iota(ci, [[1, CH]], base=0, channel_multiplier=0))
        c.wait(dve, c.now("pool"))
        c.on_dve(dve.tensor_copy(rf, ri))
        c.on_dve(dve.tensor_copy(cf, ci))
        c.on_dve(dve.tensor_tensor(xi, ri, ci, ALU.bitwise_xor))
        c.wait(dve, c.now("dve"))
        c.on_dve(dve.tensor_tensor(self.low, rf, cf, ALU.is_gt))
        c.on_dve(dve.tensor_tensor(self.up, cf, rf, ALU.is_gt))
        c.on_dve(dve.tensor_tensor(self.upi, cf, rf, ALU.is_ge))
        c.on_dve(dve.tensor_tensor(self.eye, cf, rf, ALU.is_equal))
        for j in range(6):
            c.on_dve(dve.tensor_scalar(si[j], xi, j, None, ALU.logical_shift_right))
        c.wait(dve, c.now("dve"))
        for j in range(6):
            c.on_dve(dve.tensor_copy(sf[j], si[j]))
        c.wait(dve, c.now("dve"))
        for j in range(6):
            c.on_dve(dve.scalar_tensor_tensor(self.level[j], sf[j], 1.0, self.low, ALU.is_equal, ALU.mult))
        c.on_dve(dve.scalar_tensor_tensor(self.level0t, sf[0], 1.0, self.up, ALU.is_equal, ALU.mult))
        c.wait(c.sp, c.now("pool"))
        at = 0
        for name, n in VEC_ROWS:
            v = A[name]
            flat = v if len(v.shape) == 1 else v.rearrange("a b -> (a b)") if len(v.shape) == 2 else v.rearrange("a b d -> (a b d)")
            v = flat.rearrange("(r p) -> r p", p=P)
            done = 0
            while done < n:
                m = min(n - done, P - at % P)
                t = c.load(self.misc, rows[at % P:at % P + m, at // P, :], v[done:done + m, :])
                at, done = at + m, done + m
        c.wait(c.pe, t, c.now("pool"))
        c.on_pe(c.pe.transpose(self.ps[:, 0, 0:P], rows[:, 0, :], self.ident))
        c.on_pe(c.pe.transpose(self.ps[:, 0, P:2 * P], rows[:, 1, :], self.ident))
        c.wait(dve, c.now("pe"))
        c.on_dve(dve.tensor_copy(self.vecs, self.ps[:, 0, 0:self.n_vec]))
        c.join()


    def load_rows(self, src, n_rows, n_cols, dst, at):
        c, kt = self.c, n_cols // P
        stage = [self.sb.at(at + j * n_cols, n_cols) for j in range(2)]
        c.wait(c.sp, *(c.now(n) for n in c.engines))
        with c.fori(n_rows // (2 * P)) as i:
            for j in range(2):
                c.wait_before(c.sp, f"turned{j}")
                t = c.load(self.io[j], stage[j], src[ds(i * 2 * P + j * P, P), :])
                c.wait(c.pe, t)
                c.wait_before(c.pe, *(f"copied{j}{b}" for b in range((kt + 3) // 4)))
                for f in range(kt):
                    t = c.pe.transpose(self.ps[:, 2 * j + f // 4, (f % 4) * P:(f % 4 + 1) * P],
                                       stage[j][:, f * P:(f + 1) * P], self.ident)
                t = c.on_pe(t, label=f"turned{j}")
                for b in range((kt + 3) // 4):
                    n = min(4, kt - 4 * b)
                    to = dst[:, 4 * b:4 * b + n, ds(i * 2 * P + j * P, P)]
                    fr = self.ps[:, 2 * j + b, 0:n * P].rearrange("p (a b) -> p a b", a=n)
                    if b == 0:
                        c.wait(c.dve, t)
                        c.on_dve(c.dve.tensor_copy(to, fr), label=f"copied{j}0")
                    else:
                        c.wait(c.act, t)
                        c.on_act(c.act.copy(to, fr), label=f"copied{j}1")
        c.join()

    def load_x(self):
        x = self.A["x"].rearrange("b s d -> (b s) d")
        sems = [*self.outsem, *self.io, self.wsem[2], self.wsem[3]]
        self.x_rows = [self.c.load(sems[s], self.sb.at(self.HN + s * D, D), x[s * P:(s + 1) * P, :]) for s in range(ST)]

    def turn_x(self):
        c, ps = self.c, self.ps
        copied = [(None, None)] * ST
        for s in range(ST):
            banks = 2 * (s % 4)
            c.wait(c.pe, self.x_rows[s], *(copied[s - 4] if s > 3 else ()))
            for f in range(KT):
                t = c.pe.transpose(ps[:, banks + f // 4, (f % 4) * P:(f % 4 + 1) * P],
                                   self.sb.at(self.HN + s * D + f * P, P), self.ident)
            t = c.on_pe(t)
            both = []
            for b, (e, on_e, cp) in enumerate(((c.act, c.on_act, c.act.copy), (c.dve, c.on_dve, c.dve.tensor_copy))):
                c.wait(e, t)
                both.append(on_e(cp(self.x[:, 4 * b:4 * b + 4, s * P:(s + 1) * P],
                                    ps[:, banks + b, :].rearrange("p (a b) -> p a b", a=4))))
            copied[s] = both
        c.join()


    def rstd(self, tiles, n, width, eps, out, tmp):
        c = self.c
        acc = self.sb.at(tmp, n)
        sq = [self.sb.at(tmp + n * (1 + j), n) for j in range(2)]
        c.wait(c.act, *(c.now(e) for e in c.engines))
        t = c.on_act(c.act.activation(acc, tiles[0], ACT.Square))
        added = [None, None]
        for j, tile in enumerate(tiles[1:]):
            c.wait(c.act, added[j % 2])
            s = c.on_act(c.act.activation(sq[j % 2], tile, ACT.Square))
            c.wait(c.dve, t, s)
            t = added[j % 2] = c.on_dve(c.dve.tensor_tensor(acc, acc, sq[j % 2], ALU.add))
        return self.rstd_of(acc, t, n, width, eps, out)

    def rstd_of(self, acc, summed, n, width, eps, out):
        c = self.c
        c.wait(c.pe, summed, *(c.now(e) for e in c.engines))
        for h in range(0, n, HALF):
            m = min(HALF, n - h)
            t = c.on_pe(c.pe.matmul(self.ps[:, h // HALF, 0:m], self.ones, acc[:, h:h + m], start=True, stop=True))
        c.wait(c.act, t)
        src = self.ps[:, 0:(n + HALF - 1) // HALF, :].rearrange("p a b -> p (a b)")[:, 0:n]
        c.wait(c.act, c.on_act(c.act.activation(out, src, ACT.Ln, bias=eps, scale=1.0 / width)))
        return c.on_act(c.act.activation(out, out, ACT.Exp, scale=-0.5))

    def scale_tiles(self, dst, src, gain, rstd):
        c = self.c
        c.wait(c.dve, *(c.now(e) for e in c.engines))
        for j in range(len(src)):
            c.on_dve(c.dve.scalar_tensor_tensor(dst[j], src[j], gain[:, j:j + 1], rstd, ALU.mult, ALU.mult))

    def norm_x(self, gain, hi, tmp, squares=None, again=False):
        c = self.c
        c.wait(c.act, self.x_back)
        c.wait(c.dve, self.x_back)
        r = self.sb.at(tmp, S)
        tiles = [self.x[:, j, :] for j in range(KT)]
        if again:
            c.wait(c.sp, self.r_kept, *(c.now(e) for e in c.engines))
            c.wait(c.dve, c.load(self.misc, r, self.scratch_r))
        else:
            if squares:
                t = self.rstd_of(squares[0], squares[1], S, D, self.eps, r)
            else:
                t = self.rstd(tiles, S, D, self.eps, r, tmp + S)
            c.wait(c.sp, t)
            self.r_kept = c.load(self.misc, self.scratch_r, r)
        c.wait(c.dve, *(c.now(e) for e in c.engines))
        if hi == self.X:
            c.wait(c.act, self.x_kept)
        return self.split(self.HN, hi, self.HN, KT, S, lambda j: c.on_dve(c.dve.scalar_tensor_tensor(
            self.hn[:, j, :], tiles[j], gain[:, j:j + 1], r, ALU.mult, ALU.mult)))

    def split(self, src, hi, lo, nk, n, make=None):
        c = self.c
        xs = self.sb.at(src, nk, n)
        rh, rl = ([self.sr.at(at + j * n, n) for j in range(nk)] for at in (hi, lo))
        ready, pending = [None] * nk, []
        if not make:
            for e in (c.act, c.dve, c.pool):
                c.wait(e, *(c.now(o) for o in c.engines))

        def low(j, t):
            e, on_e = (c.pool, c.on_pool) if j % 2 else (c.dve, c.on_dve)
            c.wait(e, t)
            ready[j] = (t, on_e(e.tensor_tensor(rl[j], xs[:, j, :], rh[j].bitcast(F32), ALU.subtract)))
        for j in range(nk):
            if make:
                c.wait(c.act, make(j))
            pending.append((j, c.on_act(c.act.copy(rh[j], xs[:, j, :]))))
            if j:
                low(*pending.pop(0))
        low(*pending.pop(0))
        return rh, rl, ready

    def add_normed(self, y, gain, tmp, squares=None, next_at=None):
        c = self.c
        r = self.sb.at(tmp, S)
        if squares is None:
            self.rstd([y[:, j, :] for j in range(KT)], S, D, self.eps, r, tmp + S)
        else:
            self.rstd_of(squares, None, S, D, self.eps, r)
        c.wait(c.dve, *(c.now(e) for e in c.engines))
        acc, *sq = (self.sb.at(next_at + j * S, S) for j in range(3)) if next_at else (None,)
        summed, pending = [None, None], []
        for j in range(KT + 1):
            if j < KT:
                t = c.on_dve(c.dve.scalar_tensor_tensor(y[:, j, :], y[:, j, :], gain[:, j:j + 1], r, ALU.mult, ALU.mult))
                e, on_e = (c.pool, c.on_pool) if (j not in (2, 5, 7) if next_at else j % 2) else (c.dve, c.on_dve)
                c.wait(e, t)
                t = on_e(e.tensor_tensor(self.x[:, j, :], self.x[:, j, :], y[:, j, :], ALU.add))
                if next_at:
                    c.wait(c.act, t, summed[j % 2])
                    pending.append((j, c.on_act(c.act.activation(sq[j % 2] if j else acc, self.x[:, j, :], ACT.Square))))
            if next_at and (j >= 2 or j == KT) and len(pending) > (j < KT):
                for q, t in pending[:len(pending) - (j < KT)]:
                    c.wait(c.dve, t, c.now("dve"))
                    if q:
                        summed[q % 2] = c.on_dve(c.dve.tensor_tensor(acc, acc, sq[q % 2], ALU.add))
                pending = pending[len(pending) - (j < KT):]
        return acc, summed[(KT - 1) % 2]

    def keep_x(self):
        c = self.c
        c.wait(c.sp, *(c.now(e) for e in c.engines))
        self.x_kept = c.load(self.xio, self.scratch_x, self.x)

    def fetch_x(self):
        c = self.c
        c.wait(c.sp, self.x_kept, *(c.now(e) for e in c.engines))
        self.x_back = c.load(self.xio, self.x, self.scratch_x)


    prefetched = False

    def prefetch(self, w, column, nk=KT):
        self.fetch(w, nk, column, 0)
        self.prefetched = True

    HI = FT * P // 2

    def fetch(self, w, nk, column, j, width=P):
        c = self.c
        at = self.W + 2 * j * self.HI
        raw, hi = self.sb.at(at, nk, P), self.sr.at(at + self.HI, nk, P).bitcast(F32)
        c.need(c.sp, f"wread{j}")
        if width < P:
            c.need(c.dve, f"wread{j}")
            c.wait(c.sp, c.on_dve(c.dve.memset(raw, 0.0)))
        t = c.load(self.wsem[j], raw[:, :, 0:width], w.rearrange("(k p) n -> p k n", p=P)[:, :, ds(column, width)])
        c.wait(c.act, t)
        th = c.on_act(c.act.copy(self.sr.at(at + self.HI, nk, P), raw))
        c.wait(c.dve, t, th)
        tl = c.on_dve(c.dve.tensor_tensor(self.sr.at(at, nk, P), raw, hi, ALU.subtract))
        c.post(f"wready{j}", th, tl)

    def product(self, bank, w, x, nk, ready=lambda q: ()):
        for q in range(nk):
            self.c.wait(self.c.pe, *ready(q))
            (wh, wl), (xh, xl) = w(q), x(q)
            for n, (a, b) in enumerate(((wh, xh), (wh, xl), (wl, xh))):
                t = self.c.pe.matmul(bank, a, b, start=(q == 0 and n == 0), stop=(q == nk - 1 and n == 2))
        return t

    def weight_tile(self, nk, i, j, x, evac, n_cols=S, width=P, banks=0):
        c = self.c
        at = self.W + 2 * j * self.HI
        lo, hi = self.sr.at(at, nk, P), self.sr.at(at + self.HI, nk, P)
        halves = (n_cols + HALF - 1) // HALF
        c.need(c.pe, f"wready{j}")
        for h in range(halves):
            m = min(HALF, n_cols - h * HALF)
            part = slice(h * HALF, h * HALF + m)
            bank = self.ps[:, banks + 2 * j + h, 0:m]
            c.need(c.pe, f"lbank{j}{h}")
            t = self.product(bank, lambda q: (hi[:, q, :], lo[:, q, :]), lambda q: (x[0][q][:, part], x[1][q][:, part]), nk,
                             lambda q: x[2][q])
            t = c.on_pe(t)
            if h == halves - 1:
                c.post(f"wread{j}", t)
            c.post(f"lbank{j}{h}", evac(i, j, h, bank[0:width], t))

    def linear(self, w, nk, column, n, x, evac, n_cols=S, then=None):
        c = self.c
        if not self.prefetched:
            self.fetch(w, nk, column(0, 0), 0)
        self.prefetched = False

        def pair(i, last):
            self.fetch(w, nk, column(i, 1), 1)
            self.weight_tile(nk, i, 0, x, evac, n_cols)
            if not last:
                self.fetch(w, nk, column(i + 1, 0), 0)
            elif then:
                then()
            self.weight_tile(nk, i, 1, x, evac, n_cols)
        if n > 1:
            pair(0, False)
        if n > 2:
            with c.fori(n - 2) as i:
                pair(i + 1, False)
        pair(n - 1, True)
        if not then:
            c.join()

    def linear_once(self, w, nk, col, width, x, evac, n_cols=S):
        if not self.prefetched:
            self.fetch(w, nk, col, 0, width)
        self.prefetched = False
        self.weight_tile(nk, 0, 0, x, lambda i, j, h, bank, t: evac(h, bank, t), n_cols, width)
        self.c.join()

    def linear_tokens(self, w, col, blocks, x, dst, rows=S):
        c = self.c
        width = 2 * P
        raw = self.sb.at(self.W, KT, width)
        rl, rh = ([self.sr.at(at + j * 2 * width, 2, width) for j in range(KT // 2)] for at in (self.W, self.W + KT * width))
        wv = w.rearrange("(k p) n -> p k n", p=P)
        c.wait(c.pe, *(c.now(e) for e in c.engines), *x[2][-1])
        c.need(c.sp, "wread0", "wread1")
        with c.fori(blocks) as i:
            c.need(c.sp, "vread")
            loaded = [c.load(self.wsem[q], raw[:, 2 * q:2 * q + 2, :], wv[:, 2 * q:2 * q + 2, ds(i * width + col, width)])
                      for q in range(KT // 2)]
            parts = []
            for q in range(KT // 2):
                two = raw[:, 2 * q:2 * q + 2, :]
                c.wait(c.act, loaded[q])
                t = c.on_act(c.act.copy(rh[q], two))
                c.wait(c.dve, t, loaded[q])
                parts.append(c.on_dve(c.dve.tensor_tensor(rl[q], two, rh[q].bitcast(F32), ALU.subtract)))
            for s in range(rows // P):
                bank = self.ps[:, s % 8, 0:width]
                c.need(c.pe, f"vbank{s}")
                for q in range(KT):
                    c.wait(c.pe, parts[q // 2])
                    for n, (a, b) in enumerate(((0, rh), (0, rl), (1, rh))):
                        t = c.pe.matmul(bank, x[a][q][:, s * P:(s + 1) * P], b[q // 2][:, q % 2, :],
                                        start=(q == 0 and n == 0), stop=(q == KT - 1 and n == 2))
                t = c.on_pe(t)
                c.post("vread", t)
                to = dst[:, s, ds(i * width, width)]
                e, on_e, cp = (c.dve, c.on_dve, c.dve.tensor_copy) if s % 2 else (c.act, c.on_act, c.act.copy)
                c.wait(e, t)
                c.settle(e)
                c.post(f"vbank{s}", on_e(cp(to, bank)))
        c.post("wread0", t)
        c.join()

    def to(self, dst):
        c = self.c

        def evac(i, j, h, bank, t):
            m = bank.shape[1]
            d = dst(i, j)[:, h * HALF:h * HALF + m]
            e, on_e, cp = (c.dve, c.on_dve, c.dve.tensor_copy) if h else (c.act, c.on_act, c.act.copy)
            c.wait(e, t)
            c.settle(e)
            return on_e(cp(d, bank))
        return evac

    def to_squared(self, dst, tmp):
        c = self.c
        acc, sq = self.sb.at(tmp, S), self.sb.at(tmp + S, S)
        c.wait(c.dve, *(c.now(e) for e in c.engines))
        t = c.on_dve(c.dve.memset(acc, 0.0))
        c.post("squared0", t)
        c.post("squared1", t)

        def evac(i, j, h, bank, t):
            part = slice(h * HALF, (h + 1) * HALF)
            c.wait(c.act, t)
            c.need(c.act, f"squared{h}")
            ts = c.on_act(c.act.activation(sq[:, part], bank, ACT.Square))
            c.settle(c.act)
            t = c.on_act(c.act.copy(dst(i, j)[:, part], bank))
            c.wait(c.dve, ts)
            c.need(c.dve, f"squared{h}")
            c.post(f"squared{h}", c.on_dve(c.dve.tensor_tensor(acc[:, part], acc[:, part], sq[:, part], ALU.add)))
            return t
        return evac, acc


    def attention(self, n, q, k, v, out, at, nkeys, bias=None, per_pair=None, diff=False):
        c, ps = self.c, self.ps
        qz = self.sb.at(at, 2, S)
        small = nkeys(ST - 1) <= HALF
        ahead, nb = (2, 8) if small else (1, 4)
        sc = self.sb.at(at + 2 * S, nb, 4 * S // nb)
        pt = self.sb.at(at + 6 * S, 2, HALF)
        on = self.sb.at(at + 7 * S, 2, P)
        c.on_dve(c.dve.memset(qz, 0.0))
        c.join()
        stat = lambda iq, h: self.stat[:, 4 * ((2 * iq + h) % 16):4 * ((2 * iq + h) % 16) + 4]
        with c.fori(n) as i:
            if per_pair:
                per_pair(i)
            c.need(c.dve, "scored")
            c.settle(c.dve)
            for h in range(2):
                o = slice(64 * h, 64 * h + 64)
                staged = c.on_dve(c.dve.tensor_scalar(qz[o, h, :], q(i)[o, :], 0.125, None, ALU.mult))
            src, maxed, exped, normed, group = {}, {}, {}, {}, [0]

            def scores(iq):
                nk = nkeys(iq)
                for h in range(2):
                    b0 = 2 * (iq % 2) + h if small else 2 * h
                    bank = ps[:, b0:b0 + (1 if small else 2), :].rearrange("p a b -> p (a b)")
                    c.wait(c.pe, staged)
                    c.need(c.pe, f"sbank{b0}")
                    for b in range(0, nk, HALF):
                        m = min(HALF, nk - b)
                        t = c.pe.matmul(bank[:, b:b + m], qz[:, h, iq * P:(iq + 1) * P], k(i)[:, b:b + m], start=True, stop=True)
                    t = c.on_pe(t)
                    c.post("scored", t)
                    buf, s4 = sc[:, (2 * iq + h) % nb, 0:nk], stat(iq, h)
                    c.wait(c.dve, t)
                    if bias:
                        add, ready = bias(h, iq)
                        c.wait(c.dve, ready)
                        c.need(c.dve, f"turned{(2 * iq + h) % nb}")
                        c.settle(c.dve)
                        t = c.on_dve(c.dve.tensor_tensor_reduce(buf, bank[:, 0:nk], add, 1.0, -3.0e38, ALU.add, ALU.max, s4[:, 0:1]))
                        c.post(f"sbank{b0}", t)
                        c.post(f"bias{h}{iq % 2}", t)
                        src[iq, h] = buf
                    else:
                        t = c.on_dve(c.dve.tensor_reduce(s4[:, 0:1], bank[:, 0:nk], AX.X, ALU.max))
                        src[iq, h] = bank[:, 0:nk]
                    c.wait(c.dve, t)
                    maxed[iq, h] = c.on_dve(c.dve.tensor_scalar(s4[:, 1:2], s4[:, 0:1], -1.0, None, ALU.mult))

            def exponentials(iq):
                for h in range(2):
                    s4, b = stat(iq, h), (2 * iq + h) % nb
                    c.wait(c.act, maxed[iq, h])
                    c.need(c.act, f"turned{b}")
                    exped[iq, h] = c.on_act(c.act.activation(sc[:, b, 0:nkeys(iq)], src[iq, h], ACT.Exp, bias=s4[:, 1:2],
                                                             accum_out=s4[:, 2:3]))
                    if not bias:
                        c.post(f"sbank{2 * (iq % 2) + h if small else 2 * h}", exped[iq, h])

            def normalise(iq):
                s0, s1 = stat(iq, 0), stat(iq, 1)
                for h, s in ((0, s0), (1, s1)):
                    c.wait(c.dve, exped[iq, h])
                    t = normed[iq] = c.on_dve(c.dve.reciprocal(s[:, 3:4], s[:, 2:3]))
                if diff:
                    a, b = (2 * iq) % nb, (2 * iq + 1) % nb
                    c.wait(c.dve, t)
                    t = c.on_dve(c.dve.scalar_tensor_tensor(s1[:, 0:1], s0[:, 2:3], self.neglam, s1[:, 3:4], ALU.mult, ALU.mult))
                    c.wait(c.dve, t)
                    w = nkeys(iq)
                    t = exped[iq, 0] = c.on_dve(c.dve.scalar_tensor_tensor(sc[:, a, 0:w], sc[:, b, 0:w], s1[:, 0:1],
                                                                           sc[:, a, 0:w], ALU.mult, ALU.add))
                    c.post(f"turned{b}", t)

            def values(iq):
                nj = nkeys(iq) // P
                ob = ps[:, 6 + iq % 2, :]
                c.need(c.pe, f"obank{iq % 2}")
                pending = []

                def flush(keep):
                    t = None
                    while len(pending) > keep:
                        b, h, g, m, t = pending.pop(0)
                        c.wait(c.pe, t)
                        o = slice(0, P) if diff else slice(64 * h, 64 * h + 64)
                        for j in range(m):
                            t = c.pe.matmul(ob[:, o], pt[:, b, j * P:(j + 1) * P], v(i, g + j)[:, o],
                                            start=(g + j == 0), stop=(g + j == nj - 1))
                        t = c.on_pe(t)
                        c.post(f"pt{b}", t)
                    return t
                for h in range(1 if diff else 2):
                    buf = (2 * iq + h) % nb
                    c.wait(c.pe, exped[iq, h])
                    for g in range(0, nj, 4):
                        m, b = min(4, nj - g), group[0] % 2
                        group[0] += 1
                        c.need(c.pe, f"ptbank{b}")
                        for j in range(m):
                            t = c.pe.transpose(ps[:, 4 + b, j * P:(j + 1) * P], sc[:, buf, (g + j) * P:(g + j + 1) * P], self.ident)
                        t = c.on_pe(t)
                        c.post(f"turned{buf}", t)
                        e, on_e, cp = (c.dve, c.on_dve, c.dve.tensor_copy) if b and not diff else (c.act, c.on_act, c.act.copy)
                        c.wait(e, t)
                        c.need(e, f"pt{b}")
                        t = on_e(cp(pt[:, b, 0:m * P], ps[:, 4 + b, 0:m * P]))
                        c.post(f"ptbank{b}", t)
                        pending.append((b, h, g, m, t))
                        flush(1)
                return flush(0)

            def scale(iq, multiplied):
                ob, o = ps[:, 6 + iq % 2, :], on[:, iq % 2, :]
                c.wait(c.dve, multiplied, normed[iq])
                c.need(c.dve, f"out{iq % 2}")
                for h in range(1 if diff else 2):
                    w = slice(0, P) if diff else slice(64 * h, 64 * h + 64)
                    t = c.on_dve(c.dve.tensor_scalar(o[:, w], ob[:, w], stat(iq, h)[:, 3:4], None, ALU.mult))
                return t

            def turn_out(iq, scaled):
                ob = ps[:, 6 + iq % 2, :]
                c.wait(c.pe, scaled)
                t = c.on_pe(c.pe.transpose(ob[:, P:2 * P], on[:, iq % 2, :], self.ident))
                c.post(f"out{iq % 2}", t)
                c.wait(c.act, t)
                c.settle(c.act)
                c.post(f"obank{iq % 2}", c.on_act(c.act.copy(out(i, iq), ob[:, P:2 * P])))

            for iq in range(ahead):
                scores(iq)
                exponentials(iq)
            multiplied = None
            for iq in range(ST):
                normalise(iq)
                if iq:
                    scaled = scale(iq - 1, multiplied)
                if iq + ahead < ST:
                    scores(iq + ahead)
                if iq:
                    turn_out(iq - 1, scaled)
                multiplied = values(iq)
                if iq + ahead < ST:
                    exponentials(iq + ahead)
            turn_out(ST - 1, scale(ST - 1, multiplied))
        c.join()


    def block_one(self):
        self.mixer()
        self.feed_forward()
        self.embedding_gate()

    def mixer(self):
        c, sb, A, ps = self.c, self.sb, self.A, self.ps
        B = self.BIG
        w_in, w_out = (A[n].rearrange("l a b -> (l a) b") for n in ("w_in", "w_out"))
        q, k = sb.at(B, 4, S), sb.at(B + 4096, 4, S)
        v = sb.at(B + 8192, ST, ATT_W)
        at = B + 12288
        LEAD = 16
        u = sb.at(at, POOL_G, LEAD + S)
        self.prefetch(w_in, 0)
        xs = self.norm_x(self.vec["g_mix_pre"], B + 17472, B)

        def qk(i, j):
            return sb.at(B, KT, S)[:, ds(2 * i + j, 1), :].rearrange("p a b -> p (a b)")
        u0 = 3 * ATT_W + ATT_H
        self.linear(w_in, KT, lambda i, j: (2 * i + j) * P, 4, xs, self.to(qk), then=lambda: self.prefetch(w_in, u0))
        c.on_pool(c.pool.memset(u[:, :, 0:LEAD], 0.0))
        self.linear(w_in, KT, lambda i, j: (2 * i + j) * P + u0, 2, xs,
                    self.to(lambda i, j: u[:, ds(2 * i + j, 1), LEAD:].rearrange("p a b -> p (a b)")))
        self.linear_tokens(w_in, 2 * ATT_W, 2, xs, v)

        fz, fa, fone = sb.at(at + 4160, S), sb.at(at + 5184, S), sb.at(at + 6208, S)
        bf = self.stat[0:ATT_H, 0:1]
        c.wait(c.sp, *(c.now(e) for e in c.engines))
        tb = c.load(self.misc, bf, A["b_forget"].rearrange("l h -> (l h)").rearrange("(h o) -> h o", o=1))
        c.wait(c.dve, tb)

        def forget(h, bank, t):
            c.wait(c.dve, t)
            return c.on_dve(c.dve.tensor_scalar(fz[0:ATT_H, h * HALF:(h + 1) * HALF], bank, bf, None, ALU.add))
        self.linear_once(w_in, KT, 3 * ATT_W, ATT_H, xs, forget)
        z, a, one = fz[0:ATT_H], fa[0:ATT_H], fone[0:ATT_H]
        c.on_dve(c.dve.memset(one, 1.0))
        c.wait(c.act, c.on_act(c.act.activation(a, z, ACT.Abs)))
        c.wait(c.act, c.on_act(c.act.activation(a, a, ACT.Exp, scale=-1.0)))
        t = c.on_act(c.act.activation(a, a, ACT.Ln, bias=self.ones[0:ATT_H, 0:1]))
        c.wait(c.dve, t)
        t = c.on_dve(c.dve.scalar_tensor_tensor(a, z, 0.0, a, ALU.min, ALU.subtract))
        c.wait(c.dve, t)
        t = c.on_dve(c.dve.tensor_tensor_scan(z, one, a, 0.0, ALU.mult, ALU.subtract))
        c.wait(c.sp, t)
        c.load(self.misc, self.scratch_c, z)

        mix = self.hn
        sums = [[sb.at(at + 7232 + (2 * a + b) * (LEAD + S), LEAD + S) for b in range(2)] for a in range(2)]
        inv = sb.at(at + 7232 + 4 * (LEAD + S), LEAD)
        pw = sb.at(self.W, POOL_G, P)
        c.need(c.sp, "wread0", "wread1")
        tw = c.load(self.wsem[0], pw, A["w_pool"].rearrange("l g a b -> (l g a) b").rearrange("(g a) b -> a g b", a=P))
        c.join()
        c.wait(c.dve, c.on_pool(c.pool.iota(inv, [[1, LEAD]], base=1, channel_multiplier=0,
                                            allow_small_or_imprecise_dtypes=True)))
        c.wait(c.dve, c.on_dve(c.dve.reciprocal(inv, inv)))
        for a in range(2):
            for b in range(2):
                c.wait(c.dve, c.on_dve(c.dve.memset(sums[a][b][:, 0:LEAD], 0.0)))
        pooled, copied = [None] * POOL_G, [None] * POOL_G
        for g in range(POOL_G):
            win, src = 2 << g, u[:, g, :]
            cur, bufs, step = src, list(sums[g % 2]), 1
            if g > 1:
                c.wait(c.dve, pooled[g - 2])
            while step < win:
                nxt = bufs[0]
                bufs.reverse()
                t = c.on_dve(c.dve.tensor_tensor(nxt[:, LEAD:], cur[:, LEAD:], cur[:, LEAD - step:LEAD + S - step], ALU.add))
                c.wait(c.dve, t)
                cur, step = nxt, step * 2
            first, rest = slice(LEAD, LEAD + win), slice(LEAD + win, LEAD + S)
            t = c.on_dve(c.dve.tensor_tensor(cur[:, first], cur[:, first], inv[:, 0:win], ALU.mult))
            c.wait(c.dve, t)
            c.on_dve(c.dve.tensor_tensor(cur[:, first], cur[:, first], src[:, first], ALU.subtract))
            t = c.on_dve(c.dve.scalar_tensor_tensor(cur[:, rest], cur[:, rest], 1.0 / win, src[:, rest], ALU.mult, ALU.subtract))
            c.wait(c.pe, t, tw, copied[g - 2] if g > 1 else None)
            for h in range(2):
                t = c.on_pe(c.pe.matmul(ps[:, 2 * (g % 2) + h, :], pw[:, g, :], cur[:, LEAD + h * HALF:LEAD + (h + 1) * HALF], start=True, stop=True))
            pooled[g] = t
            c.wait(c.act, t)
            copied[g] = c.on_act(c.act.activation(
                mix[:, 4 + g, :], ps[:, 2 * (g % 2):2 * (g % 2) + 2, :].rearrange("p a b -> p (a b)"), ACT.Copy,
                scale=self.vec["pool_scale"][:, g:g + 1]))
        c.join()
        c.post("wread0", c.now("pe"))

        cb, bb = sb.at(at + 7424 + 0, 2, S), sb.at(at + 7424 + 2 * S, 4, S)

        masked = c.pool.to_reg(NEG)

        def rows_of_pair(i):
            c.need(c.sp, "biased")
            self.tc = c.load(self.misc, cb, self.scratch_c[ds(2 * i, 2), :].partition_broadcast(P))

        def bias(h, iq):
            buf = bb[:, 2 * h + iq % 2, 0:(iq + 1) * P]
            c.wait(c.pool, self.tc)
            c.need(c.pool, f"bias{h}{iq % 2}")
            c.settle(c.pool)
            t = c.on_pool(c.pool.affine_select(buf, cb[:, h, 0:(iq + 1) * P], [[-1, (iq + 1) * P]], ALU.is_ge, masked,
                                               base=iq * P, channel_multiplier=1))
            c.post("biased", t)
            return buf, t
        c.wait(c.sp, *(c.now(e) for e in ("pe", "act", "dve", "pool", "misc")))
        self.attention(
            4, lambda i: q[:, ds(i, 1), :].rearrange("p a b -> p (a b)"),
            lambda i: k[:, ds(i, 1), :].rearrange("p a b -> p (a b)"),
            lambda i, j: v[:, j, ds(i * P, P)],
            lambda i, iq: mix[:, ds(i, 1), iq * P:(iq + 1) * P].rearrange("p a b -> p (a b)"),
            at, lambda iq: (iq + 1) * P, bias=bias, per_pair=rows_of_pair)

        gains, rs = (self.vec["g_attn_grp"], self.vec["g_pool_grp"]), [sb.at(B + j * S, S) for j in range(2)]
        for n in range(2):
            self.rstd([mix[:, 4 * n + j, :] for j in range(4)], S, ATT_W, self.eps, rs[n], B + (2 + 3 * n) * S)

        def normed(j):
            return c.on_dve(c.dve.scalar_tensor_tensor(mix[:, j, :], mix[:, j, :], gains[j // 4][:, j % 4:j % 4 + 1],
                                                       rs[j // 4], ALU.mult, ALU.mult))
        y = sb.at(B + 4096, KT, S)
        self.prefetch(w_out, 0)
        c.wait(c.dve, *(c.now(e) for e in c.engines))
        parts = self.split(self.HN, B + 12288, self.HN, KT, S, normed)
        evac, squares = self.to_squared(lambda i, j: y[:, ds(2 * i + j, 1), :].rearrange("p a b -> p (a b)"), B + 20480)
        self.linear(w_out, KT, lambda i, j: (2 * i + j) * P, 4, parts, evac)
        self.x_squares = self.add_normed(y, self.vec["g_mix_post"], B, squares, B + 12288)

    def feed_forward(self):
        c, sb, sr, A = self.c, self.sb, self.sr, self.A
        B = self.BIG
        y = sb.at(B + 8192, KT, S)
        down, down_hi = B + 16384, B + 18432
        g_hi, g_lo, g = B + 20480, B + 22528, sb.at(B + 24576, 2, S)
        w = [A[n].rearrange("l a b -> (l a) b") for n in ("w_ffn_gate", "w_ffn_up")]
        w_down = A["w_ffn_down"].rearrange("l a b -> (l a) b").rearrange("(k p) n -> p k n", p=P)
        self.fetch(w[0], KT, 0, 0)
        xs = self.norm_x(self.vec["g_ffn_pre"], B, B + 20480, self.x_squares)
        c.wait(c.pool, *(c.now(e) for e in c.engines))
        c.wait(c.dve, c.on_pool(c.pool.memset(y, 0.0)))

        def fetch_down(i):
            raw = sb.at(down, 2, D)
            c.need(c.sp, "down_read")
            t = c.load(self.wsem[2], raw, w_down[:, ds(2 * i, 2), :])
            c.wait(c.act, t)
            for q in range(2):
                hi = sr.at(down_hi + q * D, D)
                th = c.on_act(c.act.copy(hi, raw[:, q, :]))
                c.wait(c.dve, t, th)
                tl = c.on_dve(c.dve.tensor_tensor(sr.at(down + q * D, D), raw[:, q, :], hi.bitcast(F32), ALU.subtract))
            c.post("down_ready", th, tl)

        squares, sq = sb.at(B, S), [sb.at(B + (1 + j) * S, S) for j in range(2)]

        def down_part(last=False):
            added = [None, None]
            wh, wl, gh, gl = ([sr.at(col + q * S, S) for q in range(2)] for col in (down_hi, down, g_hi, g_lo))
            c.need(c.pe, "down_ready", "g0", "g1")
            for o in range(KT):
                for h in range(2):
                    b = 4 + (2 * o + h) % 4
                    out, tok = slice(o * P, (o + 1) * P), slice(h * HALF, (h + 1) * HALF)
                    c.need(c.pe, f"dbank{b}")
                    t = c.on_pe(self.product(self.ps[:, b, :], lambda q: (wh[q][:, out], wl[q][:, out]),
                                             lambda q: (gh[q][:, tok], gl[q][:, tok]), 2))
                    c.wait(c.dve, t)
                    t_y = c.on_dve(c.dve.tensor_tensor(y[:, o, tok], y[:, o, tok], self.ps[:, b, :], ALU.add))
                    c.post(f"dbank{b}", t_y)
                if last:
                    c.wait(c.act, t, t_y, added[o % 2])
                    t_s = c.on_act(c.act.activation(sq[o % 2] if o else squares, y[:, o, :], ACT.Square))
                    if o:
                        c.wait(c.dve, t_s, added[1 - o % 2])
                        added[o % 2] = c.on_dve(c.dve.tensor_tensor(squares, squares, sq[o % 2], ALU.add))
            c.post("down_read", t)

        def evac(n):
            gn = g[:, n, :]

            def of(i, j, h, bank, t):
                part = gn[:, h * HALF:(h + 1) * HALF]
                if j == 0:
                    c.need(c.act, f"g{n}")
                    c.wait(c.act, t)
                    self.silu[h] = c.on_act(c.act.activation(part, bank, ACT.Silu))
                    return self.silu[h]
                c.wait(c.dve, t, self.silu[h])
                free = t = c.on_dve(c.dve.tensor_tensor(part, part, bank, ALU.mult))
                if h == 1:
                    c.need(c.act, "down_read")
                    c.need(c.dve, "down_read")
                    c.wait(c.act, t)
                    hi = sr.at(g_hi + n * S, S)
                    th = c.on_act(c.act.copy(hi, gn))
                    c.wait(c.dve, th)
                    tl = c.on_dve(c.dve.tensor_tensor(sr.at(g_lo + n * S, S), gn, hi.bitcast(F32), ALU.subtract))
                    c.post(f"g{n}", th, tl)
                return free
            return of
        self.silu = {}

        def pair(i, first=False, last=False):
            for n in range(2):
                self.fetch(w[1], KT, (2 * i + n) * P, 1)
                self.weight_tile(KT, i, 0, xs, evac(n))
                if n == 0:
                    if not first:
                        down_part()
                    fetch_down(i)
                if not (n and last):
                    self.fetch(w[0], KT, (2 * i + n + 1) * P, 0)
                self.weight_tile(KT, i, 1, xs, evac(n))
        pair(0, first=True)
        with c.fori(FT // 2 - 2) as i:
            pair(i + 1)
        pair(FT // 2 - 1, last=True)
        down_part(last=True)
        c.join()
        self.add_normed(y, self.vec["g_ffn_post"], B + 4096, squares)
        c.join()

    def embedding_gate(self):
        c, sb, A = self.c, self.sb, self.A
        B = self.BIG
        pT = sb.at(B, PLE // P, S)
        self.load_rows(A["p"].rearrange("l b s d -> (l b s) d"), S, PLE, pT, B + 2 * S)
        e = self.hn
        w_gate = A["w_ple_gate"].rearrange("l a b -> (l a) b")
        pT = self.split(B, B + 2 * S, B, PLE // P, S)
        evac, squares = self.to_squared(lambda i, j: e[:, ds(2 * i + j, 1), :].rearrange("p a b -> p (a b)"), B + 4096)
        self.linear(A["w_ple_proj"].rearrange("l a b -> (l a) b"), PLE // P, lambda i, j: (2 * i + j) * P, 4, pT, evac)
        r = sb.at(B, S)
        tiles = [e[:, j, :] for j in range(KT)]
        self.rstd_of(squares, None, S, D, self.eps, r)
        self.prefetch(w_gate, 0)
        xs = self.split(self.X, B + 10240, B + 18432, KT, S)
        self.scale_tiles(tiles, tiles, self.vec["g_ple"], r)
        c.wait(c.dve, c.now("dve"))
        s = sb.at(B + S, 4, HALF)

        def gate(i, j, h, bank, t):
            b = s[:, 2 * j + h, :]
            c.wait(c.act, t)
            c.need(c.act, f"gated{j}{h}")
            t = free = c.on_act(c.act.activation(b, bank, ACT.Sigmoid))
            c.wait(c.dve, t)
            part = slice(h * HALF, (h + 1) * HALF)
            t = c.on_dve(c.dve.tensor_tensor(b, b, e[:, ds(2 * i + j, 1), part].rearrange("p a b -> p (a b)"), ALU.mult))
            c.wait(c.dve, t)
            x = self.x[:, ds(2 * i + j, 1), part].rearrange("p a b -> p (a b)")
            c.post(f"gated{j}{h}", c.on_dve(c.dve.tensor_tensor(x, x, b, ALU.add)))
            return free
        self.linear(w_gate, KT, lambda i, j: (2 * i + j) * P, 4, xs, gate)

    def store(self):
        c, ps = self.c, self.ps
        o = self.out.rearrange("b s d -> (b s) d")
        row = self.sb.at(self.BIG, 4, D)
        stored = [None] * ST
        copied = [None] * ST
        c.join()
        for s in range(ST):
            banks = 2 * (s % 4)
            if s > 3:
                c.wait(c.pe, *copied[s - 4])
            for f in range(KT):
                t = c.pe.transpose(ps[:, banks + f // 4, (f % 4) * P:(f % 4 + 1) * P], self.x[:, f, s * P:(s + 1) * P], self.ident)
            t = c.on_pe(t)
            for e in (c.act, c.dve):
                c.wait(e, t, stored[s - 4] if s > 3 else None)
            copied[s] = (c.on_act(c.act.copy(row[:, s % 4, 0:HALF], ps[:, banks, :])),
                         c.on_dve(c.dve.tensor_copy(row[:, s % 4, HALF:D], ps[:, banks + 1, :])))
            c.wait(c.sp, *copied[s])
            stored[s] = c.load(self.outsem[s % 4], o[s * P:(s + 1) * P, :], row[:, s % 4, :])
        c.wait(c.sp, *stored[-4:])


    def block_two(self):
        self.memory()
        self.layer_a()
        self.layer_b()

    def memory(self):
        c, sb = self.c, self.sb
        B = self.BIG
        self.mhat = sb.at(B + 25600, KT, MEM)
        self.load_rows(self.A["mem_2"].rearrange("b m d -> (b m) d"), MEM, D, self.mhat, B)
        r = sb.at(B, MEM)
        tiles = [self.mhat[:, j, :] for j in range(KT)]
        c.wait(c.dve, self.rstd(tiles, MEM, D, self.eps, r, B + MEM))
        for t in tiles:
            c.on_dve(c.dve.tensor_tensor(t, t, r, ALU.mult))
        c.join()

    def do(self, engine, deps, make):
        c = self.c
        c.wait(engine, *deps)
        return c.mark(c.names[id(engine)], make())

    def layer_a(self):
        c, sb, A, ps = self.c, self.sb, self.A, self.ps
        B = self.BIG
        w_in = A["a_w_in_2"].rearrange("l a b -> (l a) b")
        mix = sb.at(B, KT, S)
        rkv = sb.at(B, 3 * BT, S)
        lora = sb.at(B + 18432, S)
        rs12 = sb.at(B + 19456, S)
        w2, a2 = sb.at(B + 20480, BR), sb.at(B + 20480 + BR, BR)
        zt = [sb.at(B + 22016 + j * (S + 1), S + 1) for j in range(2)]
        dz = sb.at(B + 22016 + 2 * (S + 1), S)
        reset = sb.at(B + 22016, BT, CH)
        mu = self.vec["a_shift_mu_2"]
        self.prefetch(w_in, 0)
        self.keep_x()
        xs = self.norm_x(self.vec["pre_norm_2"][:, 0:KT], self.X, B)
        for j in range(2):
            c.on_dve(c.dve.memset(zt[j][:, 0:1], 0.0))
        c.on_dve(c.dve.memset(w2, 0.0))
        c.on_dve(c.dve.memset(a2, 0.0))
        c.wait(c.sp, c.now("dve"))
        tl = c.load(self.misc, w2[0:LORA, :], A["a_w2_2"].rearrange("l a b -> (l a) b"))
        tl = c.load(self.misc, a2[LORA:P, :], A["a_a2_2"].rearrange("l a b -> (l a) b"))
        c.join()

        def shifted(dst, j, col):
            t = self.do(c.dve, [self.copied[0], self.copied[1]],
                        lambda: c.dve.tensor_tensor(dz, zt[j][:, 0:S], zt[j][:, 1:S + 1], ALU.subtract))
            c.wait(c.dve, t)
            return c.dve.scalar_tensor_tensor(dst, dz, mu[:, col], zt[j][:, 1:S + 1], ALU.mult, ALU.add)

        self.copied = {}

        def evac(i, j, h, bank, t):
            e, on_e, cp = ((c.act, c.on_act, c.act.copy), (c.dve, c.on_dve, c.dve.tensor_copy))[h]
            c.wait(e, t)
            c.need(e, f"shifted{j}")
            free = self.copied[h] = on_e(cp(zt[j][:, 1 + h * HALF:1 + (h + 1) * HALF], bank))
            if h == 1:
                c.need(c.dve, f"shifted{1 - j}")
                ins = shifted(rkv[:, ds(2 * i + j, 1), :].rearrange("p a b -> p (a b)"), j, ds(2 * i + j, 1))
                c.post(f"shifted{j}", c.on_dve(ins))
            return free
        self.linear(w_in, KT, lambda i, j: (2 * i + j) * P, 9, xs, evac, then=lambda: self.prefetch(w_in, 3 * BR))

        def evac_lora(h, bank, t):
            c.need(c.act, "shifted0")
            self.copied[h] = self.do(c.act, [t], lambda: c.act.copy(zt[0][:, 1 + h * HALF:1 + (h + 1) * HALF], bank))
            if h == 1:
                c.need(c.dve, "shifted0", "shifted1")
                t = c.on_dve(shifted(lora, 0, slice(18, 19)))
                self.do(c.act, [t], lambda: c.act.activation(lora[0:LORA, :], lora[0:LORA, :], ACT.Tanh))
            return self.copied[h]
        self.linear_once(w_in, KT, 3 * BR, P, xs, evac_lora)

        sq = [zt[0][:, 0:S], zt[1][:, 0:S]]
        read = [None, None]
        for p in range(BT):
            c.wait(c.act, read[p % 2])
            t = c.on_act(c.act.activation(sq[p % 2], rkv[:, BT + p, :], ACT.Square, scale=self.vec["a_k_k_2"][:, p:p + 1]))
            c.wait(c.pe, t)
            for h in range(2):
                t = c.pe.matmul(ps[0:12, h, :], self.sel[:, p, :], sq[p % 2][:, h * HALF:(h + 1) * HALF],
                                start=(p == 0), stop=(p == BT - 1))
            read[p % 2] = c.on_pe(t)
        n2 = rs12[0:12, :]
        t = self.do(c.dve, [read[1]], lambda: c.dve.tensor_scalar(
            n2, ps[0:12, 0:2, :].rearrange("p a b -> p (a b)"), 1e-12, None, ALU.max))
        t = self.do(c.act, [t], lambda: c.act.activation(n2, n2, ACT.Ln))
        self.do(c.act, [t], lambda: c.act.activation(n2, n2, ACT.Exp, scale=-0.5))
        c.join()
        c.on_dve(c.dve.memset(reset, 1.0))
        c.wait(c.dve, c.now("dve"))
        c.on_dve(c.dve.memset(reset[:, :, 0:1], 0.0))
        c.wait(c.dve, tl)
        c.join()
        self.rwkv(rkv, lora, rs12, w2, a2, reset, (B + 22016 + BR // 2, B + 25600))
        self.fetch_x()
        self.rwkv_norm(mix, rkv)

        gate0 = 3 * BR + 2 * LORA
        self.prefetch(w_in, gate0)
        xs = self.norm_x(self.vec["pre_norm_2"][:, 0:KT], B + 12288, B + 20480, again=True)
        self.finish_layer(0, w_in, gate0, gate0 + BR, xs, B, sb.at(B + 8192, 4, S), B + 12288, B + 20480)

    def rwkv(self, rkv, lora, rs12, w2, a2, reset, spare):
        c, sb, ps = self.c, self.sb, self.ps
        pe, act, dve, pool, do = c.pe, c.act, c.dve, c.pool, self.do
        F16 = mybir.dt.float16
        rooms = [[self.HN, self.CONST], list(spare)]

        def buf(*shape, dtype=F32):
            shape = shape or (BT, CH)
            n = math.prod(shape)
            cols = n if dtype == F32 else n // 2
            room = next(r for r in rooms if r[0] + cols <= r[1])
            flat_ = sb.at(room[0], cols)
            room[0] += cols
            flat_ = flat_ if dtype == F32 else flat_.bitcast(dtype)
            return flat_.rearrange("p (a b) -> p a b", a=shape[0]) if len(shape) == 2 else \
                flat_.rearrange("p (a b c) -> p a b c", a=shape[0], b=shape[1])
        kkn = sb.at(self.X, BT, S)
        tw, ta = (sb.at(self.X + BT * (S + 2 * CH * j), BT, 2 * CH) for j in range(2))
        ld, run, pinv = buf(), buf(), buf()
        pc = buf(BT, CH + 1)
        kp, nb, rk = (buf() for _ in range(3))
        ar_e, bb, kb, vc = buf(BT, 2, CH), buf(), buf(), buf()
        ar, lr, ak = ([buf(*sh) for _ in range(2)] for sh in ((BT, 2, CH), (BT, 2 * CH), (BT, 2 * CH)))
        vt, kt, bt, xt = ([buf() for _ in range(2)] for _ in range(4))
        pt = [buf(BT, 1) for _ in range(2)]
        low, z, zi = buf(), buf(), buf()
        x16, xt16, w16, l16 = (buf(BT, CH, dtype=F16) for _ in range(4))
        r16 = w16
        rhs, g, st = buf(), buf(), buf()
        V = self.vec
        k_a, r_k = (over_tokens(V[n], CH) for n in ("a_k_a_2", "a_r_k_2"))
        m3 = over_pairs(sb.at(self.up_col, 2 * CH), 3)
        flat = lambda a: a.rearrange("p a b -> p (a b)")
        of = lambda a: (lambda p: a[:, p, :])

        def bank(b, n=BT, w=CH):
            return ps[:, b, 0:n * w].rearrange("p (a b) -> p a b", a=n)

        def free(b, *ticks):
            c.post(f"bank{b}", *ticks)

        def heads(out, pairs):
            c.settle(pe)
            for p in range(BT):
                for n, (lhsT, rhs_) in enumerate(pairs):
                    for h in range(2):
                        o = slice(64 * h, 64 * h + 64)
                        t = pe.matmul(out(p)[o], lhsT(p)[o], rhs_(p)[o], start=(n == 0), stop=(n == len(pairs) - 1),
                                      skip_group_check=True)
            return c.on_pe(t)

        def low_rank(m):
            for dst, weights, bias, name in ((tw, w2, V["a_w0_2"], "tw"), (ta, a2, V["a_a0_2"], "ta")):
                ticks = []
                for half, b in ((0, 7), (1, 0 if dst is tw else 1)):
                    pairs = slice(3 * half, 3 * half + 3)
                    c.need(pe, f"bank{b}")
                    for p in range(3):
                        q = 3 * half + p
                        t = pe.matmul(bank(b, 3, 2 * CH)[:, p, :], weights[:, q * P:(q + 1) * P],
                                      lora[:, ds(m * CH, 2 * CH)], start=True, stop=True)
                    t = c.on_pe(t)
                    c.need(dve, name + "_read")
                    t = do(dve, [t], lambda: dve.tensor_tensor(dst[:, pairs], bank(b, 3, 2 * CH),
                                                               over_tokens(bias[:, pairs], 2 * CH), ALU.add))
                    free(b, t)
                    t = do(act, [t], lambda: act.activation(dst[:, pairs], dst[:, pairs], ACT.Tanh, scale=0.5))
                    if dst is ta:
                        t = do(dve, [t], lambda: dve.tensor_scalar(ta[:, pairs], ta[:, pairs], 0.5, 0.5, ALU.mult, ALU.add))
                    ticks.append(t)
                    c.post(name, *ticks)
                    yield

        def elementwise(m, s):
            tok, of_pair = ds(m * CH, CH), slice(s * CH, (s + 1) * CH)
            rC, kC, vC = (rkv[:, n * BT:(n + 1) * BT, tok] for n in range(3))
            kk, rate = kkn[:, :, tok], ta[:, :, of_pair]
            c.need(pool, "e_read", "e_bonus")
            c.settle(pool)
            t_vc = do(pool, [], lambda: pool.tensor_copy(vc, vC))
            c.need(dve, "e_read", "e_bonus", "e_pool", "tw")
            t = do(dve, [], lambda: dve.tensor_scalar(ld, tw[:, :, of_pair], -0.5 * DECAY_C, -0.5 * DECAY_C, ALU.mult, ALU.add))
            c.post("tw_read", t)
            t_run = do(dve, [t], lambda: dve.tensor_tensor_scan(flat(run), flat(reset), flat(ld), 0.0, ALU.mult, ALU.add))
            t_pc = do(act, [t_run], lambda: act.activation(pc[:, :, 1:CH + 1], run, ACT.Exp))
            t_pi = do(act, [], lambda: act.activation(pinv, run, ACT.Exp, scale=-1.0))
            yield
            c.need(dve, "ta")
            t = do(dve, [], lambda: dve.scalar_tensor_tensor(kp, rate, -1.0, k_a, ALU.add, ALU.mult))
            t_kp = do(dve, [t], lambda: dve.scalar_tensor_tensor(kp, kp, 1.0, kC, ALU.add, ALU.mult))
            t = do(pool, [t_kp], lambda: pool.tensor_tensor(rk, rC, kp, ALU.mult))
            t_rk = do(pool, [t], lambda: pool.tensor_tensor(rk, rk, r_k, ALU.mult))
            t_nb = do(dve, [], lambda: dve.scalar_tensor_tensor(nb, kk, -1.0, rate, ALU.mult, ALU.mult))
            c.post("ta_read", t_nb)
            yield
            do(dve, [t_pc], lambda: dve.tensor_tensor(ar_e[:, :, 0, :], kk, pc[:, :, 0:CH], ALU.mult))
            t_ar = do(dve, [], lambda: dve.tensor_tensor(ar_e[:, :, 1, :], rC, pc[:, :, 1:CH + 1], ALU.mult))
            t_b = do(dve, [t_pi, t_nb], lambda: dve.tensor_tensor(bb, nb, pinv, ALU.mult))
            t_k = do(pool, [t_pi], lambda: pool.tensor_tensor(kb, kp, pinv, ALU.mult))
            c.post("e_out", t_ar, t_b, t_k, t_vc, t_pc)
            c.post("e_pool", t_k)
            yield
            c.need(pe, "bank7")
            c.wait(pe, t_rk)
            c.settle(pe)
            t = c.on_pe(pe.matmul(bank(7), self.block64, flat(rk), start=True, stop=True))
            t = do(dve, [t, t_vc], lambda: dve.scalar_tensor_tensor(vC, bank(7), 64.0, vc, ALU.mult, ALU.mult))
            free(7, t)
            c.post("e_bonus", t)
            yield

        def products(s):
            c.need(pe, "e_out", "bank0", "bank1")
            arf = ar_e.rearrange("p a b c -> p a (b c)")
            three = lambda b: (lambda p: bank(b + p // 3, 3, 2 * CH)[:, p % 3, :])
            t_lr = heads(three(0), [(of(bb), of(arf))])
            c.need(dve, f"state{s}", "inv")
            do(dve, [t_lr], lambda: dve.tensor_tensor(lr[s][:, 0:3, :], bank(0, 3, 2 * CH), m3, ALU.mult))
            t_lrs = do(dve, [], lambda: dve.tensor_tensor(lr[s][:, 3:6, :], bank(1, 3, 2 * CH), m3, ALU.mult))
            free(0, t_lrs)
            free(1, t_lrs)
            c.need(pool, "e_out", f"state{s}")
            c.settle(pool)
            t1 = do(pool, [], lambda: pool.tensor_copy(ar[s], ar_e))
            t2 = do(pool, [], lambda: pool.tensor_copy(pt[s], pc[:, :, CH:CH + 1]))
            c.post(f"ar{s}", t1, t2)
            c.need(pe, "bank4")
            t_x = heads(of(bank(4)), [(lambda p: ar_e[:, p, 0, :], of(bb))])
            c.need(act, "inv", f"state{s}")
            t_l16 = do(act, [t_lrs], lambda: act.copy(l16, lr[s][:, :, 0:CH]))
            t_low = do(dve, [t_x], lambda: dve.tensor_tensor(low, bank(4), over_pairs(self.low), ALU.mult))
            free(4, t_low)
            c.need(pool, "inv")
            t = do(pool, [t_lrs], lambda: pool.tensor_tensor(zi, lr[s][:, :, 0:CH], over_pairs(self.level0t), ALU.mult))
            t_xt = do(pool, [t], lambda: pool.tensor_tensor(xt16, zi, over_pairs(self.eye), ALU.add))
            t = do(dve, [t_low], lambda: dve.tensor_tensor(z, low, over_pairs(self.level[0]), ALU.mult))
            t_x = do(dve, [t], lambda: dve.tensor_tensor(x16, z, over_pairs(self.eye), ALU.add))
            c.post("inv_in", t_l16, t_x)
            c.post("inv_xt", t_xt)
            c.need(pe, "bank2", "bank3")
            t_ak = heads(three(2), [(of(kb), of(arf))])
            do(dve, [t_ak], lambda: dve.tensor_tensor(ak[s][:, 0:3, :], bank(2, 3, 2 * CH), m3, ALU.mult))
            t_aks = do(dve, [], lambda: dve.tensor_tensor(ak[s][:, 3:6, :], bank(3, 3, 2 * CH), m3, ALU.mult))
            free(2, t_aks)
            free(3, t_aks)
            yield
            for n, (dst, src) in enumerate(((vt[s], vc), (kt[s], kb), (bt[s], bb))):
                c.need(pe, "bank7")
                t_pe = heads(of(bank(7)), [(of(src), lambda p: self.eye)])
                t = do(act, [t_pe], lambda: act.copy(dst, bank(7)))
                free(7, t)
                if n == 2:
                    c.post("e_read", t_pe, t1, t2)
                    c.post(f"tri{s}", t_aks, t_lrs, t)
                yield

        def inverse(s):
            c.need(pe, "inv_in")
            t_x = t_xt = None
            for lev in range(1, 6):
                c.need(pe, "bank4")
                c.wait(pe, t_x)
                t = heads(of(bank(4)), [(of(l16), of(x16))])
                t_w = do(dve, [t], lambda: dve.tensor_tensor(w16, bank(4), over_pairs(self.level[lev]), ALU.mult))
                free(4, t_w)
                yield
                c.need(pe, "bank5", "bank6")
                c.wait(pe, t_w, t_xt)
                c.need(pe, "inv_xt")
                t1 = heads(of(bank(5)), [(of(xt16), of(w16))])
                t2 = heads(of(bank(6)), [(of(w16), of(xt16))])
                t_x = do(dve, [t1], lambda: dve.tensor_tensor(x16, x16, bank(5), ALU.add))
                free(5, t_x)
                t_xt = do(dve, [t2], lambda: dve.tensor_tensor(xt16, xt16, bank(6), ALU.add))
                free(6, t_xt)
                yield
            t_z = do(act, [t_xt], lambda: act.copy(z, xt16))
            t_zi = do(pool, [t_xt], lambda: pool.tensor_tensor(zi, xt16, over_pairs(self.eye), ALU.subtract))
            c.need(pe, "bank4")
            c.wait(pe, t_z)
            t = heads(of(bank(4)), [(of(low), of(z))])
            t = do(dve, [t, t_zi], lambda: dve.tensor_tensor(r16, bank(4), zi, ALU.subtract))
            free(4, t)
            yield
            c.need(pe, "bank5")
            c.wait(pe, t)
            t = heads(of(bank(5)), [(of(x16), of(r16))])
            c.need(dve, f"state{s}")
            t = do(dve, [t], lambda: dve.tensor_tensor(xt[s], z, bank(5), ALU.add))
            free(5, t)
            c.post(f"xt{s}", t)
            c.post("inv", t)
            yield

        def state_step(m, s):
            c.need(pe, f"tri{s}", f"ar{s}", "st", "bank0")
            t = heads(of(bank(0)), [(lambda p: ar[s][:, p, 0, :], of(st)), (lambda p: ak[s][:, p, 0:CH], of(vt[s]))])
            t = do(act, [t], lambda: act.copy(rhs, bank(0)))
            free(0, t)
            yield
            c.need(pe, f"xt{s}", "bank1")
            c.wait(pe, t)
            t = heads(of(bank(1)), [(of(xt[s]), of(rhs))])
            t = do(act, [t], lambda: act.copy(g, bank(1)))
            free(1, t)
            yield
            c.need(pe, "bank2", "bank3")
            c.wait(pe, t)
            t_s = heads(of(bank(2)), [(of(kt[s]), of(vt[s])), (of(bt[s]), of(g))])
            yield
            t_y = heads(of(bank(3)), [(of(st), lambda p: ar[s][:, p, 1, :]), (of(vt[s]), lambda p: ak[s][:, p, CH:2 * CH]),
                                      (of(g), lambda p: lr[s][:, p, CH:2 * CH])])
            c.wait(act, t_y)
            c.settle(act)
            t = c.on_act(act.copy(rkv[:, 0:BT, ds(m * CH, CH)], bank(3)))
            free(3, t)
            t = do(dve, [t_s, t_y], lambda: dve.tensor_tensor(st, st, bank(2), ALU.add))
            free(2, t)
            t = do(dve, [t], lambda: dve.tensor_tensor(st, st, pt[s].broadcast_to((P, BT, CH)), ALU.mult))
            c.post("st", t)
            c.post(f"state{s}", t_y, t)
            yield

        def emit(order, **parts):
            for letter in order.replace(" ", ""):
                next(parts[letter], None)
            for part in parts.values():
                for _ in part:
                    pass

        used = [None] * 4
        for p in range(BT):
            banks = 2 * (p % 4)
            c.wait(pe, used[p % 4])
            for h in range(2):
                t = pe.matmul(ps[:, banks + h, :], self.selt[0:12, p * P:(p + 1) * P],
                              rs12[0:12, h * HALF:(h + 1) * HALF], start=True, stop=True)
            t = c.on_pe(t)
            used[p % 4] = do(dve, [t], lambda: dve.scalar_tensor_tensor(
                kkn[:, p, :], rkv[:, BT + p, :], V["a_k_k_2"][:, p:p + 1],
                ps[:, banks:banks + 2, :].rearrange("p a b -> p (a b)"), ALU.mult, ALU.mult))
        c.on_dve(dve.memset(pc, 1.0))
        c.on_dve(dve.memset(st, 0.0))
        c.join()
        emit("", L=low_rank(0), E=elementwise(0, 0))
        emit("", P=products(0), I=inverse(0), E=elementwise(1, 1))

        def step(m, j, last=False):
            parts = dict(P=products((j + 1) % 2), I=inverse((j + 1) % 2), S=state_step(m, j))
            if last:
                return emit("P IP IP IP I S I I S I I S I I S", **parts)
            if j == 0:
                return emit("P L IP L IP L IP L I E I S E I I E S I E I S I I S I", **parts, L=low_rank(m + 2), E=elementwise(m + 2, j))
            emit("P IP IP IP E I I E I S E I S I E I S I I S I", **parts, E=elementwise(m + 2, j))
        with c.fori(NCH // 2 - 1) as i:
            for j in range(2):
                step(i * 2 + j, j)
        step(NCH - 2, 0, last=True)
        emit("", S=state_step(NCH - 1, 1))
        c.join()
        for j in range(2):
            c.post(f"wread{j}", *(c.now(e) for e in c.engines))

    def rwkv_norm(self, y, rkv):
        c, sb, ps, do = self.c, self.sb, self.ps, self.do
        yc, sq = ([sb.at(self.HN + (2 * j + o) * S, S) for j in range(3)] for o in range(2))
        banks = [ps[:, 2 * j:2 * j + 2, :].rearrange("p a b -> p (a b)") for j in range(3)]
        one = lambda a, i: a[:, ds(i, 1), :].rearrange("p a b -> p (a b)")

        def means(j, src, *deps):
            c.wait(c.pe, *deps)
            for h in range(2):
                t = c.pe.matmul(ps[:, 2 * j + h, :], self.block64, src[:, h * HALF:(h + 1) * HALF], start=True, stop=True)
            return c.on_pe(t)
        R = range(3)
        with c.fori(BT // 3) as i:
            tile = [3 * i + j for j in R]
            for j in R:
                c.need(c.pe, f"normed{j}")
            t = [means(j, one(y, tile[j])) for j in R]
            for j in R:
                c.need(c.dve, f"normed{j}")
                t[j] = do(c.dve, [t[j]], lambda: c.dve.tensor_tensor(yc[j], one(y, tile[j]), banks[j], ALU.subtract))
            t = [do(c.act, [t[j]], lambda: c.act.activation(sq[j], yc[j], ACT.Square)) for j in R]
            t = [means(j, sq[j], t[j]) for j in R]
            t = [do(c.act, [t[j]], lambda: c.act.activation(sq[j], banks[j], ACT.Ln, bias=self.lnx_eps)) for j in R]
            t = [do(c.act, [t[j]], lambda: c.act.activation(sq[j], sq[j], ACT.Exp, scale=-0.5)) for j in R]
            for j in R:
                w = self.vec["a_lnx_w_2"][:, ds(tile[j], 1)]
                b = self.vec["a_lnx_b_2"][:, ds(tile[j], 1)]
                t[j] = do(c.dve, [t[j]], lambda: c.dve.scalar_tensor_tensor(yc[j], yc[j], w, sq[j], ALU.mult, ALU.mult))
                c.post(f"normed{j}", do(c.dve, [t[j]], lambda: c.dve.scalar_tensor_tensor(
                    one(y, tile[j]), yc[j], b, one(rkv, tile[j] + 2 * BT), ALU.add, ALU.add)))
        c.join()

    def finish_layer(self, l, w_in, gate_col, mem_col, xs, mix_at, qg, tmp, tmp2):
        c, sb, A, do = self.c, self.sb, self.A, self.do
        s = sb.at(tmp2, 4, HALF)
        mix = sb.at(mix_at, KT, S)

        def silu_into(i, j, h, bank, t):
            b = s[:, 2 * j + h, :]
            c.wait(c.act, t)
            c.need(c.act, f"gated{j}{h}")
            free = c.on_act(c.act.activation(b, bank, ACT.Silu))
            c.wait(c.dve, free)
            d = mix[:, ds(2 * i + j, 1), h * HALF:(h + 1) * HALF].rearrange("p a b -> p (a b)")
            c.post(f"gated{j}{h}", c.on_dve(c.dve.tensor_tensor(d, d, b, ALU.mult)))
            return free
        self.linear(w_in, KT, lambda i, j: (2 * i + j) * P + gate_col, 3, xs, silu_into,
                    then=lambda: self.prefetch(w_in, mem_col))
        self.linear(w_in, KT, lambda i, j: (2 * i + j) * P + mem_col, 1, xs,
                    self.to(lambda i, j: qg[:, j, :]), then=lambda: self.prefetch(w_in, mem_col + MEM_W))
        self.linear(w_in, KT, lambda i, j: (2 * i + j) * P + mem_col + MEM_W, 1, xs,
                    lambda i, j, h, bank, t: do(c.act, [t], lambda: c.act.activation(
                        qg[:, 2 + j, h * HALF:(h + 1) * HALF], bank, ACT.Silu)))
        mn = sb.at(tmp, KT, MEM)
        km, vm = sb.at(tmp + 4096, 2, MEM), sb.at(tmp + 4608, 2, MEM_W)
        for j in range(KT):
            c.on_dve(c.dve.tensor_scalar(mn[:, j, :], self.mhat[:, j, :],
                                         self.vec["mem_norm_2"][:, l * KT + j:l * KT + j + 1], None, ALU.mult))
        c.join()
        mn = self.split(tmp, tmp + 2048, tmp, KT, MEM)
        w_kv = A["w_mem_kv_2"][l]
        self.linear(w_kv, KT, lambda i, j: (2 * i + j) * P, 1, mn, self.to(lambda i, j: km[:, j, :]), n_cols=MEM)
        self.linear_tokens(w_kv, MEM_W, 1, mn, vm, rows=MEM)
        one = lambda a, i: a[:, ds(i, 1), :].rearrange("p a b -> p (a b)")
        self.attention(2, lambda i: one(qg, i), lambda i: one(km, i), lambda i, j: vm[:, j, ds(i * P, P)],
                       lambda i, iq: mix[:, ds(i + 6, 1), iq * P:(iq + 1) * P].rearrange("p a b -> p (a b)"),
                       self.HN, lambda iq: MEM)
        for j in range(2):
            c.on_dve(c.dve.tensor_tensor(mix[:, 6 + j, :], mix[:, 6 + j, :], qg[:, 2 + j, :], ALU.mult))
        c.join()
        self.prefetch(A["w_out_2"][l], 0)
        mix = self.split(mix_at, tmp, mix_at, KT, S)
        evac, squares = self.to_squared(lambda i, j: self.hn[:, ds(2 * i + j, 1), :].rearrange("p a b -> p (a b)"), tmp + 8192)
        self.linear(A["w_out_2"][l], KT, lambda i, j: (2 * i + j) * P, 4, mix, evac)
        self.x_squares = self.add_normed(self.hn, self.vec["post_norm_2"][:, l * KT:(l + 1) * KT], tmp, squares,
                                         None if l else tmp + S)

    def layer_b(self):
        c, sb, A, ps, do = self.c, self.sb, self.A, self.ps, self.do
        B = self.BIG
        w_in = A["b_w_in_2"].rearrange("l a b -> (l a) b")
        mix = sb.at(B, KT, S)
        k = sb.at(B + 8192, BT, S)
        v = sb.at(B + 14336, ST, BR)
        dist, strip = sb.at(B + 20480, S), sb.at(B + 21504, S)
        one = lambda a, i: a[:, ds(i, 1), :].rearrange("p a b -> p (a b)")
        lam = [sb.at(B + 22528 + 64 * j, HD) for j in range(4)]
        e = [sb.at(B + 22528 + 256 + j, 1) for j in range(3)]
        c.wait(c.sp, *(c.now(n) for n in c.engines))
        for a, n in zip(lam, ("q1", "k1", "q2", "k2")):
            t_lam = c.load(self.misc, a, A[f"b_lam_{n}_2"].rearrange("l a -> (l a)").partition_broadcast(P))
        self.prefetch(w_in, 0)
        self.keep_x()
        xs = self.norm_x(self.vec["pre_norm_2"][:, KT:2 * KT], B + 8192, B + 16384, self.x_squares)
        self.linear(w_in, KT, lambda i, j: (2 * i + j) * P, 3, xs, self.to(lambda i, j: one(mix, 2 * i + j)))
        self.prefetch(A["w_kv_2"], 0)
        xs = self.norm_x(self.vec["kv_norm_2"], self.X, B + 8192, again=True)
        self.linear(A["w_kv_2"], KT, lambda i, j: (2 * i + j) * P, 3, xs, self.to(lambda i, j: one(k, 2 * i + j)))
        self.linear_tokens(A["w_kv_2"], BR, 3, xs, v)
        self.fetch_x()

        for j in range(2):
            t2 = do(c.dve, [t_lam], lambda: c.dve.tensor_tensor(lam[2 * j], lam[2 * j], lam[2 * j + 1], ALU.mult))
            t2 = do(c.dve, [t2], lambda: c.dve.tensor_reduce(e[j], lam[2 * j], AX.X, ALU.add))
            t2 = do(c.act, [t2], lambda: c.act.activation(e[j], e[j], ACT.Exp))
        t = do(c.dve, [t2], lambda: c.dve.tensor_tensor(e[2], e[1], e[0], ALU.subtract))
        do(c.dve, [t], lambda: c.dve.tensor_scalar(self.neglam, e[2], -LAM_INIT, None, ALU.add))
        t = do(c.pool, [c.now("dve")], lambda: c.pool.iota(dist, [[-1, S]], base=S - P, channel_multiplier=1,
                                                          allow_small_or_imprecise_dtypes=True))
        t = do(c.act, [t], lambda: c.act.activation(dist, dist, ACT.Abs))
        t = do(c.dve, [t], lambda: c.dve.tensor_scalar(dist, dist, -1.0, None, ALU.mult))
        do(c.dve, [t], lambda: c.dve.memset(dist[0:64, S - 64:S], NEG * 100))
        c.join()

        def strip_of(i):
            c.need(c.dve, "bias10", "bias11")
            self.t_strip = c.on_dve(c.dve.tensor_scalar(strip, dist, self.slopes[:, ds(i, 1)], None, ALU.mult))

        self.attention(BT, lambda i: one(mix, i), lambda i: one(k, i), lambda i, j: v[:, j, ds(i * P, P)],
                       lambda i, iq: mix[:, ds(i, 1), iq * P:(iq + 1) * P].rearrange("p a b -> p (a b)"),
                       self.HN, lambda iq: (iq + 1) * P,
                       bias=lambda h, iq: (strip[:, S - (iq + 1) * P:S], self.t_strip),
                       per_pair=strip_of, diff=True)

        sub = e[0]
        c.on_dve(c.dve.tensor_scalar(sub, self.vec["b_subln_2"], 1.0 - LAM_INIT, None, ALU.mult))
        sq = [sb.at(self.HN + j * S, S) for j in range(3)]
        banks = [ps[:, 2 * j:2 * j + 2, :].rearrange("p a b -> p (a b)") for j in range(3)]
        c.join()
        R = range(3)
        with c.fori(BT // 3) as i:
            for j in R:
                c.need(c.act, f"subnormed{j}")
            t = [do(c.act, [], lambda: c.act.activation(sq[j], one(mix, 3 * i + j), ACT.Square)) for j in R]
            for j in R:
                c.wait(c.pe, t[j])
                for h in range(2):
                    t[j] = c.pe.matmul(ps[:, 2 * j + h, :], self.ones, sq[j][:, h * HALF:(h + 1) * HALF], start=True, stop=True)
                t[j] = c.on_pe(t[j])
            t = [do(c.act, [t[j]], lambda: c.act.activation(sq[j], banks[j], ACT.Ln, bias=self.eps, scale=1.0 / P)) for j in R]
            t = [do(c.act, [t[j]], lambda: c.act.activation(sq[j], sq[j], ACT.Exp, scale=-0.5)) for j in R]
            for j in R:
                m = one(mix, 3 * i + j)
                c.post(f"subnormed{j}", do(c.dve, [t[j]], lambda: c.dve.scalar_tensor_tensor(m, m, sub, sq[j], ALU.mult, ALU.mult)))
        c.join()
        self.prefetch(w_in, BR)
        xs = self.norm_x(self.vec["pre_norm_2"][:, KT:2 * KT], B + 12288, B + 20480, again=True)
        self.finish_layer(1, w_in, BR, 2 * BR, xs, B, sb.at(B + 8192, 4, S), B + 12288, B + 20480)


_INS = [
    "x", "p", "g_mix_pre", "w_in", "b_forget", "g_attn_grp", "g_pool_grp", "w_pool", "pool_scale", "w_out",
    "g_mix_post", "g_ffn_pre", "w_ffn_gate", "w_ffn_up", "w_ffn_down", "g_ffn_post", "w_ple_proj", "g_ple",
    "w_ple_gate", "mem_2", "pre_norm_2", "post_norm_2", "w_out_2", "mem_norm_2", "w_mem_kv_2", "a_w_in_2",
    "a_shift_mu_2", "a_w0_2", "a_w2_2", "a_a0_2", "a_a2_2", "a_k_k_2", "a_k_a_2", "a_r_k_2", "a_lnx_w_2",
    "a_lnx_b_2", "kv_norm_2", "w_kv_2", "b_w_in_2", "b_lam_q1_2", "b_lam_k1_2", "b_lam_q2_2", "b_lam_k2_2",
    "b_subln_2",
]


def kernel(**inputs):
    import numpy as _np
    import concourse.bacc as _bacc
    from concourse import mybir as _mybir
    from concourse.bass_utils import run_bass_kernel_spmd as _run

    arrays = {f"in_{n}": _np.ascontiguousarray(inputs[n]) for n in _INS}
    known = {}
    for _ in range(2):
        nc = _bacc.Bacc("TRN2", target_bir_lowering=False, num_devices=1)
        A = {n: nc.dram_tensor(f"in_{n}", arrays[f"in_{n}"].shape, _mybir.dt.float32, kind="ExternalInput").ap()
             for n in _INS}
        out = nc.dram_tensor("out", (1, S, D), _mybir.dt.float32, kind="ExternalOutput").ap()
        build(nc, A, out, known)
    r = _run(nc, [arrays], core_ids=[0])
    return r.results[0]["out"]
```
